# Optimizing a Trainium2 kernel written in Bass

```python
import math
import jax, jax.numpy as jnp
from jax import lax
import numpy as np
import jax
import jax.numpy as jnp

D_MODEL = 1024
BATCH = 1
SEQ = 512
DEPTH = 2

GRID_W = 64
CTX_LEN = 256
D_FF = 4 * D_MODEL
N_MOD = 6

MLA_HEADS = 8
QK_NOPE = 64
QK_ROPE = 32
QK_DIM = QK_NOPE + QK_ROPE
V_DIM = 64
MLA_WIDTH = MLA_HEADS * V_DIM
Q_LORA = 256
KV_LORA = 128
AXIS_DIM = QK_ROPE // 2
ROPE_THETA = 10000.0
Q_BLOCK = 128
SM_SCALE = 1.0 / math.sqrt(QK_DIM)

CONF_WIDTH = 256
CONF_K = 31
SC_WIDTH = 256
SC_K = 3

MIX_WIDTH = MLA_WIDTH + CONF_WIDTH + SC_WIDTH

Q_END = Q_LORA
KV_START = Q_END
KV_END = KV_START + KV_LORA
ROPE_END = KV_END + QK_ROPE
CONF_END = ROPE_END + 2 * CONF_WIDTH
IN_WIDTH = CONF_END + 3 * SC_WIDTH

EPS = 1e-6


def rmsnorm(u, g):
    uf = u.astype(jnp.float32)
    y = uf * lax.rsqrt(jnp.mean(uf * uf, axis=-1, keepdims=True) + EPS)
    return (y * g.astype(jnp.float32)).astype(u.dtype)

def layernorm(u, g, b):
    uf = u.astype(jnp.float32)
    mu = jnp.mean(uf, axis=-1, keepdims=True)
    d = uf - mu
    y = d * lax.rsqrt(jnp.mean(d * d, axis=-1, keepdims=True) + EPS)
    return (y * g.astype(jnp.float32) + b.astype(jnp.float32)).astype(u.dtype)

def modulation(cvec, w_mod, b_mod):
    m = jax.nn.silu(cvec) @ w_mod + b_mod
    return jnp.split(m[:, None, :], N_MOD, axis=-1)

def modulate(h, shift, scale):
    return h * (1.0 + scale) + shift

def axial_rope_tables(rows):
    row = jnp.broadcast_to(jnp.arange(rows)[:, None], (rows, GRID_W)).reshape(-1).astype(jnp.float32)
    col = jnp.broadcast_to(jnp.arange(GRID_W)[None, :], (rows, GRID_W)).reshape(-1).astype(jnp.float32)
    inv = 1.0 / (ROPE_THETA ** (jnp.arange(0, AXIS_DIM, 2, dtype=jnp.float32) / AXIS_DIM))
    ar = row[:, None] * inv
    ac = col[:, None] * inv
    ang = jnp.concatenate([ar, ar, ac, ac], axis=-1)
    return jnp.cos(ang), jnp.sin(ang)

def apply_axial_rope(u, cos, sin):
    def rot(p):
        h = p.shape[-1] // 2
        return jnp.concatenate([-p[..., h:], p[..., :h]], axis=-1)
    rotated = jnp.concatenate([rot(u[..., :AXIS_DIM]), rot(u[..., AXIS_DIM:])], axis=-1)
    return (u.astype(jnp.float32) * cos + rotated.astype(jnp.float32) * sin).astype(u.dtype)

def mla_queries(zq, g_q, w_q_b, rope):
    b, s, _ = zq.shape
    q = (rmsnorm(zq, g_q) @ w_q_b).reshape(b, s, MLA_HEADS, QK_DIM)
    if rope is None:
        return q
    cos, sin = rope
    q_rope = apply_axial_rope(q[..., QK_NOPE:], cos[:, None, :], sin[:, None, :])
    return jnp.concatenate([q[..., :QK_NOPE], q_rope], axis=-1)

def mla_keys_values(zkv, g_kv, w_kv_b, rope):
    b, s, _ = zkv.shape
    ckv, k_rope = zkv[..., :KV_LORA], zkv[..., KV_LORA:]
    kv = (rmsnorm(ckv, g_kv) @ w_kv_b).reshape(b, s, MLA_HEADS, QK_NOPE + V_DIM)
    k_nope, v = kv[..., :QK_NOPE], kv[..., QK_NOPE:]
    if rope is not None:
        cos, sin = rope
        k_rope = apply_axial_rope(k_rope, cos, sin)
    k_rope = jnp.broadcast_to(k_rope[:, :, None, :], (b, s, MLA_HEADS, QK_ROPE))
    return jnp.concatenate([k_nope, k_rope], axis=-1), v

def block_attention(q, k, v):
    b, s, h, dq = q.shape
    dv = v.shape[-1]
    nb = s // Q_BLOCK
    qb = jnp.moveaxis(q.reshape(b, nb, Q_BLOCK, h, dq), 1, 0)

    def attend(qblk):
        logits = jnp.einsum('bqhd,bkhd->bhqk', qblk, k).astype(jnp.float32) * SM_SCALE
        p = jax.nn.softmax(logits, axis=-1).astype(v.dtype)
        return jnp.einsum('bhqk,bkhd->bqhd', p, v)

    o = lax.map(attend, qb)
    return jnp.moveaxis(o, 0, 1).reshape(b, s, h * dv)

def depthwise_conv(u, w):
    k, ch = w.shape
    return lax.conv_general_dilated(
        u, w[:, None, :].astype(u.dtype), window_strides=(1,),
        padding=[(k // 2, k // 2)], dimension_numbers=('NWC', 'WIO', 'NWC'),
        feature_group_count=ch)

def conformer_branch(z, dw_w, dw_b, ln_g, ln_b):
    a, g = jnp.split(z, 2, axis=-1)
    u = a * jax.nn.sigmoid(g)
    u = depthwise_conv(u, dw_w) + dw_b
    u = layernorm(u, ln_g, ln_b)
    return jax.nn.silu(u)

def shortconv_branch(z, w):
    b_gate, c_gate, h = jnp.split(z, 3, axis=-1)
    return b_gate * depthwise_conv(c_gate * h, w)

def mix_stream(z, k, v, rope, g_q, w_q_b, conf_dw_w, conf_dw_b, conf_ln_g, conf_ln_b,
               sc_dw_w, g_branch, w_o):
    q = mla_queries(z[..., :Q_END], g_q, w_q_b, rope)
    attn = block_attention(q, k, v)
    conf = conformer_branch(z[..., ROPE_END:CONF_END], conf_dw_w, conf_dw_b, conf_ln_g, conf_ln_b)
    sc = shortconv_branch(z[..., CONF_END:], sc_dw_w)
    merged = jnp.concatenate([
        rmsnorm(attn, g_branch[:MLA_WIDTH]),
        rmsnorm(conf, g_branch[MLA_WIDTH:MLA_WIDTH + CONF_WIDTH]),
        rmsnorm(sc, g_branch[MLA_WIDTH + CONF_WIDTH:])], axis=-1)
    return merged @ w_o

def sqrelu_mlp(h, w1, w2):
    a = jax.nn.relu(h @ w1)
    return (a * a) @ w2

def first_inputs(seed: int = 0) -> dict:
    key = jax.random.key(seed)
    ks = jax.random.split(key, 32)
    f32 = jnp.float32

    def nrm(k, shape, scale):
        return jax.random.normal(k, shape, f32) * scale

    def gain(k, shape):
        return 1.0 + 0.05 * jax.random.normal(k, shape, f32)

    L, D = DEPTH, D_MODEL
    return {
        "x": nrm(ks[0], (BATCH, SEQ, D), 1.0),
        "c": nrm(ks[1], (BATCH, D), 1.0),
        "ctx": nrm(ks[2], (BATCH, CTX_LEN, D), 1.0),
        "c_ctx": nrm(ks[3], (D,), 1.0),
        "w_mod": nrm(ks[4], (L, D, N_MOD * D), 0.5 * D ** -0.5),
        "b_mod": nrm(ks[5], (L, N_MOD * D), 0.02),
        "g_pre_mix": gain(ks[6], (L, D)),
        "g_post_mix": gain(ks[7], (L, D)),
        "g_pre_mlp": gain(ks[8], (L, D)),
        "g_post_mlp": gain(ks[9], (L, D)),
        "w_in": nrm(ks[10], (L, D, IN_WIDTH), D ** -0.5),
        "g_q": gain(ks[11], (L, Q_LORA)),
        "w_q_b": nrm(ks[12], (L, Q_LORA, MLA_HEADS * QK_DIM), Q_LORA ** -0.5),
        "g_kv": gain(ks[13], (L, KV_LORA)),
        "w_kv_b": nrm(ks[14], (L, KV_LORA, MLA_HEADS * (QK_NOPE + V_DIM)), KV_LORA ** -0.5),
        "conf_dw_w": nrm(ks[15], (L, CONF_K, CONF_WIDTH), CONF_K ** -0.5),
        "conf_dw_b": nrm(ks[16], (L, CONF_WIDTH), 0.02),
        "conf_ln_g": gain(ks[17], (L, CONF_WIDTH)),
        "conf_ln_b": nrm(ks[18], (L, CONF_WIDTH), 0.02),
        "sc_dw_w": nrm(ks[19], (L, SC_K, SC_WIDTH), SC_K ** -0.5),
        "g_branch": gain(ks[20], (L, MIX_WIDTH)),
        "w_o": nrm(ks[21], (L, MIX_WIDTH, D), MIX_WIDTH ** -0.5),
        "w_mlp_in": nrm(ks[22], (L, D, D_FF), D ** -0.5),
        "w_mlp_out": nrm(ks[23], (L, D_FF, D), D_FF ** -0.5),
    }

def first_block(x, c, ctx, c_ctx, w_mod, b_mod, g_pre_mix, g_post_mix, g_pre_mlp, g_post_mlp,
              w_in, g_q, w_q_b, g_kv, w_kv_b, conf_dw_w, conf_dw_b, conf_ln_g, conf_ln_b,
              sc_dw_w, g_branch, w_o, w_mlp_in, w_mlp_out):
    n_lat = x.shape[1]
    rows = n_lat // GRID_W
    rope = axial_rope_tables(rows)
    xl, xc = x, ctx
    for i in range(DEPTH):
        last = i == DEPTH - 1
        ml = modulation(c, w_mod[i], b_mod[i])
        mc = modulation(c_ctx[None, :], w_mod[i], b_mod[i])

        hl = modulate(rmsnorm(xl, g_pre_mix[i]), ml[0], ml[1])
        hc = modulate(rmsnorm(xc, g_pre_mix[i]), mc[0], mc[1])
        zl = hl @ w_in[i]
        if last:
            zc_kv = hc @ w_in[i][:, KV_START:ROPE_END]
        else:
            zc = hc @ w_in[i]
            zc_kv = zc[..., KV_START:ROPE_END]

        k_c, v_c = mla_keys_values(zc_kv, g_kv[i], w_kv_b[i], None)
        k_l, v_l = mla_keys_values(zl[..., KV_START:ROPE_END], g_kv[i], w_kv_b[i], rope)
        y_l = mix_stream(zl, jnp.concatenate([k_c, k_l], axis=1), jnp.concatenate([v_c, v_l], axis=1),
                         rope, g_q[i], w_q_b[i], conf_dw_w[i], conf_dw_b[i], conf_ln_g[i],
                         conf_ln_b[i], sc_dw_w[i], g_branch[i], w_o[i])
        xl_new = xl + ml[2] * rmsnorm(y_l, g_post_mix[i])

        h2 = modulate(rmsnorm(xl_new, g_pre_mlp[i]), ml[3], ml[4])
        xl_new = xl_new + ml[5] * rmsnorm(sqrelu_mlp(h2, w_mlp_in[i], w_mlp_out[i]), g_post_mlp[i])

        if not last:
            y_c = mix_stream(zc, k_c, v_c, None, g_q[i], w_q_b[i], conf_dw_w[i], conf_dw_b[i],
                             conf_ln_g[i], conf_ln_b[i], sc_dw_w[i], g_branch[i], w_o[i])
            xc_new = xc + mc[2] * rmsnorm(y_c, g_post_mix[i])
            h2c = modulate(rmsnorm(xc_new, g_pre_mlp[i]), mc[3], mc[4])
            xc = xc_new + mc[5] * rmsnorm(sqrelu_mlp(h2c, w_mlp_in[i], w_mlp_out[i]), g_post_mlp[i])
        xl = xl_new
    return xl


DN_HEADS = 4
DN_DK = 128
DN_DV = 128
DN_CONV = 4
DN_CHUNK = 64
DN_WIDTH = DN_HEADS * DN_DV
POOL_WINDOWS = (2, 4, 8, 16)
POOL_GROUP = 128
POOL_WIDTH = POOL_GROUP * len(POOL_WINDOWS)
SA_HEADS = 4
SA_HEAD_DIM = 128
SA_WIDTH = SA_HEADS * SA_HEAD_DIM
IDX_HEADS = 4
IDX_DIM = 64
TOPK_MAX = 256
NORM_EPS = 1e-6
N_BRANCH = 3
BRANCH_WIDTH = 512
SPLIT_SIZES = (DN_WIDTH, DN_WIDTH, DN_WIDTH, DN_WIDTH, DN_HEADS, DN_HEADS,
               POOL_WIDTH, POOL_WIDTH,
               SA_WIDTH, SA_WIDTH, SA_WIDTH, SA_WIDTH, IDX_HEADS * IDX_DIM, IDX_DIM, IDX_HEADS,
               N_BRANCH * D_MODEL)
IN_WIDTH_2 = sum(SPLIT_SIZES)


def rms_norm(x, g):
    x32 = x.astype(jnp.float32)
    y = x32 * lax.rsqrt(jnp.mean(x32 * x32, axis=-1, keepdims=True) + NORM_EPS)
    return y.astype(x.dtype) * g

def l2_normalize(x):
    x32 = x.astype(jnp.float32)
    return x32 * lax.rsqrt(jnp.sum(x32 * x32, axis=-1, keepdims=True) + NORM_EPS)

def rope_tables(seq_len, dim):
    inv_freq = ROPE_THETA ** (-jnp.arange(0, dim, 2, dtype=jnp.float32) / dim)
    ang = jnp.arange(seq_len, dtype=jnp.float32)[:, None] * inv_freq[None, :]
    return jnp.cos(ang), jnp.sin(ang)

def apply_rope(x, cos, sin):
    x32 = x.astype(jnp.float32)
    x1, x2 = jnp.split(x32, 2, axis=-1)
    c = cos[None, :, None, :]
    s = sin[None, :, None, :]
    return jnp.concatenate([x1 * c - x2 * s, x2 * c + x1 * s], axis=-1).astype(x.dtype)

def split_columns(proj):
    parts = []
    start = 0
    for size in SPLIT_SIZES:
        parts.append(proj[..., start:start + size])
        start += size
    return parts

def causal_depthwise_conv(x, w):
    k = w.shape[0]
    return lax.conv_general_dilated(x, w[:, None, :], window_strides=(1,), padding=((k - 1, 0),),
                                    dimension_numbers=('NWC', 'WIO', 'NWC'),
                                    feature_group_count=x.shape[-1])

def chunk_gated_delta_rule(q, k, v, beta, g):
    b, t, h, dk = q.shape
    dv = v.shape[-1]
    n = t // DN_CHUNK
    c = DN_CHUNK
    to_chunks4 = lambda a: a.reshape(b, n, c, h, a.shape[-1]).transpose(1, 0, 3, 2, 4)
    to_chunks3 = lambda a: a.reshape(b, n, c, h).transpose(1, 0, 3, 2)
    qc = to_chunks4(q * (dk ** -0.5))
    kc = to_chunks4(k)
    vc = to_chunks4(v)
    bc = to_chunks3(beta)
    gc = jnp.cumsum(to_chunks3(g), axis=-1)
    tril = jnp.tril(jnp.ones((c, c), dtype=bool))
    strict = jnp.tril(jnp.ones((c, c), dtype=bool), -1)
    decay = jnp.exp(jnp.where(tril, gc[..., :, None] - gc[..., None, :], -jnp.inf))
    k_beta = kc * bc[..., None]
    v_beta = vc * bc[..., None]
    lmat = jnp.where(strict, jnp.einsum('nbhid,nbhjd->nbhij', k_beta, kc) * decay, 0.0)
    eye = jnp.eye(c, dtype=jnp.float32)
    tmat = lax.linalg.triangular_solve(eye + lmat, jnp.broadcast_to(eye, lmat.shape),
                                       left_side=True, lower=True, unit_diagonal=True)
    u = jnp.einsum('nbhij,nbhjd->nbhid', tmat, v_beta)
    w = jnp.einsum('nbhij,nbhjd->nbhid', tmat, k_beta * jnp.exp(gc)[..., None])
    attn_intra = jnp.where(tril, jnp.einsum('nbhid,nbhjd->nbhij', qc, kc) * decay, 0.0)

    def step(state, xs):
        q_i, k_i, u_i, w_i, g_i, a_i = xs
        v_new = u_i - jnp.einsum('bhck,bhkv->bhcv', w_i, state)
        o = (jnp.einsum('bhck,bhkv->bhcv', q_i * jnp.exp(g_i)[..., None], state)
             + jnp.einsum('bhij,bhjv->bhiv', a_i, v_new))
        g_last = g_i[..., -1:]
        state = (state * jnp.exp(g_last)[..., None]
                 + jnp.einsum('bhck,bhcv->bhkv', k_i * jnp.exp(g_last - g_i)[..., None], v_new))
        return state, o

    state0 = jnp.zeros((b, h, dk, dv), dtype=jnp.float32)
    _, o = lax.scan(step, state0, (qc, kc, u, w, gc, attn_intra))
    return o.transpose(1, 0, 3, 2, 4).reshape(b, t, h, dv)

def deltanet_branch(qa, ka, va, za, ba, aa, conv_w, a_log, dt_bias, o_norm):
    b, t, _ = qa.shape
    qkv = jax.nn.silu(causal_depthwise_conv(jnp.concatenate([qa, ka, va], axis=-1), conv_w))
    q, k, v = jnp.split(qkv, 3, axis=-1)
    q = l2_normalize(q.reshape(b, t, DN_HEADS, DN_DK))
    k = l2_normalize(k.reshape(b, t, DN_HEADS, DN_DK))
    v = v.reshape(b, t, DN_HEADS, DN_DV).astype(jnp.float32)
    beta = jax.nn.sigmoid(ba.astype(jnp.float32))
    g = -jnp.exp(a_log.astype(jnp.float32)) * jax.nn.softplus(aa.astype(jnp.float32) + dt_bias.astype(jnp.float32))
    o = chunk_gated_delta_rule(q, k, v, beta, g)
    o = rms_norm(o, o_norm) * jax.nn.silu(za.reshape(b, t, DN_HEADS, DN_DV))
    return o.reshape(b, t, DN_WIDTH)

def pooling_branch(u, z, pool_w, pool_scale):
    b, t, _ = u.shape
    u32 = u.astype(jnp.float32)
    cs = jnp.cumsum(u32, axis=1)
    pos_count = jnp.arange(1, t + 1, dtype=jnp.int32)
    groups = []
    for gi, win in enumerate(POOL_WINDOWS):
        sl = slice(gi * POOL_GROUP, (gi + 1) * POOL_GROUP)
        cs_g = cs[..., sl]
        lagged = jnp.pad(cs_g, ((0, 0), (win, 0), (0, 0)))[:, :t]
        count = jnp.minimum(pos_count, win).astype(jnp.float32)[None, :, None]
        groups.append((cs_g - lagged) / count - u32[..., sl])
    pooled = jnp.stack(groups, axis=2)
    mixed = jnp.einsum('btgc,gcd->btgd', pooled.astype(pool_w.dtype), pool_w).reshape(b, t, POOL_WIDTH)
    return mixed * pool_scale * jax.nn.silu(z)

def sparse_attention_branch(qc, kc, vc, zc, iq, ik, iw, q_norm, k_norm, cos_a, sin_a, cos_i, sin_i):
    b, t, _ = qc.shape
    q = apply_rope(rms_norm(qc.reshape(b, t, SA_HEADS, SA_HEAD_DIM), q_norm), cos_a, sin_a)
    k = apply_rope(rms_norm(kc.reshape(b, t, SA_HEADS, SA_HEAD_DIM), k_norm), cos_a, sin_a)
    v = vc.reshape(b, t, SA_HEADS, SA_HEAD_DIM)
    qi = apply_rope(iq.reshape(b, t, IDX_HEADS, IDX_DIM), cos_i, sin_i)
    ki = apply_rope(ik.reshape(b, t, 1, IDX_DIM), cos_i, sin_i)[:, :, 0].astype(jnp.float32)
    wi = iw.astype(jnp.float32) * (IDX_HEADS ** -0.5 * IDX_DIM ** -0.5)
    topk = min(TOPK_MAX, t // 4)
    nb = t // Q_BLOCK
    to_blocks = lambda a: a.reshape((b, nb, Q_BLOCK) + a.shape[2:]).swapaxes(0, 1)
    key_pos = jnp.arange(t, dtype=jnp.int32)
    gather_rows = jax.vmap(lambda src, idx: src[idx])

    def attend(xs):
        q_b, qi_b, wi_b, start = xs
        q_pos = start + jnp.arange(Q_BLOCK, dtype=jnp.int32)
        causal = key_pos[None, :] <= q_pos[:, None]
        dots = jnp.einsum('bqhd,bsd->bqhs', qi_b.astype(jnp.float32), ki)
        score = jnp.einsum('bqh,bqhs->bqs', wi_b, jax.nn.relu(dots))
        score = jnp.where(causal[None], score, -jnp.inf)
        _, idx = lax.top_k(score, topk)
        k_sel = gather_rows(k, idx)
        v_sel = gather_rows(v, idx)
        logits = jnp.einsum('bqhd,bqkhd->bhqk', q_b.astype(jnp.float32), k_sel.astype(jnp.float32)) * (SA_HEAD_DIM ** -0.5)
        valid = idx <= q_pos[None, :, None]
        logits = jnp.where(valid[:, None], logits, -jnp.inf)
        p = jax.nn.softmax(logits, axis=-1)
        return jnp.einsum('bhqk,bqkhd->bqhd', p.astype(v_sel.dtype), v_sel)

    starts = jnp.arange(nb, dtype=jnp.int32) * Q_BLOCK
    o = lax.map(attend, (to_blocks(q), to_blocks(qi), to_blocks(wi), starts))
    o = o.swapaxes(0, 1).reshape(b, t, SA_WIDTH)
    return o * jax.nn.silu(zc)

def hybrid_layer(x, norm_g, w_in, gate_b, conv_w, a_log, dt_bias, dn_onorm, pool_w, pool_scale,
                 q_norm, k_norm, w_branch, w_out, cos_a, sin_a, cos_i, sin_i):
    b, t, _ = x.shape
    h = rms_norm(x, norm_g)
    proj = jnp.einsum('btd,de->bte', h, w_in)
    (qa, ka, va, za, ba, aa, ub, zb, qc, kc, vc, zc, iq, ik, iw, gates) = split_columns(proj)
    ya = deltanet_branch(qa, ka, va, za, ba, aa, conv_w, a_log, dt_bias, dn_onorm)
    yb = pooling_branch(ub, zb, pool_w, pool_scale)
    yc = sparse_attention_branch(qc, kc, vc, zc, iq, ik, iw, q_norm, k_norm, cos_a, sin_a, cos_i, sin_i)
    branches = jnp.stack([ya, yb, yc], axis=2).astype(w_branch.dtype)
    projected = jnp.einsum('btnc,ncd->btnd', branches, w_branch)
    gate = jax.nn.sigmoid(gates.reshape(b, t, N_BRANCH, D_MODEL).astype(jnp.float32) + gate_b.astype(jnp.float32))
    merged = jnp.sum(gate * projected, axis=2).astype(w_out.dtype)
    return x + jnp.einsum('btd,de->bte', merged, w_out).astype(x.dtype)

def second_inputs(seed: int = 0) -> dict:
    key = jax.random.key(seed)
    ks = jax.random.split(key, 16)
    f32 = jnp.float32
    x = jax.random.normal(ks[0], (BATCH, SEQ, D_MODEL), f32)
    norm_g = 1.0 + 0.02 * jax.random.normal(ks[1], (DEPTH, D_MODEL), f32)
    w_in = jax.random.normal(ks[2], (DEPTH, D_MODEL, IN_WIDTH_2), f32) * D_MODEL ** -0.5
    gate_b = 0.02 * jax.random.normal(ks[3], (DEPTH, N_BRANCH, D_MODEL), f32)
    conv_w = jax.random.normal(ks[4], (DEPTH, DN_CONV, 3 * DN_WIDTH), f32) * DN_CONV ** -0.5
    a_log = jnp.log(jax.random.uniform(ks[5], (DEPTH, DN_HEADS), f32, minval=1.0, maxval=16.0))
    dt = jnp.exp(jax.random.uniform(ks[6], (DEPTH, DN_HEADS), f32, minval=float(np.log(1e-3)), maxval=float(np.log(1e-1))))
    dt_bias = dt + jnp.log(-jnp.expm1(-dt))
    dn_onorm = 1.0 + 0.02 * jax.random.normal(ks[7], (DEPTH, DN_DV), f32)
    pool_w = jax.random.normal(ks[8], (DEPTH, len(POOL_WINDOWS), POOL_GROUP, POOL_GROUP), f32) * POOL_GROUP ** -0.5
    pool_scale = 1.0 + 0.1 * jax.random.normal(ks[9], (DEPTH, POOL_WIDTH), f32)
    q_norm = 1.0 + 0.02 * jax.random.normal(ks[10], (DEPTH, SA_HEAD_DIM), f32)
    k_norm = 1.0 + 0.02 * jax.random.normal(ks[11], (DEPTH, SA_HEAD_DIM), f32)
    w_branch = jax.random.normal(ks[12], (DEPTH, N_BRANCH, BRANCH_WIDTH, D_MODEL), f32) * BRANCH_WIDTH ** -0.5
    w_out = jax.random.normal(ks[13], (DEPTH, D_MODEL, D_MODEL), f32) * D_MODEL ** -0.5
    return {'x': x, 'norm_g': norm_g, 'w_in': w_in, 'gate_b': gate_b, 'conv_w': conv_w,
            'a_log': a_log, 'dt_bias': dt_bias, 'dn_onorm': dn_onorm, 'pool_w': pool_w,
            'pool_scale': pool_scale, 'q_norm': q_norm, 'k_norm': k_norm,
            'w_branch': w_branch, 'w_out': w_out}

def second_block(x, norm_g, w_in, gate_b, conv_w, a_log, dt_bias, dn_onorm, pool_w, pool_scale,
              q_norm, k_norm, w_branch, w_out):
    t = x.shape[1]
    cos_a, sin_a = rope_tables(t, SA_HEAD_DIM)
    cos_i, sin_i = rope_tables(t, IDX_DIM)
    for layer in range(DEPTH):
        x = hybrid_layer(x, norm_g[layer], w_in[layer], gate_b[layer], conv_w[layer], a_log[layer],
                         dt_bias[layer], dn_onorm[layer], pool_w[layer], pool_scale[layer],
                         q_norm[layer], k_norm[layer], w_branch[layer], w_out[layer],
                         cos_a, sin_a, cos_i, sin_i)
    return x


def setup_inputs(seed=0):
    out = dict(first_inputs(seed))
    for name, value in second_inputs(seed + 1).items():
        if name != "x":
            out[name + "_2"] = value
    return out


def reference(
    x, c, ctx, c_ctx, w_mod, b_mod, g_pre_mix, g_post_mix, g_pre_mlp, g_post_mlp, w_in, g_q,
    w_q_b, g_kv, w_kv_b, conf_dw_w, conf_dw_b, conf_ln_g, conf_ln_b, sc_dw_w, g_branch, w_o,
    w_mlp_in, w_mlp_out, norm_g_2, w_in_2, gate_b_2, conv_w_2, a_log_2, dt_bias_2, dn_onorm_2,
    pool_w_2, pool_scale_2, q_norm_2, k_norm_2, w_branch_2, w_out_2,
):
    x = first_block(
        x, c, ctx, c_ctx, w_mod, b_mod, g_pre_mix, g_post_mix, g_pre_mlp, g_post_mlp, w_in, g_q,
        w_q_b, g_kv, w_kv_b, conf_dw_w, conf_dw_b, conf_ln_g, conf_ln_b, sc_dw_w, g_branch, w_o,
        w_mlp_in, w_mlp_out,
    )
    return second_block(
        x, norm_g_2, w_in_2, gate_b_2, conv_w_2, a_log_2, dt_bias_2, dn_onorm_2, pool_w_2,
        pool_scale_2, q_norm_2, k_norm_2, w_branch_2, w_out_2,
    )


_drawn_inputs = setup_inputs


def setup_inputs(seed=0):
    import zlib

    import numpy as np

    out = dict(_drawn_inputs(seed))
    spreads = {}
    factors = {'g_q': 7.514,
     'conf_dw_b': 5.848,
     'conf_ln_g': 3.876,
     'conf_ln_b': 8.0,
     'norm_g_2': 3.262,
     'gate_b_2': 8.0,
     'dn_onorm_2': 8.0,
     'q_norm_2': 8.0,
     'k_norm_2': 8.0}
    for name, (base, spread) in spreads.items():
        noise = np.random.default_rng([zlib.crc32(name.encode()), seed]).standard_normal(out[name].shape)
        drawn = base * np.exp(spread * noise) if base else spread * noise
        out[name] = jnp.asarray(drawn.astype(out[name].dtype))
    for name, factor in factors.items():
        out[name] = (out[name] * factor).astype(out[name].dtype)
    return out
```

```python
import math
from contextlib import ExitStack

import numpy as np
import concourse.bass as bass
from concourse import mybir

L = 2
NH, QD = 8, 96
BIG = 1.0e30
SMALL = -3.0e38
MARK = -3.3e38
SM1 = 1.0 / math.sqrt(96.0)
SM2 = 128.0 ** -0.5

IN1 = [("zt", [(0, 416)]), ("cf", [(416, 928)]), ("sc", [(1184, 1696)]), ("sb", [(928, 1184)])]
IN2 = {"sm": [(2048, 2056), (5128, 5452)], "qa": [(0, 512)], "ka": [(512, 1024)], "va": [(1024, 1536)],
       "za": [(1536, 2048)], "ub": [(2056, 2568)], "zb": [(2568, 3080)], "qc": [(3080, 3592)],
       "kc": [(3592, 4104)], "vc": [(4104, 4616)], "zc": [(4616, 5128)]}


def gate_cols(n, half):
    at = 5452 + 1024 * n + 512 * half
    return [(at, at + 512)]


def width(cols):
    return sum(b - a for a, b in cols)


def plan():
    out = []

    def block(key, name, index, row, tiles, cols):
        for r in range(0, tiles, 4):
            out.append((key, name, index, row + 128 * r, 4, cols))

    def mod(i):
        for j in range(24):
            out.append((f"mod{i}", "w_mod", (i,), 0, 8, [(256 * j, 256 * j + 256)]))

    def mix1(i, last_ctx=False):
        for key, cols in IN1[:1] if last_ctx else IN1:
            block(key, "w_in", (i,), 0, 8, cols)
        if not last_ctx:
            out.append(("wq", "w_q_b", (i,), 0, 2, [(0, 768)]))
        out.append(("wkv", "w_kv_b", (i,), 0, 1, [(0, 1024)]))
        if not last_ctx:
            for h in range(2):
                block("wo", "w_o", (i,), 0, 8, [(512 * h, 512 * h + 512)])

    def mlp(i):
        for g in range(4):
            for h in range(2):
                block("w1", "w_mlp_in", (i,), 0, 8, [(1024 * g + 512 * h, 1024 * g + 512 * h + 512)])
            for h in range(2):
                block("w2", "w_mlp_out", (i,), 1024 * g, 8, [(512 * h, 512 * h + 512)])

    mod(0)
    mix1(0)
    mix1(0)
    mlp(0)
    mlp(0)
    mod(1)
    mix1(1, last_ctx=True)
    mix1(1)
    mlp(1)

    def branch(i, n):
        for h in range(2):
            block("gate", "w_in_2", (i,), 0, 8, gate_cols(n, h))
            block("br", "w_branch_2", (i, n), 0, 4, [(512 * h, 512 * h + 512)])

    for i in range(L):
        for key in ("sm", "qa", "ka", "va", "za"):
            block(key, "w_in_2", (i,), 0, 8, IN2[key])
        branch(i, 0)
        for key in ("ub", "zb"):
            block(key, "w_in_2", (i,), 0, 8, IN2[key])
        out.append(("pw", "pool_w_2", (i,), 0, 4, [(0, 128)]))
        branch(i, 1)
        for key in ("kc", "qc", "vc", "zc"):
            block(key, "w_in_2", (i,), 0, 8, IN2[key])
        branch(i, 2)
        for h in range(2):
            block("wout", "w_out_2", (i,), 0, 8, [(512 * h, 512 * h + 512)])
    return out


COLS1 = [("b_mod", 48), ("g_pre_mix", 8), ("g_post_mix", 8), ("g_pre_mlp", 8), ("g_post_mlp", 8),
         ("g_q", 2), ("g_kv", 1), ("conf_dw_w", 62), ("conf_dw_b", 2), ("conf_ln_g", 2), ("conf_ln_b", 2),
         ("sc_dw_w", 6), ("g_branch", 8)]
COLS2 = [("norm_g_2", 8), ("gate_b_2", 24), ("conv_w_2", 48), ("dn_onorm_2", 1), ("pool_scale_2", 4)]
ROWS2 = [("a_log_2", 4), ("dt_bias_2", 4), ("q_norm_2", 128), ("k_norm_2", 128)]


def places(parts):
    at, out = 0, {}
    for name, n in parts:
        out[name] = (at, at + n)
        at += n
    return out, at


CONSTS = [("ident", 128), ("ut", 128), ("ml", 128), ("mu", 128), ("lev", 7 * 128), ("tri", 128), ("cb", 128),
          ("pc", 64), ("r1c", 4 * 16), ("r1s", 4 * 16), ("rac", 4 * 64), ("ras", 4 * 64),
          ("ric", 4 * 32), ("ris", 4 * 32)]


def constants():
    at, n = places(CONSTS)
    c = np.zeros((128, n), np.float32)

    def put(name, a):
        c[:, at[name][0]:at[name][1]] = np.asarray(a, np.float32).reshape(128, -1)

    i, j = np.arange(128)[:, None], np.arange(128)[None, :]
    put("ident", i == j)
    put("ut", i <= j)
    put("ml", np.where(j < i, 0.0, -BIG))
    put("mu", np.where(i <= j, 0.0, -BIG))
    put("lev", np.stack([(i // (2 << s) == j // (2 << s)) & ((i >> s) % 2 == 1) & ((j >> s) % 2 == 0)
                         for s in range(7)], 1))
    put("tri", np.where(j <= i, 3.3e38, SMALL))
    put("cb", np.where(j <= i, 0.0, -BIG))
    pc = np.zeros((4, 16), np.float32)
    for g, w in enumerate((2, 4, 8, 16)):
        pc[g] = np.float32(1.0) / np.minimum(np.arange(1, 17), w).astype(np.float32)
    put("pc", np.broadcast_to(pc.reshape(1, 64), (128, 64)))

    def tables(pos, dim):
        inv = (10000.0 ** (-np.arange(0, dim, 2, dtype=np.float64) / dim)).astype(np.float32)
        ang = (pos.astype(np.float32)[:, None] * inv[None, :]).astype(np.float64)
        return np.cos(ang).astype(np.float32), np.sin(ang).astype(np.float32)

    def tiled(a):
        return a.reshape(4, 128, -1).transpose(1, 0, 2)

    t = np.arange(512)
    inv = (1.0 / (10000.0 ** (np.arange(0, 16, 2, dtype=np.float64) / 16)).astype(np.float32)).astype(np.float32)
    ar = ((t // 64).astype(np.float32)[:, None] * inv).astype(np.float64)
    ac = ((t % 64).astype(np.float32)[:, None] * inv).astype(np.float64)
    both = np.concatenate([ar, ac], 1)
    put("r1c", tiled(np.cos(both)))
    put("r1s", tiled(np.sin(both)))
    for name, dim in (("ra", 128), ("ri", 64)):
        co, si = tables(t, dim)
        put(name + "c", tiled(co))
        put(name + "s", tiled(si))
    return c


class Sem:
    def __init__(self, handle, name):
        self.h, self.name, self.n = handle, name, 0


class Engine:

    def __init__(self, eng, sem, chain):
        self.eng, self.sem, self.chain, self.seen = eng, sem, chain, {}

    def wait(self, *toks):
        for t in toks:
            if t is None:
                continue
            if isinstance(t, list):
                self.wait(*t)
                continue
            sem, value = t
            if self.seen.get(sem.name, 0) < value:
                self.seen[sem.name] = value
                self.eng.wait_ge(sem.h, value)

    def __call__(self, make, *waits):
        self.wait(*waits)
        if self.chain:
            self.wait(self.last())
        self.sem.n += 1
        make(self.eng).then_inc(self.sem.h, 1)
        return (self.sem, self.sem.n)

    def quiet(self, make, *waits):
        self.wait(*waits)
        make(self.eng)

    def dma(self, make, sem, *waits):
        self.wait(*waits)
        sem.n += 16
        make(self.eng).then_inc(sem.h, 16)
        return (sem, sem.n)

    def last(self):
        return (self.sem, self.sem.n) if self.sem.n else None


def program(nc, a_wbig, a_x, a_ctx, a_cv, a_cols1, a_cols2, a_rows2, a_const, a_out, stop=None):
    f32, f32r = mybir.dt.float32, mybir.dt.float32r
    ALU, ACT, AX = mybir.AluOpType, mybir.ActivationFunctionType, mybir.AxisListType
    C1, NC1 = places(COLS1)
    C2, NC2 = places(COLS2)
    R2, NR2 = places(ROWS2)
    CC, NCC = places(CONSTS)
    units = plan()
    ctx = ExitStack()
    with ctx:
        names = [0]

        def sb(shape, dt=f32, stack=ctx):
            names[0] += 1
            return stack.enter_context(nc.sbuf_tensor(f"t{names[0]}", shape, dt))

        def sem(name):
            return Sem(ctx.enter_context(nc.semaphore(name)), name)

        V, A, G, P, S = (Engine(e, sem(n), n in ("s_v", "s_a", "s_g")) for e, n in ((nc.vector, "s_v"), (nc.scalar, "s_a"), (nc.gpsimd, "s_g"),
                                                        (nc.tensor, "s_p"), (nc.sync, "s_s")))

        X = sb([128, 4, 1024])
        XC = sb([128, 2, 1024])
        AH, AL = sb([128, 8, 512], f32r), sb([128, 8, 512], f32r)
        NR, NS = 2, 2
        RAW = [sb([128, 2048]) for _ in range(NR)]
        WH = [sb([128, 2048], f32r) for _ in range(NS)]
        WL = [sb([128, 2048], f32r) for _ in range(NS)]
        K = sb([128, NCC])
        cols1 = sb([128, L, NC1])
        cols2 = sb([128, L, NC2])
        rows2 = sb([128, L, NR2])
        SCV = sb([128, 8, 2])
        MOD = sb([128, 48, 2])
        SA1 = sb([128, 2, 8, 2])
        GP = sb([128, 2, 8, 2])
        st = sb([128, 64])
        half = sb([128, 16])

        def con(name):
            return K[:, CC[name][0]:CC[name][1]]

        def c1(name, i):
            return cols1[:, i, C1[name][0]:C1[name][1]]

        def c2(name, i):
            return cols2[:, i, C2[name][0]:C2[name][1]]

        def r2(name, i):
            return rows2[:, i, R2[name][0]:R2[name][1]]

        ident = con("ident")

        GB = [ctx.enter_context(nc.psum_tensor(f"g{n}", [128, 512], f32)) for n in range(4)]
        PB = [ctx.enter_context(nc.psum_tensor(f"q{n}", [128, 1024], f32)) for n in range(2)]
        gfree = [[] for _ in range(4)]
        pfree = [[] for _ in range(4)]
        turn = [0]

        def pair():
            if turn[0] % 2:
                turn[0] += 1
            n = turn[0] // 2 % 2
            turn[0] += 2
            return PB[n], n, pfree[2 * n] + pfree[2 * n + 1]

        def free_pair(n, toks):
            pfree[2 * n] = list(toks)
            pfree[2 * n + 1] = list(toks)

        def bank():
            n = turn[0] % 4
            turn[0] += 1
            return PB[n // 2][:, 512 * (n % 2):512 * (n % 2) + 512], n, list(pfree[n])

        def free_bank(n, *toks):
            pfree[n] = list(toks)

        s_in = sem("s_in")
        s_raw = [sem(f"s_raw{n}") for n in range(NR)]
        for dst, src in ((K[:, :], a_const), (SCV[:, :, :], a_cv), (cols1[:, :, :], a_cols1),
                         (cols2[:, :, :], a_cols2), (rows2[:, :, :], a_rows2),
                         (XC[:, :, :], a_ctx), (X[:, :, :], a_x)):
            S.dma(lambda e, dst=dst, src=src: e.dma_start(dst, src), s_in)
        loaded = (s_in, s_in.n)

        offs, at = [], 0
        for u in units:
            offs.append(at)
            at += 128 * u[4] * width(u[5])
        raw_free = [[] for _ in range(NR)]
        w_free = [[] for _ in range(NS)]
        state = {"fetched": 0, "split": 0, "used": 0, "nsplit": 0}
        parts = {}

        def fetch():
            u = state["fetched"]
            if u >= len(units):
                return
            n = units[u][4] * width(units[u][5])
            src = a_wbig[offs[u]:offs[u] + 128 * n].rearrange("(p n) -> p n", p=128)
            dst = RAW[u % NR][:, 0:n]
            parts[u] = S.dma(lambda e: e.dma_start(dst, src), s_raw[u % NR], raw_free[u % NR])
            state["fetched"] += 1

        def release_raw(u, *toks):
            raw_free[u % NR] = list(toks)
            fetch()

        for _ in range(NR):
            fetch()

        def direct(u):
            return units[u][0] in ("wq", "wkv", "pw") or units[u][0].startswith("mod")

        split_of = {}

        def split(u):
            if u >= len(units) or u in split_of or direct(u):
                return
            n = units[u][4] * width(units[u][5])
            s = state["nsplit"] % NS
            state["nsplit"] += 1
            raw, hi, lo = RAW[u % NR][:, 0:n], WH[s][:, 0:n], WL[s][:, 0:n]
            t1 = A(lambda e: e.activation(hi, raw, ACT.Copy), parts[u], w_free[s])
            t2 = G(lambda e: e.tensor_tensor(lo, raw, hi.bitcast(f32), ALU.subtract), parts[u], t1, w_free[s])
            split_of[u] = (s, hi, lo, t1, t2)
            release_raw(u, t1, t2)

        def use(key):
            u = state["used"]
            state["used"] += 1
            assert units[u][0] == key, (units[u][0], key)
            return u

        def gemm(key, mode, act, T, tiles, w, evac, ready):
            aH, aL = act
            nb = T // 128 if mode == "TM" else w // 128
            toks = []
            for kh in range(tiles // 4):
                u = use(key)
                split(u)
                split(u + 1)
                s, hi, lo, t1, t2 = split_of[u]
                hi3, lo3 = hi.rearrange("p (k n) -> p k n", k=4), lo.rearrange("p (k n) -> p k n", k=4)
                for k in range(4):
                    kk = 4 * kh + k
                    P.wait(t1, t2, ready[kk] if isinstance(ready, dict) else ready)
                    for b in range(nb):
                        if kk == 0:
                            P.wait(gfree[b])
                        for n, (wp, ap) in enumerate(((hi3, aH), (hi3, aL), (lo3, aH))):
                            if mode == "TM":
                                lhs, rhs = ap[:, kk, 128 * b:128 * b + 128], wp[:, k, :]
                                out = GB[b][:, 0:w]
                            else:
                                lhs, rhs = wp[:, k, 128 * b:128 * b + 128], ap[:, kk, 0:T]
                                out = GB[b][:, 0:T]
                            first, final = kk == 0 and n == 0, kk == tiles - 1 and n == 2

                            def mm(e, out=out, lhs=lhs, rhs=rhs, first=first, final=final):
                                return e.matmul(out, lhs, rhs, start=first, stop=final)

                            if n == 2 and (final or (k == 3 and b == nb - 1)):
                                tok = P(mm)
                            else:
                                P.quiet(mm)
                        if kk == tiles - 1:
                            gfree[b] = evac(b, GB[b], tok)
                w_free[s] = [tok]
            return tok

        def rstd(out, ss, n, inv, eps, *waits):
            t = V(lambda e: e.tensor_scalar(out, ss, inv, eps, ALU.mult, ALU.add), *waits)
            return G(lambda e: e.tensor_tensor(out, out, half[:, 0:n], ALU.pow), t)

        def sumsq(src, junk, out, *waits):
            return A(lambda e: e.activation(junk, src, ACT.Square, accum_out=out), *waits)

        t0 = G(lambda e: e.memset(half[:, :], -0.5))
        for e_ in (V, A, G, P):
            e_.wait(loaded)
        P.wait(t0)
        th = st[:, 0:16].rearrange("p (a b) -> p a b", a=8)
        t1 = A(lambda e: e.activation(th, SCV[:, :, :], ACT.Tanh, scale=0.5))
        t1 = V(lambda e: e.tensor_scalar(th, th, 0.5, 0.5, ALU.mult, ALU.add), t1)
        scv_ready = V(lambda e: e.tensor_tensor(SCV[:, :, :], SCV[:, :, :], th, ALU.mult), t1)

        def fence():
            toks = [e_.last() for e_ in (V, A, G, P)]
            for e_ in (V, A, G, P):
                e_.wait(*toks)

        def modulation(i):
            B, bn, w0 = bank()
            P.wait(scv_ready, w0)
            for j in range(24):
                u = use(f"mod{i}")
                W = RAW[u % NR][:, :].rearrange("p (k n) -> p k n", k=8)
                P.wait(parts[u])
                for c in range(2):
                    for k in range(8):
                        o = B[:, 2 * (2 * j + c):2 * (2 * j + c) + 2]

                        def mm(e, o=o, W=W, k=k, c=c):
                            return e.matmul(o, W[:, k, 128 * c:128 * c + 128], SCV[:, k, :],
                                            start=(k == 0), stop=(k == 7))

                        if k == 7 and c == 1:
                            tok = P(mm)
                        else:
                            P.quiet(mm)
                release_raw(u, tok)
            bm = c1("b_mod", i)
            t = V(lambda e: e.tensor_tensor(MOD[:, :, :], B[:, 0:96].rearrange("p (a b) -> p a b", b=2),
                                            bm.unsqueeze(2).to_broadcast([128, 48, 2]), ALU.add), tok)
            free_bank(bn, t)
            for m, (pre, post) in enumerate((("g_pre_mix", "g_post_mix"), ("g_pre_mlp", "g_post_mlp"))):
                gp, gq = c1(pre, i), c1(post, i)
                sc, gt = MOD[:, 24 * m + 8:24 * m + 16, :], MOD[:, 24 * m + 16:24 * m + 24, :]
                t1 = V(lambda e: e.tensor_scalar(SA1[:, m, :, :], sc, 1.0, None, ALU.add), t)
                t1 = V(lambda e: e.tensor_tensor(SA1[:, m, :, :], SA1[:, m, :, :],
                                                 gp.unsqueeze(2).to_broadcast([128, 8, 2]), ALU.mult), t1)
                t2 = V(lambda e: e.tensor_tensor(GP[:, m, :, :], gt,
                                                 gq.unsqueeze(2).to_broadcast([128, 8, 2]), ALU.mult), t)
            return [t, t1, t2]

        def store_split(src, k, dst, tmp_free, *waits):
            h, l = dst
            t1 = V(lambda e: e.tensor_copy(h, src), *waits)
            t2 = G(lambda e: e.tensor_tensor(l, src, h.bitcast(f32), ALU.subtract), t1, *waits)
            return [t1, t2]

        def prep(x, nt, scale, shift, stk, afree):
            T = 128 * nt
            J, jn, w0 = pair()
            tk = None
            for t in range(nt):
                tk = sumsq(x[:, t, :], J[:, :], st[:, t:t + 1], w0 if t == 0 else None)
            free_pair(jn, [tk])
            r = st[:, 8:8 + nt]
            tr = rstd(r, st[:, 0:nt], nt, 1.0 / 1024, 1e-6, tk)
            xn = [sb([128, nt, 128], stack=stk) for _ in range(2)]
            tm = [sb([128, T], stack=stk) for _ in range(2)]
            xfree, tfree = [None, None], [[], []]
            ready = {}
            for k in range(8):
                y, f = xn[k % 2], tm[k % 2]
                a = V(lambda e: e.tensor_tensor(y[:, :, :], x[:, :, 128 * k:128 * k + 128],
                                                r.unsqueeze(2).to_broadcast([128, nt, 128]), ALU.mult),
                      tr, xfree[k % 2])
                B, bn, w0 = bank()
                P.wait(a, w0)
                for t in range(nt):
                    def tp(e, t=t):
                        return e.transpose(B[:, 128 * t:128 * t + 128], y[:, t, :], ident)
                    if t < nt - 1:
                        P.quiet(tp)
                    else:
                        tok = P(tp)
                xfree[k % 2] = tok
                if shift is None:
                    e1 = A(lambda e: e.activation(f[:, :], B[:, 0:T], ACT.Copy, scale=scale(k)), tok, tfree[k % 2])
                else:
                    e1 = A(lambda e: e.activation(f[:, :], B[:, 0:T], ACT.Identity, bias=shift(k),
                                                  scale=scale(k)), tok, tfree[k % 2])
                free_bank(bn, e1)
                ready[k] = store_split(f[:, :], k, (AH[:, k, 0:T], AL[:, k, 0:T]), None, e1, afree)
                tfree[k % 2] = ready[k]
            return ready

        def row_of(col, stk, *waits):
            row = sb([128, 1024], stack=stk)
            Q, qn, w0 = pair()
            P.wait(w0, *waits)
            for j in range(8):
                tok = P(lambda e: e.matmul(Q[:, 128 * j:128 * j + 128],
                                           col[:, j:j + 1].to_broadcast([128, 128]), ident, start=True, stop=True))
            t = A(lambda e: e.activation(row[:, :], Q[:, :], ACT.Copy), tok)
            free_pair(qn, [t])
            return row, t

        def residual(x, y, nt, row, trow, stk, ready):
            J, jn, w0 = pair()
            for t in range(nt):
                tk = sumsq(y[:, t, :], J[:, :], st[:, t:t + 1], w0 if t == 0 else None, ready)
            free_pair(jn, [tk])
            r = st[:, 8:8 + nt]
            tr = rstd(r, st[:, 0:nt], nt, 1.0 / 1024, 1e-6, tk)
            for t in range(nt):
                a = V(lambda e: e.scalar_tensor_tensor(y[:, t, :], y[:, t, :], r[:, t:t + 1], row[:, :],
                                                       ALU.mult, ALU.mult), tr, trow)
                V(lambda e: e.tensor_tensor(x[:, t, :], x[:, t, :], y[:, t, :], ALU.add), a)

        def rotate(dst, p1, p2, co, si, tmp, waits):
            d1, d2 = dst
            ta, tb, tc, td = tmp
            a = V(lambda e: e.tensor_tensor(ta, p1, co, ALU.mult), *waits)
            b = V(lambda e: e.tensor_tensor(tb, p2, si, ALU.mult))
            c = G(lambda e: e.tensor_tensor(tc, p2, co, ALU.mult), *waits)
            d = G(lambda e: e.tensor_tensor(td, p1, si, ALU.mult))
            u = V(lambda e: e.tensor_tensor(d1, ta, tb, ALU.subtract), a, b, c, d)
            return [u, V(lambda e: e.tensor_tensor(d2, tc, td, ALU.add), c, d)]

        def transposes(out, srcs, waits):
            P.wait(*waits)
            for j, (o, s_) in enumerate(zip(out, srcs)):
                f = (lambda e, o=o, s_=s_: e.transpose(o, s_, ident))
                if j < len(srcs) - 1:
                    P.quiet(f)
                else:
                    return P(f)

        def attention1(qtm, ktm, Vb, kt0, nk, nt, Z8, stk):
            KT = [sb([96, nk * 128], stack=stk) for _ in range(2)]
            QT = [sb([96, nt * 128], stack=stk) for _ in range(2)]
            PP = [sb([128, nk * 128], stack=stk) for _ in range(2)]
            PT = [sb([128, nk * 128], stack=stk) for _ in range(2)]
            free_k, free_p, free_t = [None, None], [None, None], [None, None]
            nh = (nk + 1) // 2 * 128
            pend = None

            def finish(job):
                h, t, n, Q, qn, te, tn = job
                tok = transposes([Q[:, 128 * j:128 * j + 128] for j in range(nk)],
                                 [PP[n][:, 128 * j:128 * j + 128] for j in range(nk)], [te])
                free_p[n] = tok
                eng = A if (t + h) % 2 else V
                if eng is A:
                    ev = A(lambda e: e.activation(PT[n][:, :], Q[:, 0:nk * 128], ACT.Copy), tok, free_t[n])
                else:
                    ev = V(lambda e: e.tensor_copy(PT[n][:, :], Q[:, 0:nk * 128]), tok, free_t[n])
                P.wait(ev)
                for j in range(nk):
                    tok = P(lambda e: e.matmul(Q[:, 896:960], PT[n][:, 128 * j:128 * j + 128],
                                               Vb[:, kt0 + j, 64 * h:64 * h + 64], start=(j == 0), stop=(j == nk - 1)))
                free_t[n] = tok
                o = V(lambda e: e.tensor_scalar(Z8[:, t, 64 * h:64 * h + 64], Q[:, 896:960],
                                                st[:, 34 + 3 * n:35 + 3 * n], None, ALU.mult), tok, tn)
                free_pair(qn, [o])
                stat_free[n] = o

            stat_free = [None, None]
            cnt = 0
            for h in range(NH):
                b = h % 2
                Bq, w0 = GB[0], gfree[0]
                tok = transposes([Bq[0:96, 128 * t:128 * t + 128] for t in range(nt)],
                                 [qtm[:, t, 96 * h:96 * h + 96] for t in range(nt)], [w0])
                eq = A(lambda e: e.activation(QT[b][:, :], Bq[0:96, 0:128 * nt], ACT.Copy), tok, free_k[b])
                gfree[0] = [eq]
                ek = []
                for k0 in range(0, nk, 4):
                    kn = min(4, nk - k0)
                    bk = 1 + k0 // 4
                    Bk, w0 = GB[bk], gfree[bk]
                    tok = transposes([Bk[0:96, 128 * j:128 * j + 128] for j in range(kn)],
                                     [ktm[:, kt0 + k0 + j, 96 * h:96 * h + 96] for j in range(kn)], [w0])
                    ek.append(V(lambda e: e.tensor_copy(KT[b][:, 128 * k0:128 * (k0 + kn)], Bk[0:96, 0:128 * kn]),
                                tok, free_k[b]))
                    gfree[bk] = [ek[-1]]
                for t in range(nt):
                    n = cnt % 2
                    cnt += 1
                    Q, qn, w0 = pair()
                    P.wait(w0, eq, ek)
                    for j in range(2):
                        c0, cn = j * nh, min(nh, nk * 128 - j * nh)
                        if cn <= 0:
                            continue
                        tok = P(lambda e: e.matmul(Q[:, 512 * j:512 * j + cn], QT[b][:, 128 * t:128 * t + 128],
                                                   KT[b][:, c0:c0 + cn], start=True, stop=True))
                    free_k[b] = tok
                    lg = Q[:, :].rearrange("p (a n) -> p a n", a=2)[:, :, 0:nh]
                    mx, nm, rs, ri = (st[:, 32 + 3 * n:33 + 3 * n], st[:, 33 + 3 * n:34 + 3 * n],
                                      st[:, 40 + n:41 + n], st[:, 34 + 3 * n:35 + 3 * n])
                    a = V(lambda e: e.tensor_reduce(mx, lg, AX.XY, ALU.max), tok)
                    a = V(lambda e: e.tensor_scalar(nm, mx, -SM1, None, ALU.mult), a)
                    te = A(lambda e: e.activation(PP[n][:, :].rearrange("p (a n) -> p a n", a=2), lg, ACT.Exp,
                                                  bias=nm, scale=SM1, accum_out=rs), a, free_p[n], stat_free[n])
                    tn = V(lambda e: e.reciprocal(ri, rs), te, stat_free[n])
                    if pend:
                        finish(pend)
                    pend = (h, t, n, Q, qn, te, tn)
            finish(pend)

        def mix1(i, s, x, nt, Z8, qtm, ktm, Vb, zT, last_ctx, stk, modtok):
            T = 128 * nt
            t_off = 0 if s else 2
            rope = not s
            sub = ExitStack()
            ready = prep(x, nt, lambda k: SA1[:, 0, k, s:s + 1], lambda k: MOD[:, k, s:s + 1], sub, modtok)
            z = Z8[:, :].rearrange("p (t n) -> p t n", t=4)
            zt = []

            def ev_z(b, B, tok):
                t = A(lambda e: e.activation(z[:, b, 0:416], B[:, 0:416], ACT.Copy), tok)
                zt.append(t)
                return [t]

            gemm("zt", "TM", (AH, AL), T, 8, 416, ev_z, ready)
            fence()
            sub.close()
            sub = ExitStack()
            J = sb([128, 256], stack=sub)
            for t in range(nt):
                sumsq(z[:, t, 0:256], J[:, :], st[:, t:t + 1], A.last())
                tk = sumsq(z[:, t, 256:384], J[:, 0:128], st[:, 4 + t:5 + t], A.last())
            rr = st[:, 8:16]
            if nt < 4:
                V(lambda e: e.memset(rr, 1.0))
            a = rstd(rr[:, 0:nt], st[:, 0:nt], nt, 1.0 / 256, 1e-6, tk, V.last())
            b = rstd(rr[:, 4:4 + nt], st[:, 4:4 + nt], nt, 1.0 / 128, 1e-6, tk, V.last())
            for t in range(nt):
                a1 = V(lambda e: e.tensor_scalar(z[:, t, 0:256], z[:, t, 0:256], rr[:, t:t + 1], None, ALU.mult), a, b)
                a2 = V(lambda e: e.tensor_scalar(z[:, t, 256:384], z[:, t, 256:384], rr[:, 4 + t:5 + t], None,
                                                 ALU.mult), b)
            gq, gkv = c1("g_q", i), c1("g_kv", i)
            zr = []
            for j in range(3):
                if last_ctx and j < 2:
                    continue
                B, bn, w0 = bank()
                tok = transposes([B[:, 128 * t:128 * t + 128] for t in range(nt)],
                                 [z[:, t, 128 * j:128 * j + 128] for t in range(nt)], [a1, a2, w0])
                sc = gq[:, j:j + 1] if j < 2 else gkv[:, 0:1]
                zr.append(A(lambda e: e.activation(zT[:, j, 0:T], B[:, 0:T], ACT.Copy, scale=sc), tok))
                free_bank(bn, zr[-1])
            kr = z[:, 0:nt, 384:416]
            if rope:
                kv = kr.rearrange("p t (h a c) -> p t h a c", h=2, a=2)
                tmp = [sb([128, nt, 2, 8], stack=sub) for _ in range(4)]
                co = con("r1c").rearrange("p (t h c) -> p t h c", t=4, h=2)
                si = con("r1s").rearrange("p (t h c) -> p t h c", t=4, h=2)
                krt = rotate((kv[:, :, :, 0, :], kv[:, :, :, 1, :]), kv[:, :, :, 0, :], kv[:, :, :, 1, :], co, si,
                             [x_[:, :, :, :] for x_ in tmp], [zt])
            else:
                krt = zt
            if not last_ctx:
                Cv = sb([128, 2, T], stack=sub)
                S2 = sb([128, 2, T], stack=sub)
                gg = S2
                m1 = sb([128, 256], stack=sub)
                m2 = sb([128, 256], stack=sub)
                rt = [sb([128, 8, 2, 8], stack=sub) for _ in range(4)]
                sub2 = ExitStack()
                U = sb([128, 2, T + 30], stack=sub2)
                H2 = sb([128, 2, T + 2], stack=sub2)
                for c in range(2):
                    G(lambda e: e.memset(U[:, c, 0:15], 0.0))
                    tz = G(lambda e: e.memset(U[:, c, T + 15:T + 30], 0.0))
                hold = {}

                def ev_cf(b, B, tok):
                    if b < 2:
                        hold[b] = A(lambda e: e.activation(U[:, b, 15:15 + T], B[:, 0:T], ACT.Copy), tok)
                        return [hold[b]]
                    c = b - 2
                    t = A(lambda e: e.activation(gg[:, c, :], B[:, 0:T], ACT.Tanh, scale=0.5), tok)
                    t1 = V(lambda e: e.tensor_scalar(gg[:, c, :], gg[:, c, :], 0.5, 0.5, ALU.mult, ALU.add), t)
                    hold[b] = V(lambda e: e.tensor_tensor(U[:, c, 15:15 + T], U[:, c, 15:15 + T], gg[:, c, :],
                                                          ALU.mult), t1, hold[c])
                    return [t]

                gemm("cf", "FM", (AH, AL), T, 8, 512, ev_cf, ready)
                W = c1("conf_dw_w", i).rearrange("p (c k) -> p c k", c=2)
                db = c1("conf_dw_b", i)
                for c in range(2):
                    t = V(lambda e: e.tensor_scalar(Cv[:, c, :], U[:, c, 0:T], W[:, c, 0:1], db[:, c:c + 1],
                                                    ALU.mult, ALU.add), hold[2 + c], tz)
                    for k in range(1, 31):
                        t = V(lambda e, k=k: e.scalar_tensor_tensor(Cv[:, c, :], U[:, c, k:k + T], W[:, c, k:k + 1],
                                                                    Cv[:, c, :], ALU.mult, ALU.add), t)
                conv_done = t
                for c in range(2):
                    G(lambda e: e.memset(H2[:, c, 0:1], 0.0))
                    tz = G(lambda e: e.memset(H2[:, c, T + 1:T + 2], 0.0))
                hs = {}

                def ev_sc(b, B, tok):
                    if b < 2:
                        hs[b] = A(lambda e: e.activation(H2[:, b, 1:1 + T], B[:, 0:T], ACT.Copy), tok)
                        return [hs[b]]
                    hs[b] = V(lambda e: e.tensor_tensor(H2[:, b - 2, 1:1 + T], B[:, 0:T], H2[:, b - 2, 1:1 + T],
                                                        ALU.mult), tok, hs[b - 2])
                    W3 = c1("sc_dw_w", i).rearrange("p (c k) -> p c k", c=2)
                    c = b - 2
                    t = V(lambda e: e.tensor_scalar(S2[:, c, :], H2[:, c, 0:T], W3[:, c, 0:1], None, ALU.mult),
                          hs[b], tz)
                    for k in range(1, 3):
                        t = V(lambda e, k=k: e.scalar_tensor_tensor(S2[:, c, :], H2[:, c, k:k + T], W3[:, c, k:k + 1],
                                                                    S2[:, c, :], ALU.mult, ALU.add), t)
                    hs[b] = t
                    return [hs[b]]

                gemm("sc", "FM", (AH, AL), T, 8, 512, ev_sc, ready)

                def ev_sb(b, B, tok):
                    hs[b] = V(lambda e: e.tensor_tensor(S2[:, b, :], B[:, 0:T], S2[:, b, :], ALU.mult), tok, hs[b + 2])
                    return [hs[b]]

                adone = gemm("sb", "FM", (AH, AL), T, 8, 256, ev_sb, ready)
            co = con("r1c").rearrange("p (t h c) -> p t h c", t=4, h=2)
            si = con("r1s").rearrange("p (t h c) -> p t h c", t=4, h=2)
            if not last_ctx:
                u = use("wq")
                Wq = RAW[u % NR][:, 0:1536].rearrange("p (k n) -> p k n", k=2)
                for t in range(nt):
                    Q, qn, w0 = pair()
                    P.wait(parts[u], w0, zr)
                    for hf in range(2):
                        for k in range(2):
                            tok = P(lambda e: e.matmul(Q[:, 512 * hf:512 * hf + 384], zT[:, k, 128 * t:128 * t + 128],
                                                       Wq[:, k, 384 * hf:384 * hf + 384], start=(k == 0), stop=(k == 1)))
                    ev = A(lambda e: e.activation(qtm[:, t, :].rearrange("p (a n) -> p a n", a=2),
                                                  Q[:, :].rearrange("p (a n) -> p a n", a=2)[:, :, 0:384], ACT.Copy), tok)
                    free_pair(qn, [ev])
                    if rope:
                        v = qtm[:, t, :].rearrange("p (h n) -> p h n", h=8)[:, :, 64:96]
                        v = v.rearrange("p h (b a c) -> p h b a c", b=2, a=2)
                        rotate((v[:, :, :, 0, :], v[:, :, :, 1, :]), v[:, :, :, 0, :], v[:, :, :, 1, :],
                               co[:, t, :, :].unsqueeze(1).to_broadcast([128, 8, 2, 8]),
                               si[:, t, :, :].unsqueeze(1).to_broadcast([128, 8, 2, 8]),
                               [x_[:, :, :, :] for x_ in rt], [ev, V.last(), G.last()])
                release_raw(u, tok)
            u = use("wkv")
            for t in range(nt):
                Q, qn, w0 = pair()
                P.wait(parts[u], w0, zr)
                for hf in range(2):
                    tok = P(lambda e: e.matmul(Q[:, 512 * hf:512 * hf + 512], zT[:, 2, 128 * t:128 * t + 128],
                                               RAW[u % NR][:, 512 * hf:512 * hf + 512], start=True, stop=True))
                q3 = Q[:, :].rearrange("p (h n) -> p h n", h=8)
                k3 = ktm[:, t_off + t, :].rearrange("p (h n) -> p h n", h=8)
                e1 = A(lambda e: e.activation(k3[:, :, 0:64], q3[:, :, 0:64], ACT.Copy), tok)
                e2 = V(lambda e: e.tensor_copy(Vb[:, t_off + t, :].rearrange("p (h n) -> p h n", h=8),
                                               q3[:, :, 64:128]), tok, e1)
                V(lambda e: e.tensor_copy(k3[:, :, 64:96], kr[:, t, :].unsqueeze(1).to_broadcast([128, 8, 32])), krt)
                free_pair(qn, [e1, e2])
            release_raw(u, tok)
            if last_ctx:
                fence()
                sub.close()
                return
            g_br = c1("g_branch", i)
            lg_, lb_ = c1("conf_ln_g", i), c1("conf_ln_b", i)
            G_ln = LN[i]
            fence()
            sub2.close()
            mf = sb([128, 4, T], stack=sub)
            for t in range(nt):
                B, bn, w0 = bank()
                tok = transposes([B[:, 128 * c:128 * c + 128] for c in range(2)] +
                                 [B[:, 256 + 128 * c:384 + 128 * c] for c in range(2)],
                                 [Cv[:, c, 128 * t:128 * t + 128] for c in range(2)] +
                                 [S2[:, c, 128 * t:128 * t + 128] for c in range(2)], [w0, V.last()])
                s_ = st[:, 16:32]
                a = V(lambda e: e.bn_stats(s_[:, 0:6], B[:, 0:256]), tok)
                a = V(lambda e: e.bn_aggr(s_[:, 6:8], s_[:, 0:6]), a)
                b = rstd(s_[:, 8:9], s_[:, 7:8], 1, 1.0, 1e-6, a)
                a = V(lambda e: e.tensor_scalar(m1[:, :], B[:, 0:256], s_[:, 6:7], s_[:, 8:9], ALU.subtract, ALU.mult),
                      b, P.last())
                a = V(lambda e: e.tensor_tensor(m1[:, :], m1[:, :], G_ln[:, 0, :], ALU.mult), a)
                a = V(lambda e: e.tensor_tensor(m1[:, :], m1[:, :], G_ln[:, 1, :], ALU.add), a)
                c = A(lambda e: e.activation(m2[:, :], m1[:, :], ACT.Tanh, scale=0.5), a)
                a = V(lambda e: e.tensor_scalar(m2[:, :], m2[:, :], 0.5, 0.5, ALU.mult, ALU.add), c)
                a = V(lambda e: e.tensor_tensor(m1[:, :], m1[:, :], m2[:, :], ALU.mult), a)
                c = sumsq(m1[:, :], J[:, :], s_[:, 9:10], a)
                c = sumsq(B[:, 256:512], J[:, :], s_[:, 10:11], c)
                d = rstd(s_[:, 11:13], s_[:, 9:11], 2, 1.0 / 256, 1e-6, c)
                a = V(lambda e: e.tensor_scalar(m1[:, :], m1[:, :], s_[:, 11:12], None, ALU.mult), d)
                b = V(lambda e: e.tensor_scalar(m2[:, :], B[:, 256:512], s_[:, 12:13], None, ALU.mult), d)
                free_bank(bn, b)
                B2, bn2, w0 = bank()
                tok = transposes([B2[:, 128 * c:128 * c + 128] for c in range(4)],
                                 [m1[:, 0:128], m1[:, 128:256], m2[:, 0:128], m2[:, 128:256]], [a, b, w0])
                a = V(lambda e: e.tensor_tensor(mf[:, :, 128 * t:128 * t + 128],
                                                B2[:, :].rearrange("p (c n) -> p c n", c=4),
                                                g_br[:, 4:8].unsqueeze(2).to_broadcast([128, 4, 128]), ALU.mult), tok)
                free_bank(bn2, a)
            for c in range(4):
                store_split(mf[:, c, :], c, (AH[:, 4 + c, 0:T], AL[:, 4 + c, 0:T]), None, a, adone)
            fence()
            sub.close()
            sub = ExitStack()
            at = Z8[:, :].rearrange("p (t n) -> p t n", t=4)
            attention1(qtm, ktm, Vb, 0, 2 if s else 6, nt, at, sub)
            fence()
            sub.close()
            sub = ExitStack()
            J = sb([128, 512], stack=sub)
            mf = [sb([128, T], stack=sub) for _ in range(2)]
            for t in range(nt):
                tk = sumsq(at[:, t, :], J[:, :], st[:, t:t + 1], A.last())
            tr = rstd(st[:, 8:8 + nt], st[:, 0:nt], nt, 1.0 / 512, 1e-6, tk)
            for t in range(nt):
                a = V(lambda e: e.tensor_scalar(at[:, t, :], at[:, t, :], st[:, 8 + t:9 + t], None, ALU.mult), tr)
            ready = {k: [V.last(), G.last()] for k in range(4, 8)}
            for c in range(4):
                B, bn, w0 = bank()
                tok = transposes([B[:, 128 * t:128 * t + 128] for t in range(nt)],
                                 [at[:, t, 128 * c:128 * c + 128] for t in range(nt)], [a, w0])
                b = A(lambda e: e.activation(mf[c % 2][:, :], B[:, 0:T], ACT.Copy, scale=g_br[:, c:c + 1]), tok,
                      ready.get(c - 2))
                free_bank(bn, b)
                ready[c] = store_split(mf[c % 2][:, :], c, (AH[:, c, 0:T], AL[:, c, 0:T]), None, b)
            fence()
            sub.close()
            return ready

        def project(key, nt, y, ready, act=None):
            for hf in range(2):
                def ev(b, B, tok):
                    if b % 2:
                        return [A(lambda e: e.activation(y[:, b, 512 * hf:512 * hf + 512], B[:, :], ACT.Copy), tok)]
                    return [V(lambda e: e.tensor_copy(y[:, b, 512 * hf:512 * hf + 512], B[:, :]), tok)]
                gemm(key, "TM", act or (AH, AL), 128 * nt, 8, 512, ev, ready)

        def mlp(i, s, x, nt):
            T = 128 * nt
            stk = ExitStack()
            fence()
            row, trow = row_of(GP[:, 1, :, s], stk)
            sub = ExitStack()
            BH, BL = sb([128, 8, T], f32r, stk), sb([128, 8, T], f32r, stk)
            Y = sb([128, nt, 1024], stack=stk)
            ready = prep(x, nt, lambda k: SA1[:, 1, k, s:s + 1], lambda k: MOD[:, 24 + k, s:s + 1], stk, None)
            r = [sb([128, T], stack=stk) for _ in range(3)]
            rfree = [None] * 3
            bfree, cnt = None, 0
            for g in range(4):
                done = {}
                for hf in range(2):
                    def ev(b, B, tok, hf=hf):
                        kk = 4 * hf + b
                        q = r[kk % 3]
                        a = A(lambda e: e.activation(q[:, :], B[:, 0:T], ACT.Relu), tok, rfree[kk % 3])
                        c = V(lambda e: e.tensor_tensor(q[:, :], q[:, :], q[:, :], ALU.mult), a)
                        done[kk] = store_split(q[:, :], kk, (BH[:, kk, :], BL[:, kk, :]), None, c, bfree)
                        rfree[kk % 3] = done[kk]
                        return [a]
                    gemm("w1", "FM", (AH, AL), T, 8, 512, ev, ready)
                for hf in range(2):
                    def ev(b, B, tok, hf=hf, g=g):
                        y = Y[:, b, 512 * hf:512 * hf + 512]
                        if g == 0:
                            ytok[(b, hf)] = V(lambda e: e.tensor_copy(y, B[:, :]), tok)
                        else:
                            ytok[(b, hf)] = V(lambda e: e.tensor_tensor(y, B[:, :], y, ALU.add), tok, ytok[(b, hf)])
                        return [ytok[(b, hf)]]
                    if g == 0 and hf == 0:
                        ytok = {}
                    bfree = gemm("w2", "TM", (BH, BL), T, 8, 512, ev, done)
            residual(x, Y, nt, row, trow, stk, list(ytok.values()))
            fence()
            stk.close()

        LN = [sb([128, 2, 256]) for _ in range(L)]

        def ln_rows():
            for i in range(L):
                B, bn, w0 = bank()
                P.wait(w0)
                for j, name in enumerate(("conf_ln_g", "conf_ln_b")):
                    for c in range(2):
                        col = c1(name, i)[:, c:c + 1].to_broadcast([128, 128])
                        tok = P(lambda e: e.matmul(B[:, 256 * j + 128 * c:256 * j + 128 * c + 128], col, ident,
                                                   start=True, stop=True))
                t = A(lambda e: e.activation(LN[i][:, :, :].rearrange("p a b -> p (a b)"), B[:, :], ACT.Copy), tok)
                free_bank(bn, t)

        def block1():
            for i in range(L):
                mt = modulation(i)
                fence()
                if i == 0:
                    ln_rows()
                stk = ExitStack()
                Z8 = sb([128, 2048], stack=stk)
                qtm = sb([128, 4, 768], stack=stk)
                ktm = sb([128, 6, 768], stack=stk)
                Vb = sb([128, 6, 512], stack=stk)
                zT = sb([128, 3, 512], stack=stk)
                if i == 0:
                    ready = mix1(i, 1, XC, 2, Z8, qtm, ktm, Vb, zT, False, stk, mt)
                    y = Z8[:, :].rearrange("p (t n) -> p t n", t=2)
                    project("wo", 2, y, ready)
                    fence()
                    sub = ExitStack()
                    row, trow = row_of(GP[:, 0, :, 1], sub)
                    residual(XC, y, 2, row, trow, sub, None)
                    fence()
                    sub.close()
                else:
                    mix1(i, 1, XC, 2, Z8, qtm, ktm, Vb, zT, True, stk, mt)
                ready = mix1(i, 0, X, 4, Z8, qtm, ktm, Vb, zT, False, stk, mt)
                fence()
                stk.close()
                stk = ExitStack()
                y = sb([128, 4, 1024], stack=stk)
                row, trow = row_of(GP[:, 0, :, 0], stk)
                project("wo", 4, y, ready)
                fence()
                residual(X, y, 4, row, trow, stk, None)
                fence()
                stk.close()
                if stop == f"mix{i}":
                    return
                if i == 0:
                    mlp(i, 1, XC, 2)
                mlp(i, 0, X, 4)
                if stop == f"mlp{i}":
                    return

        def silu_psum(dst, B, tok, *waits):
            a = A(lambda e: e.activation(dst, B, ACT.Tanh, scale=0.5), tok, *waits)
            b = V(lambda e: e.tensor_scalar(dst, dst, 0.5, 0.5, ALU.mult, ALU.add), a)
            return V(lambda e: e.tensor_tensor(dst, B, dst, ALU.mult), b)

        def gated(i, n, YH, YL, M, ready, yready, stk):
            GT = sb([128, 4, 512], stack=stk)
            bt = c2("gate_b_2", i)
            gf = [None] * 4
            for hf in range(2):
                gt = {}

                def ev_g(b, B, tok):
                    a = V(lambda e: e.tensor_scalar(GT[:, b, :], B[:, :], bt[:, 8 * n + 4 * hf + b:8 * n + 4 * hf + b + 1],
                                                    0.5, ALU.add, ALU.mult), tok, gf[b])
                    c = A(lambda e: e.activation(GT[:, b, :], GT[:, b, :], ACT.Tanh), a)
                    gt[b] = V(lambda e: e.tensor_scalar(GT[:, b, :], GT[:, b, :], 0.5, 0.5, ALU.mult, ALU.add), c)
                    return [a]

                gemm("gate", "FM", (AH, AL), 512, 8, 512, ev_g, ready)

                def ev_b(b, B, tok):
                    m = M[:, 4 * hf + b, :]
                    if n == 0:
                        gf[b] = V(lambda e: e.tensor_tensor(m, B[:, :], GT[:, b, :], ALU.mult), tok, gt[b])
                        return [gf[b]]
                    a = V(lambda e: e.tensor_tensor(GT[:, b, :], B[:, :], GT[:, b, :], ALU.mult), tok, gt[b])
                    gf[b] = V(lambda e: e.tensor_tensor(m, m, GT[:, b, :], ALU.add), a)
                    return [a]

                gemm("br", "FM", (YH, YL), 512, 4, 512, ev_b, yready)

        def delta(i, SM, SZ, M, ready, stk0):
            stk = ExitStack()
            F = [sb([128, 4, 512], stack=stk) for _ in range(3)]
            sub = ExitStack()
            U = sb([128, 4, 515], stack=sub)
            tz = None
            for c in range(4):
                tz = G(lambda e: e.memset(U[:, c, 0:3], 0.0))
            cw = c2("conv_w_2", i).rearrange("p (c k) -> p c k", c=12)
            ufree = [None] * 4
            tmp = sb([128, 512], stack=sub)
            for n, key in enumerate(("qa", "ka", "va")):
                def ev(b, B, tok, n=n):
                    f = F[n][:, b, :]
                    a = A(lambda e: e.activation(U[:, b, 3:515], B[:, :], ACT.Copy), tok, ufree[b])
                    w = cw[:, 4 * n + b, :]
                    t = V(lambda e: e.tensor_scalar(f, U[:, b, 0:512], w[:, 0:1], None, ALU.mult), a, tz)
                    for k in range(1, 4):
                        t = V(lambda e, k=k: e.scalar_tensor_tensor(f, U[:, b, k:k + 512], w[:, k:k + 1], f,
                                                                    ALU.mult, ALU.add), t)
                    ufree[b] = t
                    c = A(lambda e: e.activation(tmp[:, :], f, ACT.Tanh, scale=0.5), t, V.last())
                    t = V(lambda e: e.tensor_scalar(tmp[:, :], tmp[:, :], 0.5, 0.5, ALU.mult, ALU.add), c)
                    V(lambda e: e.tensor_tensor(f, f, tmp[:, :], ALU.mult), t)
                    return [a]
                gemm(key, "FM", (AH, AL), 512, 8, 512, ev, ready)

            def ev_za(b, B, tok):
                return [silu_psum(SZ[:, b, :], B[:, :], tok)]

            gemm("za", "FM", (AH, AL), 512, 8, 512, ev_za, ready)
            fence()
            sub.close()
            be = sb([128, 4, 4], stack=stk)
            gg = sb([128, 4, 4], stack=stk)
            gt = sb([128, 4, 4], stack=stk)
            gc = sb([128, 4, 4], stack=stk)
            ea = sb([128, 4], stack=stk)
            a = A(lambda e: e.activation(be[:, :, :], SM[:, :, 0:4], ACT.Tanh, scale=0.5))
            tbe = V(lambda e: e.tensor_scalar(be[:, :, :], be[:, :, :], 0.5, 0.5, ALU.mult, ALU.add), a)
            t = V(lambda e: e.tensor_tensor(gg[:, :, :], SM[:, :, 4:8],
                                            r2("dt_bias_2", i).unsqueeze(1).to_broadcast([128, 4, 4]), ALU.add))
            t = V(lambda e: e.tensor_scalar(gt[:, :, :], gg[:, :, :], -1.0, None, ALU.mult), t)
            t = V(lambda e: e.tensor_tensor(gt[:, :, :], gt[:, :, :], gg[:, :, :], ALU.min), t)
            c = A(lambda e: e.activation(ea[:, :], r2("a_log_2", i), ACT.Exp))
            c = A(lambda e: e.activation(gt[:, :, :], gt[:, :, :], ACT.Exp), t)
            c = A(lambda e: e.activation(gt[:, :, :], gt[:, :, :], ACT.Ln, bias=1.0), c)
            t = V(lambda e: e.scalar_tensor_tensor(gg[:, :, :], gg[:, :, :], 0.0, gt[:, :, :], ALU.max, ALU.add), c)
            t = V(lambda e: e.tensor_tensor(gg[:, :, :], gg[:, :, :],
                                            ea[:, :].unsqueeze(1).to_broadcast([128, 4, 4]), ALU.mult), t)
            tg = V(lambda e: e.tensor_scalar(gg[:, :, :], gg[:, :, :], -1.0, None, ALU.mult), t)
            B, bn, w0 = bank()
            tok = P(lambda e: e.matmul(B[:, 0:16], con("ut"), gg[:, :, :].rearrange("p a b -> p (a b)"),
                                       start=True, stop=True), tg, w0)
            tgc = V(lambda e: e.tensor_copy(gc[:, :, :].rearrange("p a b -> p (a b)"), B[:, 0:16]), tok)
            free_bank(bn, tgc)
            St = sb([128, 512], stack=stk)
            V(lambda e: e.memset(St[:, :], 0.0))

            def h4(ap):
                return ap.rearrange("p (h n) -> p h n", h=4)

            def bc(col):
                return col.unsqueeze(2).to_broadcast([128, 4, 128])

            def mm4(o, lhs, rhs, start=True, stop=True):
                for h in range(4):
                    tok = P(lambda e, h=h: e.matmul(o[:, 128 * h:128 * h + 128], lhs[:, 128 * h:128 * h + 128],
                                                    rhs[:, 128 * h:128 * h + 128], start=start, stop=stop))
                return tok

            buf = {n: sb([128, 512], stack=stk) for n in
                   ("kn", "vb", "ke", "kd", "kT", "qT", "GR", "Lm", "LT", "AT", "T", "TT", "X")}
            YT = SZ
            D = {n: b_[:, :] for n, b_ in buf.items()}
            lev = con("lev").rearrange("p (s n) -> p s n", s=7)
            Ft = [F[n][:, :, :] for n in range(3)]
            for n in range(4):
                cs = slice(128 * n, 128 * n + 128)
                prev = [e_.last() for e_ in (V, A, G, P)]
                s_ = st[:, 16:64]
                B, b1, w0 = bank()
                tk = transposes([B[:, 128 * h:128 * h + 128] for h in range(4)],
                                [Ft[1][:, h, cs] for h in range(4)], [w0, prev])
                sq = D["X"]
                a = A(lambda e: e.activation(sq, B, ACT.Square), tk, prev)
                a = V(lambda e: e.tensor_reduce(s_[:, 0:4], h4(sq), AX.X, ALU.add), a)
                r = rstd(s_[:, 4:8], s_[:, 0:4], 4, 1.0, 1e-6, a)
                tkn = V(lambda e: e.tensor_tensor(h4(D["kn"]), h4(B), bc(s_[:, 4:8]), ALU.mult), r)
                free_bank(b1, tkn)
                B, b1, w0 = bank()
                tk = transposes([B[:, 128 * h:128 * h + 128] for h in range(4)],
                                [Ft[0][:, h, cs] for h in range(4)], [w0])
                a = A(lambda e: e.activation(sq, B, ACT.Square), tk, a)
                a = V(lambda e: e.tensor_reduce(s_[:, 8:12], h4(sq), AX.X, ALU.add), a)
                r = rstd(s_[:, 12:16], s_[:, 8:12], 4, 1.0, 1e-6, a)
                r = V(lambda e: e.tensor_scalar(s_[:, 12:16], s_[:, 12:16], SM2, None, ALU.mult), r)
                qn = D["T"]
                tqn = V(lambda e: e.tensor_tensor(h4(qn), h4(B), bc(s_[:, 12:16]), ALU.mult), r)
                free_bank(b1, tqn)
                B, b1, w0 = bank()
                tk = transposes([B[:, 128 * h:128 * h + 128] for h in range(4)],
                                [Ft[2][:, h, cs] for h in range(4)], [w0])
                tvb = V(lambda e: e.tensor_tensor(h4(D["vb"]), h4(B), bc(be[:, n, :]), ALU.mult), tk, tbe)
                free_bank(b1, tvb)
                B, b1, w0 = bank()
                P.wait(w0)
                for h in range(4):
                    tk = P(lambda e, h=h: e.matmul(B[:, 128 * h:128 * h + 128],
                                                   gg[:, n, h:h + 1].to_broadcast([128, 128]), con("ut"),
                                                   start=True, stop=True))
                tgr = A(lambda e: e.activation(D["GR"], B, ACT.Copy), tk)
                free_bank(b1, tgr)
                gl = h4(D["GR"])[:, :, 127]
                a = A(lambda e: e.activation(s_[:, 16:20], gc[:, n, :], ACT.Exp), tgc)
                a = V(lambda e: e.tensor_tensor(s_[:, 16:20], s_[:, 16:20], be[:, n, :], ALU.mult), a)
                tke = V(lambda e: e.tensor_tensor(h4(D["ke"]), h4(D["kn"]), bc(s_[:, 16:20]), ALU.mult), a, tkn)
                a = V(lambda e: e.tensor_tensor(s_[:, 20:24], gl, gc[:, n, :], ALU.subtract), tgr, tgc)
                a = A(lambda e: e.activation(s_[:, 20:24], s_[:, 20:24], ACT.Exp), a)
                tkd = V(lambda e: e.tensor_tensor(h4(D["kd"]), h4(D["kn"]), bc(s_[:, 20:24]), ALU.mult), a, tkn)
                tgl = A(lambda e: e.activation(s_[:, 24:28], gl, ACT.Exp), tgr)
                B, b1, w0 = bank()
                tk = transposes([B[:, 128 * h:128 * h + 128] for h in range(4)],
                                [D["kn"][:, 128 * h:128 * h + 128] for h in range(4)], [w0, tkn])
                tkT = A(lambda e: e.activation(D["kT"], B, ACT.Copy), tk)
                free_bank(b1, tkT)
                B, b1, w0 = bank()
                tk = transposes([B[:, 128 * h:128 * h + 128] for h in range(4)],
                                [qn[:, 128 * h:128 * h + 128] for h in range(4)], [w0, tqn])
                tqT = A(lambda e: e.activation(D["qT"], B, ACT.Copy), tk)
                free_bank(b1, tqT)
                mlb = con("ml").unsqueeze(1).to_broadcast([128, 4, 128])
                mub = con("mu").unsqueeze(1).to_broadcast([128, 4, 128])
                E1 = D["X"]
                a = V(lambda e: e.tensor_tensor(h4(E1), mlb, h4(D["GR"]), ALU.subtract), tgr, tqn)
                a = V(lambda e: e.tensor_tensor(h4(E1), h4(E1), bc(gc[:, n, :]), ALU.add), a)
                a = A(lambda e: e.activation(E1, E1, ACT.Exp), a)
                a = V(lambda e: e.tensor_tensor(h4(E1), h4(E1), bc(be[:, n, :]), ALU.mult), a)
                B, b1, w0 = bank()
                P.wait(w0, tkT)
                tk = mm4(B, D["kT"], D["kT"])
                tL = V(lambda e: e.tensor_tensor(D["Lm"], B, E1, ALU.mult), tk, a)
                free_bank(b1, tL)
                B, b1, w0 = bank()
                tk = transposes([B[:, 128 * h:128 * h + 128] for h in range(4)],
                                [D["Lm"][:, 128 * h:128 * h + 128] for h in range(4)], [w0, tL])
                tLT = A(lambda e: e.activation(D["LT"], B, ACT.Copy), tk)
                free_bank(b1, tLT)
                a = V(lambda e: e.tensor_tensor(h4(E1), mub, h4(D["GR"]), ALU.add), tL)
                a = V(lambda e: e.tensor_tensor(h4(E1), h4(E1), bc(gc[:, n, :]), ALU.subtract), a)
                a = A(lambda e: e.activation(E1, E1, ACT.Exp), a)
                B, b1, w0 = bank()
                P.wait(w0, tqT)
                tk = mm4(B, D["kT"], D["qT"])
                tAT = V(lambda e: e.tensor_tensor(D["AT"], B, E1, ALU.mult), tk, a)
                free_bank(b1, tAT)
                a = A(lambda e: e.activation(E1, D["GR"], ACT.Exp), tAT)
                tqg = V(lambda e: e.tensor_tensor(D["qT"], D["qT"], E1, ALU.mult), a, tqT)
                l0 = lev[:, 0, :].unsqueeze(1).to_broadcast([128, 4, 128])
                idb = ident.unsqueeze(1).to_broadcast([128, 4, 128])
                t = V(lambda e: e.tensor_tensor(h4(D["X"]), h4(D["Lm"]), l0, ALU.mult), tqg, tL)
                tT = V(lambda e: e.tensor_tensor(h4(D["T"]), idb, h4(D["X"]), ALU.subtract), t, tqT)
                B, b1, w0 = bank()
                tk = transposes([B[:, 128 * h:128 * h + 128] for h in range(4)],
                                [D["T"][:, 128 * h:128 * h + 128] for h in range(4)], [w0, tT])
                tTT = A(lambda e: e.activation(D["TT"], B, ACT.Copy), tk)
                free_bank(b1, tTT)
                for s in range(1, 7):
                    ls = lev[:, s, :].unsqueeze(1).to_broadcast([128, 4, 128])
                    B, b1, w0 = bank()
                    P.wait(w0, tLT, tT)
                    tk = mm4(B, D["LT"], D["T"])
                    tX = V(lambda e: e.tensor_tensor(h4(D["X"]), h4(B), ls, ALU.mult), tk, P.last())
                    free_bank(b1, tX)
                    B, b1, w0 = bank()
                    P.wait(w0, tX, tTT)
                    tk = mm4(B, D["X"], D["TT"])
                    if s < 6:
                        B2, b2, w0 = bank()
                        P.wait(w0)
                        tk2 = mm4(B2, D["TT"], D["X"])
                    else:
                        tk2 = tk
                    tTT = V(lambda e: e.tensor_tensor(D["TT"], D["TT"], B, ALU.subtract), tk, tk2)
                    free_bank(b1, tTT)
                    if s < 6:
                        tT = V(lambda e: e.tensor_tensor(D["T"], D["T"], B2, ALU.subtract), tk2)
                        free_bank(b2, tT)
                B, b1, w0 = bank()
                P.wait(w0, tTT, tvb, tke)
                tk = mm4(B, D["TT"], D["vb"])
                tu = A(lambda e: e.activation(D["T"], B, ACT.Copy), tk)
                free_bank(b1, tu)
                B, b1, w0 = bank()
                P.wait(w0)
                tk = mm4(B, D["ke"], D["TT"])
                tw = A(lambda e: e.activation(D["X"], B, ACT.Copy), tk)
                free_bank(b1, tw)
                B, b1, w0 = bank()
                P.wait(w0, tw, V.last())
                tk = mm4(B, D["X"], St[:, :])
                tv = V(lambda e: e.tensor_tensor(D["T"], D["T"], B, ALU.subtract), tk, tu)
                free_bank(b1, tv)
                B, b1, w0 = bank()
                P.wait(w0, tqg, tv, tAT)
                for h in range(4):
                    hs_ = slice(128 * h, 128 * h + 128)
                    P(lambda e: e.matmul(B[:, hs_], D["qT"][:, hs_], St[:, hs_], start=True, stop=False))
                    to = P(lambda e: e.matmul(B[:, hs_], D["AT"][:, hs_], D["T"][:, hs_], start=False, stop=True))
                B2, b2, w0 = bank()
                P.wait(w0, tkd)
                tk = mm4(B2, D["kd"], D["T"])
                a = V(lambda e: e.tensor_tensor(h4(St[:, :]), h4(St[:, :]), bc(s_[:, 24:28]), ALU.mult), to, tgl)
                tS = V(lambda e: e.tensor_tensor(St[:, :], St[:, :], B2, ALU.add), a, tk)
                free_bank(b2, tS)
                a = A(lambda e: e.activation(D["X"], B, ACT.Square), to)
                a = V(lambda e: e.tensor_reduce(s_[:, 28:32], h4(D["X"]), AX.X, ALU.add), a)
                r = rstd(s_[:, 32:36], s_[:, 28:32], 4, 1.0 / 128, 1e-6, a)
                a = V(lambda e: e.tensor_tensor(h4(D["X"]), h4(B), bc(s_[:, 32:36]), ALU.mult), r)
                free_bank(b1, a)
                B, b1, w0 = bank()
                tk = transposes([B[:, 128 * h:128 * h + 128] for h in range(4)],
                                [D["X"][:, 128 * h:128 * h + 128] for h in range(4)], [w0, a])
                a = V(lambda e: e.scalar_tensor_tensor(YT[:, :, cs], h4(B), c2("dn_onorm_2", i)[:, 0:1],
                                                       SZ[:, :, cs], ALU.mult, ALU.mult), tk)
                free_bank(b1, a)
            return YT, a, stk

        def to_branch(YT, yt, stk_y):
            YH, YL = sb([128, 4, 512], f32r, stk_y), sb([128, 4, 512], f32r, stk_y)
            yr = {}
            for c in range(4):
                yr[c] = store_split(YT[:, c, :], c, (YH[:, c, :], YL[:, c, :]), None, yt)
            return YH, YL, yr

        def pooling(i, SZ, ready):
            stk = ExitStack()
            U = sb([128, 4, 528], stack=stk)
            YT = sb([128, 4, 512], stack=stk)
            W1, W2 = sb([128, 528], stack=stk), sb([128, 528], stack=stk)
            tz = G(lambda e: e.memset(U[:, :, 0:16], 0.0))
            pooled = {}
            pcs = con("pc").rearrange("p (g n) -> p g n", g=4)

            def ev(b, B, tok):
                a = A(lambda e: e.activation(U[:, b, 16:528], B[:, :], ACT.Copy), tok)
                src, w, t = U[:, b, :], 1, [a, tz]
                bufs = [W1, W2]
                for m in range(b + 1):
                    dst = bufs[m % 2]
                    t = V(lambda e, dst=dst, src=src, w=w: e.tensor_tensor(dst[:, 2 * w - 1:528], src[:, 2 * w - 1:528],
                                                                           src[:, w - 1:528 - w], ALU.add), t)
                    src, w = dst[:, :], 2 * w
                o = YT[:, b, :]
                t = V(lambda e, src=src, w=w: e.scalar_tensor_tensor(o[:, 16:512], src[:, 32:528], 1.0 / w,
                                                                     U[:, b, 32:528], ALU.mult, ALU.subtract), t)
                t1 = V(lambda e, src=src: e.tensor_tensor(o[:, 0:16], src[:, 16:32], pcs[:, b, :], ALU.mult), t)
                pooled[b] = V(lambda e: e.tensor_tensor(o[:, 0:16], o[:, 0:16], U[:, b, 16:32], ALU.subtract), t1)
                return [a]

            gemm("ub", "FM", (AH, AL), 512, 8, 512, ev, ready)
            zt = {}

            def ev_z(b, B, tok):
                zt[b] = silu_psum(SZ[:, b, :], B[:, :], tok)
                return [zt[b]]

            gemm("zb", "FM", (AH, AL), 512, 8, 512, ev_z, ready)
            u = use("pw")
            W = RAW[u % NR][:, 0:512].rearrange("p (g n) -> p g n", g=4)
            ps = c2("pool_scale_2", i)
            for b in range(4):
                B, bn, w0 = bank()
                tok = P(lambda e: e.matmul(B, W[:, b, :], YT[:, b, :], start=True, stop=True), parts[u], w0, pooled[b])
                t = V(lambda e: e.scalar_tensor_tensor(SZ[:, b, :], B, ps[:, b:b + 1], SZ[:, b, :],
                                                       ALU.mult, ALU.mult), tok, zt[b])
                free_bank(bn, t)
            release_raw(u, tok)
            return SZ, t, stk

        def sparse(i, SM, SZ, ready):
            stk = ExitStack()
            KT, QT = sb([128, 4, 512], stack=stk), sb([128, 4, 512], stack=stk)
            VV = sb([128, 4, 512], stack=stk)
            IQ = sb([64, 4, 512], stack=stk)
            IK = sb([64, 512], stack=stk)
            sub = ExitStack()
            TM = sb([128, 4, 512], stack=sub)
            rt = [sb([128, 4, 64], stack=sub) for _ in range(4)]
            sq = sb([128, 512], stack=sub)
            tmfree = []
            rac, ras = (con(n_).rearrange("p (t n) -> p t n", t=4) for n_ in ("rac", "ras"))
            for key, dst, gname in (("kc", KT, "k_norm_2"), ("qc", QT, "q_norm_2")):
                g = r2(gname, i).unsqueeze(1).to_broadcast([128, 4, 128])

                def ev(b, B, tok):
                    nonlocal tmfree
                    a = A(lambda e: e.activation(sq[:, :], B[:, :], ACT.Square), tok, V.last())
                    a = V(lambda e: e.tensor_reduce(st[:, 0:4], sq[:, :].rearrange("p (h n) -> p h n", h=4), AX.X,
                                                    ALU.add), a)
                    r = rstd(st[:, 8:12], st[:, 0:4], 4, 1.0 / 128, 1e-6, a)
                    tm = TM[:, b, :].rearrange("p (h n) -> p h n", h=4)
                    f = V(lambda e: e.tensor_tensor(tm, B[:, :].rearrange("p (h n) -> p h n", h=4),
                                                    st[:, 8:12].unsqueeze(2).to_broadcast([128, 4, 128]), ALU.mult),
                          r, tmfree)
                    a = V(lambda e: e.tensor_tensor(tm, tm, g, ALU.mult), f)
                    co = rac[:, b, :].unsqueeze(1).to_broadcast([128, 4, 64])
                    si = ras[:, b, :].unsqueeze(1).to_broadcast([128, 4, 64])
                    rot[b] = rotate((tm[:, :, 0:64], tm[:, :, 64:128]), tm[:, :, 0:64], tm[:, :, 64:128], co, si,
                                    [x_[:, :, :] for x_ in rt], [a, V.last(), G.last()])
                    return [f]

                rot = {}
                gemm(key, "TM", (AH, AL), 512, 8, 512, ev, ready)
                for h in range(4):
                    B, bn, w0 = bank()
                    tk = transposes([B[:, 128 * t:128 * t + 128] for t in range(4)],
                                    [TM[:, t, 128 * h:128 * h + 128] for t in range(4)],
                                    [w0, [rot[b] for b in range(4)]])
                    a = A(lambda e: e.activation(dst[:, h, :], B, ACT.Copy), tk)
                    free_bank(bn, a)
                tmfree = [tk]

            def ev_v(b, B, tok):
                return [A(lambda e: e.activation(VV[:, b, :], B[:, :], ACT.Copy), tok)]

            gemm("vc", "TM", (AH, AL), 512, 8, 512, ev_v, ready)

            def ev_z(b, B, tok):
                return [silu_psum(SZ[:, b, :], B[:, :], tok)]

            gemm("zc", "FM", (AH, AL), 512, 8, 512, ev_z, ready)
            fence()
            ric, ris = (con(n_).rearrange("p (t n) -> p t n", t=4) for n_ in ("ric", "ris"))
            for t in range(4):
                v = SM[:, t, 8:328].rearrange("p (h n) -> p h n", h=5)
                tmp = [x_[:, :, :].rearrange("p a b -> p (a b)")[:, 0:160].rearrange("p (h n) -> p h n", h=5) for x_ in rt]
                ir = rotate((v[:, :, 0:32], v[:, :, 32:64]), v[:, :, 0:32], v[:, :, 32:64],
                            ric[:, t, :].unsqueeze(1).to_broadcast([128, 5, 32]),
                            ris[:, t, :].unsqueeze(1).to_broadcast([128, 5, 32]), tmp, [V.last(), G.last()])
            for h in range(5):
                B, bn, w0 = bank()
                tk = transposes([B[0:64, 128 * t:128 * t + 128] for t in range(4)],
                                [SM[:, t, 8 + 64 * h:72 + 64 * h] for t in range(4)], [w0, ir])
                dst = IQ[:, h, :] if h < 4 else IK[:, :]
                a = A(lambda e: e.activation(dst, B[0:64, :], ACT.Copy), tk)
                free_bank(bn, a)
            wi = st[:, 48:64].rearrange("p (t h) -> p t h", t=4)
            V(lambda e: e.tensor_scalar(wi, SM[:, :, 328:332], 1.0 / 16, None, ALU.mult))
            fence()
            sub.close()
            YT = SZ
            sc, rl = sb([128, 512], stack=stk), [sb([128, 512], stack=stk) for _ in range(2)]
            bias = sb([128, 512], stack=stk)
            PP = [sb([128, 512], stack=stk) for _ in range(2)]
            PT = [sb([128, 512], stack=stk) for _ in range(2)]
            O = sb([128, 512], stack=stk)
            m8 = st[:, 40:48]
            rlf = [None, None]
            pf, tf, of = [None, None], [None, None], None
            for t in range(4):
                nk = 128 * (t + 1)
                cs = slice(128 * t, 128 * t + 128)
                if t == 0:
                    tb = V(lambda e: e.tensor_copy(bias[:, 0:128], con("cb")))
                else:
                    acc = V.last()
                    for h in range(4):
                        B, bn, w0 = bank()
                        tk = P(lambda e: e.matmul(B[:, 0:nk], IQ[:, h, cs], IK[:, 0:nk], start=True, stop=True), w0)
                        q = rl[h % 2]
                        a = A(lambda e: e.activation(q[:, 0:nk], B[:, 0:nk], ACT.Relu), tk, rlf[h % 2])
                        free_bank(bn, a)
                        w_ = wi[:, t, h:h + 1]
                        if h == 0:
                            acc = V(lambda e: e.tensor_scalar(sc[:, 0:nk], q[:, 0:nk], w_, None, ALU.mult), a)
                        else:
                            acc = V(lambda e: e.scalar_tensor_tensor(sc[:, 0:nk], q[:, 0:nk], w_, sc[:, 0:nk],
                                                                     ALU.mult, ALU.add), a, acc)
                        rlf[h % 2] = acc
                    a = V(lambda e: e.tensor_tensor(sc[:, cs], sc[:, cs], con("tri"), ALU.min), acc)
                    for _ in range(16):
                        a = V(lambda e: e.max(out=m8, in_=sc[:, 0:nk]), a)
                        a = V(lambda e: e.match_replace(out=sc[:, 0:nk], in_to_replace=m8, in_values=sc[:, 0:nk],
                                                        imm_value=MARK), a)
                    tb = V(lambda e: e.tensor_scalar(bias[:, 0:nk], sc[:, 0:nk], -3.2e38, -BIG, ALU.is_gt, ALU.mult),
                           a)
                for h in range(4):
                    n = h % 2
                    hs_ = slice(128 * h, 128 * h + 128)
                    B, bn, w0 = bank()
                    tk = P(lambda e: e.matmul(B[:, 0:nk], QT[:, h, cs], KT[:, h, 0:nk], start=True, stop=True), w0)
                    p = PP[n][:, 0:nk]
                    mx, nm, rs, ri = (st[:, 16 + 4 * n + j:17 + 4 * n + j] for j in range(4))
                    a = V(lambda e: e.tensor_tensor(p, B[:, 0:nk], bias[:, 0:nk], ALU.add), tk, tb, pf[n])
                    free_bank(bn, a)
                    a = V(lambda e: e.tensor_reduce(mx, p, AX.X, ALU.max), a)
                    a = V(lambda e: e.tensor_scalar(nm, mx, -SM2, None, ALU.mult), a)
                    te = A(lambda e: e.activation(p, p, ACT.Exp, bias=nm, scale=SM2, accum_out=rs), a)
                    tr = V(lambda e: e.reciprocal(ri, rs), te)
                    B, bn, w0 = bank()
                    tk = transposes([B[:, 128 * j:128 * j + 128] for j in range(t + 1)],
                                    [PP[n][:, 128 * j:128 * j + 128] for j in range(t + 1)], [w0, te])
                    pf[n] = tk
                    ev_ = A(lambda e: e.activation(PT[n][:, 0:nk], B[:, 0:nk], ACT.Copy), tk, tf[n])
                    free_bank(bn, ev_)
                    B, bn, w0 = bank()
                    P.wait(w0, ev_)
                    for j in range(t + 1):
                        tk = P(lambda e: e.matmul(B[:, 0:128], PT[n][:, 128 * j:128 * j + 128], VV[:, j, hs_],
                                                  start=(j == 0), stop=(j == t)))
                    tf[n] = tk
                    a = V(lambda e: e.tensor_scalar(O[:, hs_], B[:, 0:128], ri, None, ALU.mult), tk, tr, of)
                    free_bank(bn, a)
                B, bn, w0 = bank()
                of = transposes([B[:, 128 * h:128 * h + 128] for h in range(4)],
                                [O[:, 128 * h:128 * h + 128] for h in range(4)], [w0, a])
                ty = V(lambda e: e.tensor_tensor(YT[:, :, cs], B.rearrange("p (h n) -> p h n", h=4), SZ[:, :, cs],
                                                 ALU.mult), of)
                free_bank(bn, ty)
            return YT, ty, stk

        def block2():
            for i in range(L):
                fence()
                base = ExitStack()
                M = sb([128, 8, 512], stack=base)
                SM = sb([128, 4, 332], stack=base)
                SZ = sb([128, 4, 512], stack=base)
                sub = ExitStack()
                ready = prep(X, 4, lambda k: c2("norm_g_2", i)[:, k:k + 1], None, sub, None)

                def ev_s(b, B, tok):
                    return [A(lambda e: e.activation(SM[:, b, :], B[:, 0:332], ACT.Copy), tok)]

                gemm("sm", "TM", (AH, AL), 512, 8, 332, ev_s, ready)
                fence()
                sub.close()
                for n in range(3):
                    if n == 0:
                        YT, yt, stk = delta(i, SM, SZ, M, ready, base)
                    elif n == 1:
                        YT, yt, stk = pooling(i, SZ, ready)
                    else:
                        YT, yt, stk = sparse(i, SM, SZ, ready)
                    fence()
                    stk.close()
                    sub = ExitStack()
                    YH, YL, yr = to_branch(SZ, yt, sub)
                    gated(i, n, YH, YL, M, ready, yr, sub)
                    fence()
                    sub.close()
                    if stop == f"br{i}{n}":
                        V(lambda e: e.tensor_copy(X[:, :, :].rearrange("p t n -> p (t n)"),
                                                  M[:, :, :].rearrange("p t n -> p (t n)")))
                        return
                mr = {k: store_split(M[:, k, :], k, (AH[:, k, :], AL[:, k, :]), None) for k in range(8)}
                for hf in range(2):
                    def ev(b, B, tok):
                        xs = X[:, b, 512 * hf:512 * hf + 512]
                        return [V(lambda e: e.tensor_tensor(xs, xs, B[:, :], ALU.add), tok)]
                    gemm("wout", "TM", (AH, AL), 512, 8, 512, ev, mr)
                fence()
                base.close()
                if stop == f"l{i}":
                    return

        if stop != "b2only":
            block1()
        else:
            while state["used"] < next(j for j, u in enumerate(units) if u[0] == "sm"):
                u = state["used"]
                state["used"] += 1
                release_raw(u, parts[u])
        if stop is None or stop[0] in "bl":
            block2()
        fence()
        s_out = sem("s_out")
        S.wait(V.last(), A.last(), G.last(), P.last())
        t = S.dma(lambda e: e.dma_start(a_out.rearrange("b (t p) d -> p (b t) d", p=128), X[:, :, :]), s_out)
        S.wait(t)
        for p in s_raw:
            if p.n:
                S.wait((p, p.n))


def pack(inputs):
    a = {k: np.asarray(v) for k, v in inputs.items()}

    def unit(u):
        _, name, index, row, tiles, cols = u
        m = a[name][index]
        if name == "pool_w_2":
            return m.transpose(1, 0, 2).reshape(-1)
        m = np.concatenate([m[row:row + 128 * tiles, c0:c1] for c0, c1 in cols], axis=1)
        return m.reshape(tiles, 128, -1).transpose(1, 0, 2).reshape(-1)

    def col(v):
        return v.reshape(-1, 128).T

    def taps(w):
        return w.reshape(w.shape[0], -1, 128).transpose(2, 1, 0).reshape(128, -1)

    def cols(parts, i):
        return np.concatenate([taps(a[n][i]) if n in ("conf_dw_w", "sc_dw_w", "conv_w_2") else col(a[n][i])
                               for n, _ in parts], axis=1)

    def tiled(v, nt):
        return v.reshape(nt, 128, -1).transpose(1, 0, 2)

    out = {
        "wbig": np.concatenate([unit(u) for u in plan()]),
        "x": tiled(a["x"], 4),
        "ctx": tiled(a["ctx"], 2),
        "cv": np.stack([col(a["c"]), col(a["c_ctx"])], axis=2),
        "cols1": np.stack([cols(COLS1, i) for i in range(L)], axis=1),
        "cols2": np.stack([cols(COLS2, i) for i in range(L)], axis=1),
        "rows2": np.stack([np.concatenate([np.broadcast_to(a[n][i][None, :], (128, w)) for n, w in ROWS2], axis=1)
                           for i in range(L)], axis=1),
        "const": constants(),
    }
    return {"in_" + k: np.ascontiguousarray(v) for k, v in out.items()}


def kernel(**inputs):
    import concourse.bacc as _bacc
    from concourse.bass_utils import run_bass_kernel_spmd as _run

    arrays = pack(inputs)
    nc = _bacc.Bacc("TRN2", target_bir_lowering=False, num_devices=1)
    args = [nc.dram_tensor(k, v.shape, mybir.dt.from_np(v.dtype), kind="ExternalInput").ap()
            for k, v in arrays.items()]
    args.append(nc.dram_tensor("out_0", (1, 512, 1024), mybir.dt.float32, kind="ExternalOutput").ap())
    program(nc, *args)
    r = _run(nc, [arrays], core_ids=[0])
    return r.results[0]["out_0"]
```

```python
import math
from contextlib import ExitStack

import numpy as np
import concourse.bass as bass
from concourse import mybir

L = 2
NH, QD = 8, 96
BIG = 1.0e30
SMALL = -3.0e38
MARK = -3.3e38
SM1 = 1.0 / math.sqrt(96.0)
SM2 = 128.0 ** -0.5

IN1 = [("zt", [(0, 416)]), ("cf", [(416, 928)]), ("sc", [(1184, 1696)]), ("sb", [(928, 1184)])]
IN2 = {"sm": [(2048, 2056), (5128, 5452)], "qa": [(0, 512)], "ka": [(512, 1024)], "va": [(1024, 1536)],
       "za": [(1536, 2048)], "ub": [(2056, 2568)], "zb": [(2568, 3080)], "qc": [(3080, 3592)],
       "kc": [(3592, 4104)], "vc": [(4104, 4616)], "zc": [(4616, 5128)]}


def gate_cols(n, half):
    at = 5452 + 1024 * n + 512 * half
    return [(at, at + 512)]


def width(cols):
    return sum(b - a for a, b in cols)


def plan():
    out = []

    def block(key, name, index, row, tiles, cols):
        for r in range(0, tiles, 2):
            out.append((key, name, index, row + 128 * r, 2, cols))

    def mix1(i, last_ctx=False):
        for key, cols in IN1[:1] if last_ctx else IN1:
            block(key, "w_in", (i,), 0, 8, cols)
        if not last_ctx:
            for h in range(2):
                out.append(("wq", "w_q_b", (i,), 0, 2, [(384 * h, 384 * h + 384)]))
        out.append(("wkv", "w_kv_b", (i,), 0, 1, [(0, 1024)]))
        if not last_ctx:
            for h in range(2):
                block("wo", "w_o", (i,), 0, 8, [(512 * h, 512 * h + 512)])

    def mlp(i):
        for g in range(4):
            for h in range(2):
                block("w1", "w_mlp_in", (i,), 0, 8, [(1024 * g + 512 * h, 1024 * g + 512 * h + 512)])
            for h in range(2):
                block("w2", "w_mlp_out", (i,), 1024 * g, 8, [(512 * h, 512 * h + 512)])

    mix1(0)
    mix1(0)
    mlp(0)
    mlp(0)
    mix1(1, last_ctx=True)
    mix1(1)
    mlp(1)

    def gate(i, n, h):
        block("gate", "w_in_2", (i,), 0, 8, gate_cols(n, h))

    def br(i, n, h):
        block("br", "w_branch_2", (i, n), 0, 4, [(512 * h, 512 * h + 512)])

    for i in range(L):
        for key in ("sm", "qa", "ka", "va", "za", "ub", "zb"):
            block(key, "w_in_2", (i,), 0, 8, IN2[key])
        out.append(("pw", "pool_w_2", (i,), 0, 4, [(0, 128)]))
        for h in range(2):
            gate(i, 1, h)
            br(i, 1, h)
        for key in ("kc", "qc", "vc", "zc"):
            block(key, "w_in_2", (i,), 0, 8, IN2[key])
        for h in range(2):
            gate(i, 0, h)
            br(i, 0, h)
        for h in range(2):
            gate(i, 2, h)
        for h in range(2):
            br(i, 2, h)
        for h in range(2):
            block("wout", "w_out_2", (i,), 0, 8, [(512 * h, 512 * h + 512)])
    return out


def mod_plan(i):
    return [("mod", "w_mod", (i,), 0, 8, [(256 * j, 256 * j + 256)]) for j in range(24)]


COLS1 = [("b_mod", 48), ("g_pre_mix", 8), ("g_post_mix", 8), ("g_pre_mlp", 8), ("g_post_mlp", 8),
         ("g_q", 2), ("g_kv", 1), ("conf_dw_w", 62), ("conf_dw_b", 2), ("conf_ln_g", 2), ("conf_ln_b", 2),
         ("sc_dw_w", 6), ("g_branch", 8)]
COLS2 = [("norm_g_2", 8), ("gate_b_2", 24), ("conv_w_2", 48), ("dn_onorm_2", 1), ("pool_scale_2", 4)]
ROWS2 = [("a_log_2", 4), ("dt_bias_2", 4), ("q_norm_2", 128), ("k_norm_2", 128)]


def places(parts):
    at, out = 0, {}
    for name, n in parts:
        out[name] = (at, at + n)
        at += n
    return out, at


CONSTS = [("ident", 128), ("ut", 128), ("ml", 128), ("mu", 128), ("lev", 7 * 128), ("tri", 128), ("cb", 128),
          ("pc", 64), ("r1c", 4 * 16), ("r1s", 4 * 16), ("rac", 4 * 64), ("ras", 4 * 64),
          ("ric", 4 * 32), ("ris", 4 * 32)]


def constants():
    at, n = places(CONSTS)
    c = np.zeros((128, n), np.float32)

    def put(name, a):
        c[:, at[name][0]:at[name][1]] = np.asarray(a, np.float32).reshape(128, -1)

    i, j = np.arange(128)[:, None], np.arange(128)[None, :]
    put("ident", i == j)
    put("ut", i <= j)
    put("ml", np.where(j < i, 0.0, -BIG))
    put("mu", np.where(i <= j, 0.0, -BIG))
    put("lev", np.stack([(i // (2 << s) == j // (2 << s)) & ((i >> s) % 2 == 1) & ((j >> s) % 2 == 0)
                         for s in range(7)], 1))
    put("tri", np.where(j <= i, 3.3e38, SMALL))
    put("cb", np.where(j <= i, 0.0, -BIG))
    pc = np.zeros((4, 16), np.float32)
    for g, w in enumerate((2, 4, 8, 16)):
        pc[g] = np.float32(1.0) / np.minimum(np.arange(1, 17), w).astype(np.float32)
    put("pc", np.broadcast_to(pc.reshape(1, 64), (128, 64)))

    def tables(pos, dim):
        inv = (10000.0 ** (-np.arange(0, dim, 2, dtype=np.float64) / dim)).astype(np.float32)
        ang = (pos.astype(np.float32)[:, None] * inv[None, :]).astype(np.float64)
        return np.cos(ang).astype(np.float32), np.sin(ang).astype(np.float32)

    def tiled(a):
        return a.reshape(4, 128, -1).transpose(1, 0, 2)

    t = np.arange(512)
    inv = (1.0 / (10000.0 ** (np.arange(0, 16, 2, dtype=np.float64) / 16)).astype(np.float32)).astype(np.float32)
    ar = ((t // 64).astype(np.float32)[:, None] * inv).astype(np.float64)
    ac = ((t % 64).astype(np.float32)[:, None] * inv).astype(np.float64)
    both = np.concatenate([ar, ac], 1)
    put("r1c", tiled(np.cos(both)))
    put("r1s", tiled(np.sin(both)))
    for name, dim in (("ra", 128), ("ri", 64)):
        co, si = tables(t, dim)
        put(name + "c", tiled(co))
        put(name + "s", tiled(si))
    return c


class Sem:
    def __init__(self, handle, name):
        self.h, self.name, self.n = handle, name, 0


class Engine:

    def __init__(self, eng, sem, chain, task):
        self.eng, self.sem, self.chain, self.seen, self.task = eng, sem, chain, {}, task

    def wait(self, *toks):
        for t in toks:
            if t is None:
                continue
            if isinstance(t, list):
                self.wait(*t)
                continue
            sem, value = t
            if self.seen.get(sem.name, 0) < value:
                self.seen[sem.name] = value
                self.eng.wait_ge(sem.h, value)

    def __call__(self, make, *waits):
        self.wait(*waits)
        if self.chain:
            self.wait(self.last())
        self.sem.n += 1
        make(self.eng).then_inc(self.sem.h, 1)
        self.task[0].lasts[self.sem.name] = (self.sem, self.sem.n)
        return (self.sem, self.sem.n)

    def quiet(self, make, *waits):
        self.wait(*waits)
        make(self.eng)

    def dma(self, make, sem, *waits):
        self.wait(*waits)
        sem.n += 16
        make(self.eng).then_inc(sem.h, 16)
        return (sem, sem.n)

    def last(self):
        return (self.sem, self.sem.n) if self.sem.n else None


class Task:

    def __init__(self, banks, small, st):
        self.gb, self.small, self.st, self.lasts = banks, small, st, {}


class Scope:

    def __init__(self, arena, task):
        self.arena, self.task, self.held = arena, task, []

    def close(self):
        for a, b in self.held:
            self.arena.free(a, b, list(self.task[0].lasts.values()))
        self.held = []


class Arena:

    def __init__(self, lo, hi):
        self.holes = [(lo, hi, [])]

    def take(self, n):
        n = (n + 31) // 32 * 32
        total, start, toks = 0, None, []
        for a, b, t in self.holes:
            if start is None or a != start + total:
                start, total, toks = a, 0, []
            total, toks = total + b - a, toks + t
            if total >= n:
                break
        assert start is not None and total >= n, (n, [(a, b) for a, b, _ in self.holes])
        out = []
        for a, b, t in self.holes:
            if b <= start or a >= start + n:
                out.append((a, b, t))
            elif b > start + n:
                out.append((start + n, b, t))
        self.holes = out
        return start, start + n, toks

    def free(self, a, b, toks):
        self.holes = sorted(self.holes + [(a, b, toks)], key=lambda h: h[0])


def program(nc, a_wbig, a_wmod, a_x, a_ctx, a_cv, a_cols1, a_cols2, a_rows2, a_const, a_out, stop=None):
    f32, f32r = mybir.dt.float32, mybir.dt.float32r
    ALU, ACT, AX = mybir.AluOpType, mybir.ActivationFunctionType, mybir.AxisListType
    C1, NC1 = places(COLS1)
    C2, NC2 = places(COLS2)
    R2, NR2 = places(ROWS2)
    CC, NCC = places(CONSTS)
    units = plan()
    ctx = ExitStack()
    with ctx:
        names = [0]
        arena = Arena((nc.sbuf_base + 31) // 32 * 32, nc.sbuf_top // 32 * 32)
        task = [None]

        def scope():
            return Scope(arena, task)

        whole = scope()

        def sb(shape, dt=f32, stack=None):
            names[0] += 1
            a, b, toks = arena.take(4 * int(np.prod(shape[1:])))
            (stack or whole).held.append((a, b))
            for e_ in (V, A, G, P, S):
                e_.wait(*toks)
            return nc.alloc_sbuf_tensor_at(f"t{names[0]}", shape, dt, offset=a)

        def sem(name):
            return Sem(ctx.enter_context(nc.semaphore(name)), name)

        V, A, G, P, S = (Engine(e, sem(n), n in ("s_v", "s_a", "s_g"), task) for e, n in ((nc.vector, "s_v"), (nc.scalar, "s_a"), (nc.gpsimd, "s_g"),
                                                        (nc.tensor, "s_p"), (nc.sync, "s_s")))

        X = sb([128, 4, 1024])
        first = scope()
        XC = sb([128, 2, 1024], stack=first)
        AH, AL = sb([128, 8, 512], f32r), sb([128, 8, 512], f32r)
        NR, NS = 3, 3
        RAW = [sb([128, 1024]) for _ in range(NR)]
        WH = [sb([128, 1024], f32r) for _ in range(NS)]
        WL = [sb([128, 1024], f32r) for _ in range(NS)]
        K = sb([128, NCC])
        cols1 = sb([128, L, NC1])
        cols2 = sb([128, L, NC2])
        rows2 = sb([128, L, NR2])
        SCV = sb([128, 8, 2])
        MODS = [sb([128, 48, 2], stack=first) for _ in range(L)]
        SA1S = [sb([128, 2, 8, 2], stack=first) for _ in range(L)]
        GPS = [sb([128, 2, 8, 2], stack=first) for _ in range(L)]
        half = sb([128, 16])

        def con(name):
            return K[:, CC[name][0]:CC[name][1]]

        def c1(name, i):
            return cols1[:, i, C1[name][0]:C1[name][1]]

        def c2(name, i):
            return cols2[:, i, C2[name][0]:C2[name][1]]

        def r2(name, i):
            return rows2[:, i, R2[name][0]:R2[name][1]]

        ident = con("ident")

        PS = ctx.enter_context(nc.psum_tensor("ps", [128, 4096], f32))
        BK = [PS[:, 512 * n:512 * n + 512] for n in range(8)]
        bfree = [[] for _ in range(8)]
        busy = [False] * 8
        main, side = (Task(list(b_), list(c_), sb([128, 64])) for b_, c_ in
                      (((0, 1, 2, 3), (4, 5, 6, 7)), ((4, 5, 6, 7), (4, 5, 6, 7))))
        task[0] = main

        def pair():
            sm = task[0].small
            n = next(n for n in sm if n % 2 == 0 and n + 1 in sm and not busy[n] and not busy[n + 1])
            sm.remove(n)
            sm.remove(n + 1)
            sm += [n, n + 1]
            busy[n] = busy[n + 1] = True
            return PS[:, 512 * n:512 * n + 1024], n, bfree[n] + bfree[n + 1]

        def free_pair(n, toks):
            for m in (n, n + 1):
                busy[m] = False
                bfree[m] = list(toks)

        def bank():
            sm = task[0].small
            n = next(n for n in sm if not busy[n])
            sm.remove(n)
            sm.append(n)
            busy[n] = True
            return BK[n], n, list(bfree[n])

        def free_bank(n, *toks):
            busy[n] = False
            bfree[n] = list(toks)

        def run(gen):
            for _ in gen:
                pass

        def both(gen, other, ratio=1.0):
            due, left = 0.0, True
            main.small = list(main.gb)
            side.lasts = dict(main.lasts)
            for _ in gen:
                due += ratio
                while left and due >= 1.0:
                    due -= 1.0
                    task[0] = side
                    left = next(other, "end") != "end"
                task[0] = main
            task[0] = side
            side.small, side.spare = list(range(4, 8)), None
            if left:
                run(other)
            task[0] = main
            main.small = [4, 5, 6, 7]
            for k_, v_ in side.lasts.items():
                main.lasts[k_] = max(main.lasts.get(k_, v_), v_, key=lambda t: t[1])

        s_in = sem("s_in")
        s_raw = [sem(f"s_raw{n}") for n in range(NR)]
        for dst, src in ((K[:, :], a_const), (SCV[:, :, :], a_cv), (cols1[:, :, :], a_cols1),
                         (cols2[:, :, :], a_cols2), (rows2[:, :, :], a_rows2),
                         (XC[:, :, :], a_ctx), (X[:, :, :], a_x)):
            S.dma(lambda e, dst=dst, src=src: e.dma_start(dst, src), s_in)
        loaded = (s_in, s_in.n)

        offs, at = [], 0
        for u in units:
            offs.append(at)
            at += 128 * u[4] * width(u[5])
        raw_free = [[] for _ in range(NR)]
        w_free = [[] for _ in range(NS)]
        state = {"fetched": 0, "split": 0, "used": 0, "nsplit": 0}
        parts = {}

        def fetch():
            u = state["fetched"]
            if u >= len(units):
                return
            n = units[u][4] * width(units[u][5])
            src = a_wbig[offs[u]:offs[u] + 128 * n].rearrange("(p n) -> p n", p=128)
            dst = RAW[u % NR][:, 0:n]
            parts[u] = S.dma(lambda e: e.dma_start(dst, src), s_raw[u % NR], raw_free[u % NR])
            state["fetched"] += 1

        released = set()

        def release_raw(u, *toks):
            raw_free[u % NR] = list(toks)
            released.add(u)
            while state["fetched"] < len(units) and state["fetched"] - NR in released:
                fetch()

        for _ in range(NR):
            fetch()

        def direct(u):
            return units[u][0] in ("wq", "wkv", "pw")

        split_of = {}

        def split(u):
            if u >= len(units) or u in split_of or direct(u):
                return
            n = units[u][4] * width(units[u][5])
            s = state["nsplit"] % NS
            state["nsplit"] += 1
            raw, hi, lo = RAW[u % NR][:, 0:n], WH[s][:, 0:n], WL[s][:, 0:n]
            t1 = A(lambda e: e.activation(hi, raw, ACT.Copy), parts[u], w_free[s])
            t2 = G(lambda e: e.tensor_tensor(lo, raw, hi.bitcast(f32), ALU.subtract), parts[u], t1, w_free[s])
            split_of[u] = (s, hi, lo, t1, t2)
            release_raw(u, t1, t2)

        def use(key):
            u = state["used"]
            state["used"] += 1
            assert units[u][0] == key, (units[u][0], key)
            return u

        def gemm(key, mode, act, T, tiles, w, evac, ready):
            aH, aL = act
            nb = T // 128 if mode == "TM" else w // 128
            GB, gfree = [BK[n] for n in task[0].gb], bfree
            for kh in range(tiles // 2):
                u = use(key)
                split(u)
                split(u + 1)
                if u + 2 < state["fetched"]:
                    split(u + 2)
                s, hi, lo, t1, t2 = split_of[u]
                hi3, lo3 = hi.rearrange("p (k n) -> p k n", k=2), lo.rearrange("p (k n) -> p k n", k=2)
                for k in range(2):
                    kk = 2 * kh + k
                    P.wait(t1, t2, ready[kk] if isinstance(ready, dict) else ready)
                    for b in range(nb):
                        if kk == 0:
                            P.wait(gfree[task[0].gb[b]])
                        for n, (wp, ap) in enumerate(((hi3, aH), (hi3, aL), (lo3, aH))):
                            if mode == "TM":
                                lhs, rhs = ap[:, kk, 128 * b:128 * b + 128], wp[:, k, :]
                                out = GB[b][:, 0:w]
                            else:
                                lhs, rhs = wp[:, k, 128 * b:128 * b + 128], ap[:, kk, 0:T]
                                out = GB[b][:, 0:T]
                            first, final = kk == 0 and n == 0, kk == tiles - 1 and n == 2

                            def mm(e, out=out, lhs=lhs, rhs=rhs, first=first, final=final):
                                return e.matmul(out, lhs, rhs, start=first, stop=final)

                            if n == 2 and (final or (k == 1 and b == nb - 1)):
                                tok = P(mm)
                            else:
                                P.quiet(mm)
                        if kk == tiles - 1:
                            gfree[task[0].gb[b]] = evac(b, GB[b], tok)
                        if b % 2:
                            yield
                w_free[s] = [tok]
            return tok

        def rstd(out, ss, n, inv, eps, *waits):
            t = V(lambda e: e.tensor_scalar(out, ss, inv, eps, ALU.mult, ALU.add), *waits)
            return G(lambda e: e.tensor_tensor(out, out, half[:, 0:n], ALU.pow), t)

        def sumsq(src, junk, out, *waits):
            return A(lambda e: e.activation(junk, src, ACT.Square, accum_out=out), *waits)

        t0 = G(lambda e: e.memset(half[:, :], -0.5))
        for e_ in (V, A, G, P):
            e_.wait(loaded)
        P.wait(t0)
        th = main.st[:, 0:16].rearrange("p (a b) -> p a b", a=8)
        t1 = A(lambda e: e.activation(th, SCV[:, :, :], ACT.Tanh, scale=0.5))
        t1 = V(lambda e: e.tensor_scalar(th, th, 0.5, 0.5, ALU.mult, ALU.add), t1)
        scv_ready = V(lambda e: e.tensor_tensor(SCV[:, :, :], SCV[:, :, :], th, ALU.mult), t1)

        def fence():
            toks = list(task[0].lasts.values())
            for e_ in (V, A, G, P):
                e_.wait(*toks)

        s_mod = [sem(f"s_mod{n}") for n in range(8)]
        modtok = {}

        def modulation(i, slots):
            B, bn, w0 = bank()
            P.wait(scv_ready, w0)
            sc = scope()
            ring = [sb([128, 2048], stack=sc) for _ in range(slots)]
            free = [[] for _ in range(slots)]
            got = {}

            def load(j):
                if j < 24:
                    src = a_wmod[(24 * i + j) * 262144:(24 * i + j + 1) * 262144].rearrange("(p n) -> p n", p=128)
                    got[j] = S.dma(lambda e: e.dma_start(ring[j % slots][:, :], src), s_mod[j % slots], free[j % slots])

            for j in range(slots):
                load(j)
            for j in range(24):
                W = ring[j % slots][:, :].rearrange("p (k n) -> p k n", k=8)
                P.wait(got[j])
                for c in range(2):
                    for k in range(8):
                        o = B[:, 2 * (2 * j + c):2 * (2 * j + c) + 2]

                        def mm(e, o=o, W=W, k=k, c=c):
                            return e.matmul(o, W[:, k, 128 * c:128 * c + 128], SCV[:, k, :],
                                            start=(k == 0), stop=(k == 7))

                        if k == 7 and c == 1:
                            tok = P(mm)
                        else:
                            P.quiet(mm)
                    yield
                free[j % slots] = [tok]
                load(j + slots)
            sc.close()
            bm = c1("b_mod", i)
            t = V(lambda e: e.tensor_tensor(MODS[i][:, :, :], B[:, 0:96].rearrange("p (a b) -> p a b", b=2),
                                            bm.unsqueeze(2).to_broadcast([128, 48, 2]), ALU.add), tok)
            free_bank(bn, t)
            for m, (pre, post) in enumerate((("g_pre_mix", "g_post_mix"), ("g_pre_mlp", "g_post_mlp"))):
                gp, gq = c1(pre, i), c1(post, i)
                sc, gt = MODS[i][:, 24 * m + 8:24 * m + 16, :], MODS[i][:, 24 * m + 16:24 * m + 24, :]
                t1 = V(lambda e: e.tensor_scalar(SA1S[i][:, m, :, :], sc, 1.0, None, ALU.add), t)
                t1 = V(lambda e: e.tensor_tensor(SA1S[i][:, m, :, :], SA1S[i][:, m, :, :],
                                                 gp.unsqueeze(2).to_broadcast([128, 8, 2]), ALU.mult), t1)
                t2 = V(lambda e: e.tensor_tensor(GPS[i][:, m, :, :], gt,
                                                 gq.unsqueeze(2).to_broadcast([128, 8, 2]), ALU.mult), t)
            modtok[i] = [t, t1, t2]

        def store_split(src, k, dst, tmp_free, *waits):
            h, l = dst
            t1 = V(lambda e: e.tensor_copy(h, src), *waits)
            t2 = G(lambda e: e.tensor_tensor(l, src, h.bitcast(f32), ALU.subtract), t1, *waits)
            return [t1, t2]

        def prep(x, nt, scale, shift, stk, afree):
            T = 128 * nt
            A.wait(afree)
            J, jn, w0 = pair()
            tk = None
            for t in range(nt):
                tk = sumsq(x[:, t, :], J[:, :], task[0].st[:, t:t + 1], w0 if t == 0 else None)
            free_pair(jn, [tk])
            r = task[0].st[:, 8:8 + nt]
            tr = rstd(r, task[0].st[:, 0:nt], nt, 1.0 / 1024, 1e-6, tk)
            xn = [sb([128, nt, 128], stack=stk) for _ in range(2)]
            tm = [sb([128, T], stack=stk) for _ in range(2)]
            xfree, tfree = [None, None], [[], []]
            ready = {}
            for k in range(8):
                y, f = xn[k % 2], tm[k % 2]
                a = V(lambda e: e.tensor_tensor(y[:, :, :], x[:, :, 128 * k:128 * k + 128],
                                                r.unsqueeze(2).to_broadcast([128, nt, 128]), ALU.mult),
                      tr, xfree[k % 2])
                B, bn, w0 = bank()
                P.wait(a, w0)
                for t in range(nt):
                    def tp(e, t=t):
                        return e.transpose(B[:, 128 * t:128 * t + 128], y[:, t, :], ident)
                    if t < nt - 1:
                        P.quiet(tp)
                    else:
                        tok = P(tp)
                xfree[k % 2] = tok
                if shift is None:
                    e1 = A(lambda e: e.activation(f[:, :], B[:, 0:T], ACT.Copy, scale=scale(k)), tok, tfree[k % 2])
                else:
                    e1 = A(lambda e: e.activation(f[:, :], B[:, 0:T], ACT.Identity, bias=shift(k),
                                                  scale=scale(k)), tok, tfree[k % 2])
                free_bank(bn, e1)
                ready[k] = store_split(f[:, :], k, (AH[:, k, 0:T], AL[:, k, 0:T]), None, e1, afree)
                tfree[k % 2] = ready[k]
            return ready

        def row_of(col, stk, *waits):
            row = sb([128, 1024], stack=stk)
            Q, qn, w0 = pair()
            P.wait(w0, *waits)
            for j in range(8):
                tok = P(lambda e: e.matmul(Q[:, 128 * j:128 * j + 128],
                                           col[:, j:j + 1].to_broadcast([128, 128]), ident, start=True, stop=True))
            t = A(lambda e: e.activation(row[:, :], Q[:, :], ACT.Copy), tok)
            free_pair(qn, [t])
            return row, t

        def residual(x, y, nt, row, trow, stk, ready):
            J, jn, w0 = pair()
            for t in range(nt):
                tk = sumsq(y[:, t, :], J[:, :], task[0].st[:, t:t + 1], w0 if t == 0 else None, ready)
            free_pair(jn, [tk])
            r = task[0].st[:, 8:8 + nt]
            tr = rstd(r, task[0].st[:, 0:nt], nt, 1.0 / 1024, 1e-6, tk)
            for t in range(nt):
                a = V(lambda e: e.scalar_tensor_tensor(y[:, t, :], y[:, t, :], r[:, t:t + 1], row[:, :],
                                                       ALU.mult, ALU.mult), tr, trow)
                V(lambda e: e.tensor_tensor(x[:, t, :], x[:, t, :], y[:, t, :], ALU.add), a)

        def rotate(dst, p1, p2, co, si, tmp, waits):
            d1, d2 = dst
            ta, tb, tc, td = tmp
            a = V(lambda e: e.tensor_tensor(ta, p1, co, ALU.mult), *waits)
            b = V(lambda e: e.tensor_tensor(tb, p2, si, ALU.mult))
            c = G(lambda e: e.tensor_tensor(tc, p2, co, ALU.mult), *waits)
            d = G(lambda e: e.tensor_tensor(td, p1, si, ALU.mult))
            u = V(lambda e: e.tensor_tensor(d1, ta, tb, ALU.subtract), a, b, c, d)
            return [u, V(lambda e: e.tensor_tensor(d2, tc, td, ALU.add), c, d)]

        def transposes(out, srcs, waits):
            P.wait(*waits)
            for j, (o, s_) in enumerate(zip(out, srcs)):
                f = (lambda e, o=o, s_=s_: e.transpose(o, s_, ident))
                if j < len(srcs) - 1:
                    P.quiet(f)
                else:
                    return P(f)

        def attention1(qtm, ktm, Vb, nk, nt, Z8, stk):
            KT = [sb([96, nk * 128], stack=stk) for _ in range(2)]
            QT = [sb([96, nt * 128], stack=stk) for _ in range(2)]
            PP = [sb([128, nk * 128], stack=stk) for _ in range(3)]
            PT = [sb([128, nk * 128], stack=stk) for _ in range(2)]
            sm = task[0].st
            free_h, free_p, free_t, free_s = [[], []], [None] * 3, [None] * 2, [None] * 3
            nh = (nk + 1) // 2 * 128
            was = task[0].small
            task[0].small = list(range(8))
            kq = {}

            def load_head(h, last):
                b = h % 2
                Q, qn, w0 = pair()
                tok = transposes([Q[0:96, 128 * t:128 * t + 128] for t in range(nt)],
                                 [qtm[:, t, 96 * h:96 * h + 96] for t in range(nt)], [w0])
                eq = A(lambda e: e.activation(QT[b][:, :], Q[0:96, 0:128 * nt], ACT.Copy), tok, free_h[b])
                got, at = [eq], eq
                for k0 in range(0, nk, 4):
                    kn = min(4, nk - k0)
                    base = 512 if k0 == 0 else 0
                    tok = transposes([Q[0:64, base + 128 * j:base + 128 * j + 128] for j in range(kn)],
                                     [ktm[:, k0 + j, 64 * h:64 * h + 64] for j in range(kn)],
                                     [at if k0 else None])
                    at = V(lambda e: e.tensor_copy(KT[b][0:64, 128 * k0:128 * (k0 + kn)],
                                                   Q[0:64, base:base + 128 * kn]), tok, free_h[b], eq)
                    got.append(at)
                if h < 2:
                    for k0 in range(0, nk, 4):
                        kn = min(4, nk - k0)
                        tok = transposes([Q[0:96, 128 * j:128 * j + 128] for j in range(kn)],
                                         [ktm[:, k0 + j, 448:544] for j in range(kn)], [at, eq])
                        at = V(lambda e: e.tensor_copy(KT[b][64:96, 128 * k0:128 * (k0 + kn)],
                                                       Q[64:96, 0:128 * kn]), tok)
                        got.append(at)
                free_pair(qn, [at, eq])
                kq[h] = got

            def logits(u):
                h, t = divmod(u, nt)
                b, n = h % 2, u % 3
                Q, qn, w0 = pair()
                P.wait(w0, kq[h])
                for j in range(2):
                    c0, cn = j * nh, min(nh, nk * 128 - j * nh)
                    tok = P(lambda e: e.matmul(Q[:, 512 * j:512 * j + cn], QT[b][:, 128 * t:128 * t + 128],
                                               KT[b][:, c0:c0 + cn], start=True, stop=True))
                free_h[b] = [tok]
                lg = Q.rearrange("p (a n) -> p a n", a=2)[:, :, 0:nh]
                mx, nm, rs, ri = (sm[:, 32 + 4 * n + j:33 + 4 * n + j] for j in range(4))
                a = V(lambda e: e.tensor_reduce(mx, lg, AX.XY, ALU.max), tok, free_s[n])
                a = G(lambda e: e.tensor_scalar(nm, mx, -SM1, None, ALU.mult), a)
                te = A(lambda e: e.activation(PP[n][:, :].rearrange("p (a n) -> p a n", a=2), lg, ACT.Exp,
                                              bias=nm, scale=SM1, accum_out=rs), a, free_p[n])
                return Q, qn, te, rs, ri

            def turned(u, job):
                Q, qn, te, rs, ri = job
                n, m = u % 3, u % 2
                tn = V(lambda e: e.reciprocal(ri, rs), te)
                tok = transposes([Q[:, 128 * j:128 * j + 128] for j in range(nk)],
                                 [PP[n][:, 128 * j:128 * j + 128] for j in range(nk)], [te])
                free_p[n] = tok
                c = min(512, 128 * nk)
                ev = [A(lambda e: e.activation(PT[m][:, 0:c], Q[:, 0:c], ACT.Copy), tok, free_t[m])]
                if nk > 4:
                    ev.append(V(lambda e: e.tensor_copy(PT[m][:, 512:128 * nk], Q[:, 512:128 * nk]), tok, free_t[m]))
                return Q, qn, ev, ri, tn

            def valued(u, job):
                Q, qn, ev, ri, tn = job
                h, t = divmod(u, nt)
                m = u % 2
                P.wait(ev)
                for j in range(nk):
                    tok = P(lambda e: e.matmul(Q[:, 896:960], PT[m][:, 128 * j:128 * j + 128],
                                               Vb[:, j, 64 * h:64 * h + 64], start=(j == 0), stop=(j == nk - 1)))
                free_t[m] = tok
                o = V(lambda e: e.tensor_scalar(Z8[:, t, 64 * h:64 * h + 64], Q[:, 896:960], ri, None, ALU.mult),
                      tok, tn)
                free_s[u % 3] = o
                free_pair(qn, [o] + ev)

            load_head(0, None)
            jobs, turn_ = {}, {}
            n_u = NH * nt
            for u in range(n_u + 2):
                if u < n_u:
                    jobs[u] = logits(u)
                if u >= 2:
                    valued(u - 2, turn_.pop(u - 2))
                if 1 <= u <= n_u:
                    turn_[u - 1] = turned(u - 1, jobs.pop(u - 1))
                if u % nt == (1 if nt > 1 else 0) and u // nt + 1 < NH:
                    load_head(u // nt + 1, None)
                yield
            task[0].small = was

        def mix1(i, s, x, nt, Z8, qtm, ktm, Vb, zT, last_ctx):
            T = 128 * nt
            t_off = 0 if s else 2
            rope = not s
            sub = scope()
            ready = prep(x, nt, lambda k: SA1S[i][:, 0, k, s:s + 1], lambda k: MODS[i][:, k, s:s + 1], sub, modtok[i])
            z = Z8[:, 0:416 * nt].rearrange("p (t n) -> p t n", t=nt)
            zt = []

            def ev_z(b, B, tok):
                t = A(lambda e: e.activation(z[:, b, 0:416], B[:, 0:416], ACT.Copy), tok)
                zt.append(t)
                return [t]

            yield from gemm("zt", "TM", (AH, AL), T, 8, 416, ev_z, ready)
            fence()
            sub.close()
            sub = scope()
            J = sb([128, 256], stack=sub)
            for t in range(nt):
                sumsq(z[:, t, 0:256], J[:, :], task[0].st[:, t:t + 1], A.last())
                tk = sumsq(z[:, t, 256:384], J[:, 0:128], task[0].st[:, 4 + t:5 + t], A.last())
            rr = task[0].st[:, 8:16]
            if nt < 4:
                V(lambda e: e.memset(rr, 1.0))
            a = rstd(rr[:, 0:nt], task[0].st[:, 0:nt], nt, 1.0 / 256, 1e-6, tk, V.last())
            b = rstd(rr[:, 4:4 + nt], task[0].st[:, 4:4 + nt], nt, 1.0 / 128, 1e-6, tk, V.last())
            for t in range(nt):
                a1 = V(lambda e: e.tensor_scalar(z[:, t, 0:256], z[:, t, 0:256], rr[:, t:t + 1], None, ALU.mult), a, b)
                a2 = V(lambda e: e.tensor_scalar(z[:, t, 256:384], z[:, t, 256:384], rr[:, 4 + t:5 + t], None,
                                                 ALU.mult), b)
            gq, gkv = c1("g_q", i), c1("g_kv", i)
            zr = []
            for j in range(3):
                if last_ctx and j < 2:
                    continue
                B, bn, w0 = bank()
                tok = transposes([B[:, 128 * t:128 * t + 128] for t in range(nt)],
                                 [z[:, t, 128 * j:128 * j + 128] for t in range(nt)], [a1, a2, w0])
                sc = gq[:, j:j + 1] if j < 2 else gkv[:, 0:1]
                zr.append(A(lambda e: e.activation(zT[:, j, 0:T], B[:, 0:T], ACT.Copy, scale=sc), tok))
                free_bank(bn, zr[-1])
            kr = z[:, 0:nt, 384:416]
            if rope:
                kv = kr.rearrange("p t (h a c) -> p t h a c", h=2, a=2)
                tmp = [sb([128, nt, 2, 8], stack=sub) for _ in range(4)]
                co = con("r1c").rearrange("p (t h c) -> p t h c", t=4, h=2)
                si = con("r1s").rearrange("p (t h c) -> p t h c", t=4, h=2)
                krt = rotate((kv[:, :, :, 0, :], kv[:, :, :, 1, :]), kv[:, :, :, 0, :], kv[:, :, :, 1, :], co, si,
                             [x_[:, :, :, :] for x_ in tmp], [zt])
            else:
                krt = zt
            if not last_ctx:
                Cv = sb([128, 2, T], stack=sub)
                S2 = sb([128, 2, T], stack=sub)
                gg = S2
                m1 = sb([128, 256], stack=sub)
                m2 = sb([128, 256], stack=sub)
                rt = [sb([128, 8, 2, 8], stack=sub) for _ in range(4)]
                sub2 = scope()
                U = sb([128, 2, T + 30], stack=sub2)
                H2 = sb([128, 2, T + 2], stack=sub2)
                for c in range(2):
                    G(lambda e: e.memset(U[:, c, 0:15], 0.0))
                    tz = G(lambda e: e.memset(U[:, c, T + 15:T + 30], 0.0))
                hold = {}

                def ev_cf(b, B, tok):
                    if b < 2:
                        hold[b] = A(lambda e: e.activation(U[:, b, 15:15 + T], B[:, 0:T], ACT.Copy), tok)
                        return [hold[b]]
                    c = b - 2
                    t = A(lambda e: e.activation(gg[:, c, :], B[:, 0:T], ACT.Tanh, scale=0.5), tok)
                    t1 = V(lambda e: e.tensor_scalar(gg[:, c, :], gg[:, c, :], 0.5, 0.5, ALU.mult, ALU.add), t)
                    hold[b] = V(lambda e: e.tensor_tensor(U[:, c, 15:15 + T], U[:, c, 15:15 + T], gg[:, c, :],
                                                          ALU.mult), t1, hold[c])
                    return [t]

                yield from gemm("cf", "FM", (AH, AL), T, 8, 512, ev_cf, ready)
                W = c1("conf_dw_w", i).rearrange("p (c k) -> p c k", c=2)
                db = c1("conf_dw_b", i)
                for c in range(2):
                    t = V(lambda e: e.tensor_scalar(Cv[:, c, :], U[:, c, 0:T], W[:, c, 0:1], db[:, c:c + 1],
                                                    ALU.mult, ALU.add), hold[2 + c], tz)
                    for k in range(1, 31):
                        t = V(lambda e, k=k: e.scalar_tensor_tensor(Cv[:, c, :], U[:, c, k:k + T], W[:, c, k:k + 1],
                                                                    Cv[:, c, :], ALU.mult, ALU.add), t)
                conv_done = t
                for c in range(2):
                    G(lambda e: e.memset(H2[:, c, 0:1], 0.0))
                    tz = G(lambda e: e.memset(H2[:, c, T + 1:T + 2], 0.0))
                hs = {}

                def ev_sc(b, B, tok):
                    if b < 2:
                        hs[b] = A(lambda e: e.activation(H2[:, b, 1:1 + T], B[:, 0:T], ACT.Copy), tok)
                        return [hs[b]]
                    hs[b] = V(lambda e: e.tensor_tensor(H2[:, b - 2, 1:1 + T], B[:, 0:T], H2[:, b - 2, 1:1 + T],
                                                        ALU.mult), tok, hs[b - 2])
                    W3 = c1("sc_dw_w", i).rearrange("p (c k) -> p c k", c=2)
                    c = b - 2
                    t = V(lambda e: e.tensor_scalar(S2[:, c, :], H2[:, c, 0:T], W3[:, c, 0:1], None, ALU.mult),
                          hs[b], tz)
                    for k in range(1, 3):
                        t = V(lambda e, k=k: e.scalar_tensor_tensor(S2[:, c, :], H2[:, c, k:k + T], W3[:, c, k:k + 1],
                                                                    S2[:, c, :], ALU.mult, ALU.add), t)
                    hs[b] = t
                    return [hs[b]]

                yield from gemm("sc", "FM", (AH, AL), T, 8, 512, ev_sc, ready)

                def ev_sb(b, B, tok):
                    hs[b] = V(lambda e: e.tensor_tensor(S2[:, b, :], B[:, 0:T], S2[:, b, :], ALU.mult), tok, hs[b + 2])
                    return [hs[b]]

                adone = yield from gemm("sb", "FM", (AH, AL), T, 8, 256, ev_sb, ready)
            co = con("r1c").rearrange("p (t h c) -> p t h c", t=4, h=2)
            si = con("r1s").rearrange("p (t h c) -> p t h c", t=4, h=2)
            if not last_ctx:
                us = [use("wq"), use("wq")]
                Wq = [RAW[u % NR][:, 0:768].rearrange("p (k n) -> p k n", k=2) for u in us]
                for t in range(nt):
                    Q, qn, w0 = pair()
                    P.wait(parts[us[0]], parts[us[1]], w0, zr)
                    for hf in range(2):
                        for k in range(2):
                            tok = P(lambda e: e.matmul(Q[:, 512 * hf:512 * hf + 384], zT[:, k, 128 * t:128 * t + 128],
                                                       Wq[hf][:, k, :], start=(k == 0), stop=(k == 1)))
                    ev = A(lambda e: e.activation(qtm[:, t, :].rearrange("p (a n) -> p a n", a=2),
                                                  Q[:, :].rearrange("p (a n) -> p a n", a=2)[:, :, 0:384], ACT.Copy), tok)
                    free_pair(qn, [ev])
                    if rope:
                        v = qtm[:, t, :].rearrange("p (h n) -> p h n", h=8)[:, :, 64:96]
                        v = v.rearrange("p h (b a c) -> p h b a c", b=2, a=2)
                        rotate((v[:, :, :, 0, :], v[:, :, :, 1, :]), v[:, :, :, 0, :], v[:, :, :, 1, :],
                               co[:, t, :, :].unsqueeze(1).to_broadcast([128, 8, 2, 8]),
                               si[:, t, :, :].unsqueeze(1).to_broadcast([128, 8, 2, 8]),
                               [x_[:, :, :, :] for x_ in rt], [ev, V.last(), G.last()])
                for u in us:
                    release_raw(u, tok)
            V(lambda e: e.tensor_copy(ktm[:, t_off:t_off + nt, 512:544], kr), krt)
            u = use("wkv")
            for t in range(nt):
                Q, qn, w0 = pair()
                P.wait(parts[u], w0, zr)
                for hf in range(2):
                    tok = P(lambda e: e.matmul(Q[:, 512 * hf:512 * hf + 512], zT[:, 2, 128 * t:128 * t + 128],
                                               RAW[u % NR][:, 512 * hf:512 * hf + 512], start=True, stop=True))
                q3 = Q[:, :].rearrange("p (h n) -> p h n", h=8)
                k3 = ktm[:, t_off + t, 0:512].rearrange("p (h n) -> p h n", h=8)
                e1 = A(lambda e: e.activation(k3, q3[:, :, 0:64], ACT.Copy), tok)
                e2 = V(lambda e: e.tensor_copy(Vb[:, t_off + t, :].rearrange("p (h n) -> p h n", h=8),
                                               q3[:, :, 64:128]), tok, e1)
                free_pair(qn, [e1, e2])
            release_raw(u, tok)
            if last_ctx:
                fence()
                sub.close()
                return
            g_br = c1("g_branch", i)
            lg_, lb_ = c1("conf_ln_g", i), c1("conf_ln_b", i)
            G_ln = LN[i]
            fence()
            sub2.close()
            mf = sb([128, 4, T], stack=sub)
            for t in range(nt):
                B, bn, w0 = bank()
                tok = transposes([B[:, 128 * c:128 * c + 128] for c in range(2)] +
                                 [B[:, 256 + 128 * c:384 + 128 * c] for c in range(2)],
                                 [Cv[:, c, 128 * t:128 * t + 128] for c in range(2)] +
                                 [S2[:, c, 128 * t:128 * t + 128] for c in range(2)], [w0, V.last()])
                s_ = task[0].st[:, 16:32]
                a = V(lambda e: e.bn_stats(s_[:, 0:6], B[:, 0:256]), tok)
                a = V(lambda e: e.bn_aggr(s_[:, 6:8], s_[:, 0:6]), a)
                b = rstd(s_[:, 8:9], s_[:, 7:8], 1, 1.0, 1e-6, a)
                a = V(lambda e: e.tensor_scalar(m1[:, :], B[:, 0:256], s_[:, 6:7], s_[:, 8:9], ALU.subtract, ALU.mult),
                      b, P.last())
                a = V(lambda e: e.tensor_tensor(m1[:, :], m1[:, :], G_ln[:, 0, :], ALU.mult), a)
                a = V(lambda e: e.tensor_tensor(m1[:, :], m1[:, :], G_ln[:, 1, :], ALU.add), a)
                c = A(lambda e: e.activation(m2[:, :], m1[:, :], ACT.Tanh, scale=0.5), a)
                a = V(lambda e: e.tensor_scalar(m2[:, :], m2[:, :], 0.5, 0.5, ALU.mult, ALU.add), c)
                a = V(lambda e: e.tensor_tensor(m1[:, :], m1[:, :], m2[:, :], ALU.mult), a)
                c = sumsq(m1[:, :], J[:, :], s_[:, 9:10], a)
                c = sumsq(B[:, 256:512], J[:, :], s_[:, 10:11], c)
                d = rstd(s_[:, 11:13], s_[:, 9:11], 2, 1.0 / 256, 1e-6, c)
                a = V(lambda e: e.tensor_scalar(m1[:, :], m1[:, :], s_[:, 11:12], None, ALU.mult), d)
                b = V(lambda e: e.tensor_scalar(m2[:, :], B[:, 256:512], s_[:, 12:13], None, ALU.mult), d)
                free_bank(bn, b)
                B2, bn2, w0 = bank()
                tok = transposes([B2[:, 128 * c:128 * c + 128] for c in range(4)],
                                 [m1[:, 0:128], m1[:, 128:256], m2[:, 0:128], m2[:, 128:256]], [a, b, w0])
                a = V(lambda e: e.tensor_tensor(mf[:, :, 128 * t:128 * t + 128],
                                                B2[:, :].rearrange("p (c n) -> p c n", c=4),
                                                g_br[:, 4:8].unsqueeze(2).to_broadcast([128, 4, 128]), ALU.mult), tok)
                free_bank(bn2, a)
            for c in range(4):
                store_split(mf[:, c, :], c, (AH[:, 4 + c, 0:T], AL[:, 4 + c, 0:T]), None, a, adone)
            fence()
            sub.close()
            sub = scope()
            at = Z8[:, 0:512 * nt].rearrange("p (t n) -> p t n", t=nt)
            yield from attention1(qtm, ktm, Vb, 2 if s else 6, nt, at, sub)
            fence()
            sub.close()
            sub = scope()
            J = sb([128, 512], stack=sub)
            mf = [sb([128, T], stack=sub) for _ in range(2)]
            for t in range(nt):
                tk = sumsq(at[:, t, :], J[:, :], task[0].st[:, t:t + 1], A.last())
            tr = rstd(task[0].st[:, 8:8 + nt], task[0].st[:, 0:nt], nt, 1.0 / 512, 1e-6, tk)
            for t in range(nt):
                a = V(lambda e: e.tensor_scalar(at[:, t, :], at[:, t, :], task[0].st[:, 8 + t:9 + t], None, ALU.mult), tr)
            ready = {k: [V.last(), G.last()] for k in range(4, 8)}
            for c in range(4):
                B, bn, w0 = bank()
                tok = transposes([B[:, 128 * t:128 * t + 128] for t in range(nt)],
                                 [at[:, t, 128 * c:128 * c + 128] for t in range(nt)], [a, w0])
                b = A(lambda e: e.activation(mf[c % 2][:, :], B[:, 0:T], ACT.Copy, scale=g_br[:, c:c + 1]), tok,
                      ready.get(c - 2))
                free_bank(bn, b)
                ready[c] = store_split(mf[c % 2][:, :], c, (AH[:, c, 0:T], AL[:, c, 0:T]), None, b)
            fence()
            sub.close()
            return ready

        def project(key, nt, y, ready, act=None):
            yt = []
            for hf in range(2):
                def ev(b, B, tok):
                    if b % 2:
                        t = A(lambda e: e.activation(y[:, b, 512 * hf:512 * hf + 512], B[:, :], ACT.Copy), tok)
                    else:
                        t = V(lambda e: e.tensor_copy(y[:, b, 512 * hf:512 * hf + 512], B[:, :]), tok)
                    yt.append(t)
                    return [t]
                yield from gemm(key, "TM", act or (AH, AL), 128 * nt, 8, 512, ev, ready)
            return yt

        def mlp(i, s, x, nt):
            T = 128 * nt
            stk = scope()
            row, trow = row_of(GPS[i][:, 1, :, s], stk)
            BH, BL = sb([128, 8, T], f32r, stk), sb([128, 8, T], f32r, stk)
            Y = sb([128, nt, 1024], stack=stk)
            ready = prep(x, nt, lambda k: SA1S[i][:, 1, k, s:s + 1], lambda k: MODS[i][:, 24 + k, s:s + 1], stk, None)
            r = [sb([128, T], stack=stk) for _ in range(3)]
            rfree = [None] * 3
            bfree, cnt = None, 0
            for g in range(4):
                done = {}
                for hf in range(2):
                    def ev(b, B, tok, hf=hf):
                        kk = 4 * hf + b
                        q = r[kk % 3]
                        a = A(lambda e: e.activation(q[:, :], B[:, 0:T], ACT.Relu), tok, rfree[kk % 3])
                        c = V(lambda e: e.tensor_tensor(q[:, :], q[:, :], q[:, :], ALU.mult), a)
                        done[kk] = store_split(q[:, :], kk, (BH[:, kk, :], BL[:, kk, :]), None, c, bfree)
                        rfree[kk % 3] = done[kk]
                        return [a]
                    yield from gemm("w1", "FM", (AH, AL), T, 8, 512, ev, ready)
                for hf in range(2):
                    def ev(b, B, tok, hf=hf, g=g):
                        y = Y[:, b, 512 * hf:512 * hf + 512]
                        if g == 0:
                            ytok[(b, hf)] = V(lambda e: e.tensor_copy(y, B[:, :]), tok)
                        else:
                            ytok[(b, hf)] = V(lambda e: e.tensor_tensor(y, B[:, :], y, ALU.add), tok, ytok[(b, hf)])
                        return [ytok[(b, hf)]]
                    if g == 0 and hf == 0:
                        ytok = {}
                    bfree = yield from gemm("w2", "TM", (BH, BL), T, 8, 512, ev, done)
            residual(x, Y, nt, row, trow, stk, list(ytok.values()))
            stk.close()

        LN = [sb([128, 2, 256], stack=first) for _ in range(L)]

        def ln_rows():
            for i in range(L):
                B, bn, w0 = bank()
                P.wait(w0)
                for j, name in enumerate(("conf_ln_g", "conf_ln_b")):
                    for c in range(2):
                        col = c1(name, i)[:, c:c + 1].to_broadcast([128, 128])
                        tok = P(lambda e: e.matmul(B[:, 256 * j + 128 * c:256 * j + 128 * c + 128], col, ident,
                                                   start=True, stop=True))
                t = A(lambda e: e.activation(LN[i][:, :, :].rearrange("p a b -> p (a b)"), B[:, :], ACT.Copy), tok)
                free_bank(bn, t)

        def block1():
            run(modulation(0, 8))
            ln_rows()
            for i in range(L):
                stk = scope()
                ktm = sb([128, 6, 544], stack=stk)
                Vb = sb([128, 6, 512], stack=stk)
                own = scope()
                Z8 = sb([128, 1024], stack=own)
                qtm = sb([128, 2, 768], stack=own)
                zT = sb([128, 3, 256], stack=own)
                if i == 0:
                    ready = yield from mix1(i, 1, XC, 2, Z8, qtm, ktm, Vb, zT, False)
                    sub = scope()
                    y = sb([128, 2, 1024], stack=sub)
                    row, trow = row_of(GPS[i][:, 0, :, 1], sub)
                    yt = yield from project("wo", 2, y, ready)
                    residual(XC, y, 2, row, trow, sub, yt)
                    sub.close()
                else:
                    yield from mix1(i, 1, XC, 2, Z8, qtm, ktm, Vb, zT, True)
                own.close()
                own = scope()
                Z8 = sb([128, 2048], stack=own)
                qtm = sb([128, 4, 768], stack=own)
                zT = sb([128, 3, 512], stack=own)
                ready = yield from mix1(i, 0, X, 4, Z8, qtm, ktm, Vb, zT, False)
                own.close()
                stk.close()
                stk = scope()
                y = sb([128, 4, 1024], stack=stk)
                row, trow = row_of(GPS[i][:, 0, :, 0], stk)
                yt = yield from project("wo", 4, y, ready)
                residual(X, y, 4, row, trow, stk, yt)
                stk.close()
                if stop == f"mix{i}":
                    return
                if i == 0:
                    yield from mlp(i, 1, XC, 2)
                    both(mlp(i, 0, X, 4), modulation(1, 2), 0.2)
                else:
                    yield from mlp(i, 0, X, 4)
                if stop == f"mlp{i}":
                    return

        def silu_psum(dst, B, tok, *waits):
            a = A(lambda e: e.activation(dst, B, ACT.Tanh, scale=0.5), tok, *waits)
            b = G(lambda e: e.tensor_scalar(dst, dst, 0.5, 0.5, ALU.mult, ALU.add), a)
            return V(lambda e: e.tensor_tensor(dst, B, dst, ALU.mult), b)

        def gates(i, n, hf, GT, gt, ready, gfree_):
            bt = c2("gate_b_2", i)

            def ev_g(b, B, tok):
                a = V(lambda e: e.tensor_scalar(GT[:, b, :], B, bt[:, 8 * n + 4 * hf + b:8 * n + 4 * hf + b + 1],
                                                0.5, ALU.add, ALU.mult), tok, gfree_.get(b))
                c = A(lambda e: e.activation(GT[:, b, :], GT[:, b, :], ACT.Tanh), a)
                gt[b] = G(lambda e: e.tensor_scalar(GT[:, b, :], GT[:, b, :], 0.5, 0.5, ALU.mult, ALU.add), c)
                return [a]

            yield from gemm("gate", "FM", (AH, AL), 512, 8, 512, ev_g, ready)

        def branch(first, hf, GT, gt, M, Y, yready, mt):
            gf = {}

            def ev_b(b, B, tok):
                m = M[:, 4 * hf + b, :]
                if first:
                    gf[b] = mt[4 * hf + b] = V(lambda e: e.tensor_tensor(m, B, GT[:, b, :], ALU.mult), tok, gt[b])
                    return [gf[b]]
                a = V(lambda e: e.tensor_tensor(GT[:, b, :], B, GT[:, b, :], ALU.mult), tok, gt[b])
                gf[b] = mt[4 * hf + b] = V(lambda e: e.tensor_tensor(m, m, GT[:, b, :], ALU.add), a, mt[4 * hf + b])
                return [a]

            yield from gemm("br", "FM", Y, 512, 4, 512, ev_b, yready)
            return gf

        def delta_in(i, F, ready):
            sub = scope()
            U = sb([128, 4, 515], stack=sub)
            tz = None
            for c in range(4):
                tz = G(lambda e: e.memset(U[:, c, 0:3], 0.0))
            cw = c2("conv_w_2", i).rearrange("p (c k) -> p c k", c=12)
            ufree = [None] * 4
            tmp, tfree = [sb([128, 512], stack=sub) for _ in range(2)], [None, None]
            for n, key in enumerate(("qa", "ka", "va")):
                def ev(b, B, tok, n=n):
                    f = F[n][:, b, :]
                    a = A(lambda e: e.activation(U[:, b, 3:515], B[:, :], ACT.Copy), tok, ufree[b])
                    w = cw[:, 4 * n + b, :]
                    t = V(lambda e: e.tensor_scalar(f, U[:, b, 0:512], w[:, 0:1], None, ALU.mult), a, tz)
                    for k in range(1, 4):
                        t = V(lambda e, k=k: e.scalar_tensor_tensor(f, U[:, b, k:k + 512], w[:, k:k + 1], f,
                                                                    ALU.mult, ALU.add), t)
                    ufree[b] = t
                    q = tmp[b % 2][:, :]
                    c = A(lambda e: e.activation(q, f, ACT.Tanh, scale=0.5), t, tfree[b % 2])
                    t = G(lambda e: e.tensor_scalar(q, q, 0.5, 0.5, ALU.mult, ALU.add), c)
                    tfree[b % 2] = V(lambda e: e.tensor_tensor(f, f, q, ALU.mult), t)
                    return [a]
                yield from gemm(key, "FM", (AH, AL), 512, 8, 512, ev, ready)

            sub.close()

        def delta(i, F, SM, SZ, za):
            stk = scope()
            fence()
            be = sb([128, 4, 4], stack=stk)
            gg = sb([128, 4, 4], stack=stk)
            gt = sb([128, 4, 4], stack=stk)
            gc = sb([128, 4, 4], stack=stk)
            ea = sb([128, 4], stack=stk)
            a = A(lambda e: e.activation(be[:, :, :], SM[:, :, 0:4], ACT.Tanh, scale=0.5))
            tbe = V(lambda e: e.tensor_scalar(be[:, :, :], be[:, :, :], 0.5, 0.5, ALU.mult, ALU.add), a)
            t = V(lambda e: e.tensor_tensor(gg[:, :, :], SM[:, :, 4:8],
                                            r2("dt_bias_2", i).unsqueeze(1).to_broadcast([128, 4, 4]), ALU.add))
            t = V(lambda e: e.tensor_scalar(gt[:, :, :], gg[:, :, :], -1.0, None, ALU.mult), t)
            t = V(lambda e: e.tensor_tensor(gt[:, :, :], gt[:, :, :], gg[:, :, :], ALU.min), t)
            c = A(lambda e: e.activation(ea[:, :], r2("a_log_2", i), ACT.Exp))
            c = A(lambda e: e.activation(gt[:, :, :], gt[:, :, :], ACT.Exp), t)
            c = A(lambda e: e.activation(gt[:, :, :], gt[:, :, :], ACT.Ln, bias=1.0), c)
            t = V(lambda e: e.scalar_tensor_tensor(gg[:, :, :], gg[:, :, :], 0.0, gt[:, :, :], ALU.max, ALU.add), c)
            t = V(lambda e: e.tensor_tensor(gg[:, :, :], gg[:, :, :],
                                            ea[:, :].unsqueeze(1).to_broadcast([128, 4, 4]), ALU.mult), t)
            tg = V(lambda e: e.tensor_scalar(gg[:, :, :], gg[:, :, :], -1.0, None, ALU.mult), t)
            B, bn, w0 = bank()
            tok = P(lambda e: e.matmul(B[:, 0:16], con("ut"), gg[:, :, :].rearrange("p a b -> p (a b)"),
                                       start=True, stop=True), tg, w0)
            tgc = V(lambda e: e.tensor_copy(gc[:, :, :].rearrange("p a b -> p (a b)"), B[:, 0:16]), tok)
            free_bank(bn, tgc)
            St = sb([128, 512], stack=stk)
            V(lambda e: e.memset(St[:, :], 0.0))

            def h4(ap):
                return ap.rearrange("p (h n) -> p h n", h=4)

            def bc(col):
                return col.unsqueeze(2).to_broadcast([128, 4, 128])

            def mm4(o, lhs, rhs, start=True, stop=True):
                for h in range(4):
                    tok = P(lambda e, h=h: e.matmul(o[:, 128 * h:128 * h + 128], lhs[:, 128 * h:128 * h + 128],
                                                    rhs[:, 128 * h:128 * h + 128], start=start, stop=stop))
                return tok

            buf = {n: sb([128, 512], stack=stk) for n in
                   ("kn", "kT", "qT", "GR", "Lm", "LT", "AT", "T", "TT", "X")}
            YT = SZ
            D = {n: b_[:, :] for n, b_ in buf.items()}
            lev = con("lev").rearrange("p (s n) -> p s n", s=7)
            Ft = [F[n][:, :, :] for n in range(3)]
            for n in range(4):
                cs = slice(128 * n, 128 * n + 128)
                prev = list(task[0].lasts.values())
                s_ = task[0].st[:, 16:64]
                B, b1, w0 = bank()
                tk = transposes([B[:, 128 * h:128 * h + 128] for h in range(4)],
                                [Ft[1][:, h, cs] for h in range(4)], [w0, prev])
                yield
                sq = D["X"]
                a = A(lambda e: e.activation(sq, B, ACT.Square), tk, prev)
                a = V(lambda e: e.tensor_reduce(s_[:, 0:4], h4(sq), AX.X, ALU.add), a)
                r = rstd(s_[:, 4:8], s_[:, 0:4], 4, 1.0, 1e-6, a)
                tkn = V(lambda e: e.tensor_tensor(h4(D["kn"]), h4(B), bc(s_[:, 4:8]), ALU.mult), r)
                free_bank(b1, tkn)
                B, b1, w0 = bank()
                tk = transposes([B[:, 128 * h:128 * h + 128] for h in range(4)],
                                [Ft[0][:, h, cs] for h in range(4)], [w0])
                yield
                a = A(lambda e: e.activation(sq, B, ACT.Square), tk, a)
                a = V(lambda e: e.tensor_reduce(s_[:, 8:12], h4(sq), AX.X, ALU.add), a)
                r = rstd(s_[:, 12:16], s_[:, 8:12], 4, 1.0, 1e-6, a)
                r = V(lambda e: e.tensor_scalar(s_[:, 12:16], s_[:, 12:16], SM2, None, ALU.mult), r)
                qn = D["T"]
                tqn = V(lambda e: e.tensor_tensor(h4(qn), h4(B), bc(s_[:, 12:16]), ALU.mult), r)
                free_bank(b1, tqn)
                B, b1, w0 = bank()
                P.wait(w0)
                for h in range(4):
                    tk = P(lambda e, h=h: e.matmul(B[:, 128 * h:128 * h + 128],
                                                   gg[:, n, h:h + 1].to_broadcast([128, 128]), con("ut"),
                                                   start=True, stop=True))
                tgr = A(lambda e: e.activation(D["GR"], B, ACT.Copy), tk)
                free_bank(b1, tgr)
                gl = h4(D["GR"])[:, :, 127]
                a = A(lambda e: e.activation(s_[:, 16:20], gc[:, n, :], ACT.Exp), tgc)
                a = V(lambda e: e.tensor_tensor(s_[:, 16:20], s_[:, 16:20], be[:, n, :], ALU.mult), a)
                tbg = a
                a = V(lambda e: e.tensor_tensor(s_[:, 20:24], gl, gc[:, n, :], ALU.subtract), tgr, tgc)
                a = A(lambda e: e.activation(s_[:, 20:24], s_[:, 20:24], ACT.Exp), a)
                tdg = a
                tgl = A(lambda e: e.activation(s_[:, 24:28], gl, ACT.Exp), tgr)
                B, b1, w0 = bank()
                tk = transposes([B[:, 128 * h:128 * h + 128] for h in range(4)],
                                [D["kn"][:, 128 * h:128 * h + 128] for h in range(4)], [w0, tkn])
                yield
                tkT = A(lambda e: e.activation(D["kT"], B, ACT.Copy), tk)
                free_bank(b1, tkT)
                B, b1, w0 = bank()
                tk = transposes([B[:, 128 * h:128 * h + 128] for h in range(4)],
                                [qn[:, 128 * h:128 * h + 128] for h in range(4)], [w0, tqn])
                yield
                tqT = A(lambda e: e.activation(D["qT"], B, ACT.Copy), tk)
                free_bank(b1, tqT)
                mlb = con("ml").unsqueeze(1).to_broadcast([128, 4, 128])
                mub = con("mu").unsqueeze(1).to_broadcast([128, 4, 128])
                E1 = D["X"]
                a = V(lambda e: e.tensor_tensor(h4(E1), mlb, h4(D["GR"]), ALU.subtract), tgr, tqn)
                a = V(lambda e: e.tensor_tensor(h4(E1), h4(E1), bc(gc[:, n, :]), ALU.add), a)
                a = A(lambda e: e.activation(E1, E1, ACT.Exp), a)
                a = V(lambda e: e.tensor_tensor(h4(E1), h4(E1), bc(be[:, n, :]), ALU.mult), a)
                B, b1, w0 = bank()
                P.wait(w0, tkT)
                tk = mm4(B, D["kT"], D["kT"])
                yield
                tL = V(lambda e: e.tensor_tensor(D["Lm"], B, E1, ALU.mult), tk, a)
                free_bank(b1, tL)
                B, b1, w0 = bank()
                tk = transposes([B[:, 128 * h:128 * h + 128] for h in range(4)],
                                [D["Lm"][:, 128 * h:128 * h + 128] for h in range(4)], [w0, tL])
                yield
                tLT = A(lambda e: e.activation(D["LT"], B, ACT.Copy), tk)
                free_bank(b1, tLT)
                a = V(lambda e: e.tensor_tensor(h4(E1), mub, h4(D["GR"]), ALU.add), tL)
                a = V(lambda e: e.tensor_tensor(h4(E1), h4(E1), bc(gc[:, n, :]), ALU.subtract), a)
                a = A(lambda e: e.activation(E1, E1, ACT.Exp), a)
                B, b1, w0 = bank()
                P.wait(w0, tqT)
                tk = mm4(B, D["kT"], D["qT"])
                yield
                tAT = V(lambda e: e.tensor_tensor(D["AT"], B, E1, ALU.mult), tk, a)
                free_bank(b1, tAT)
                a = A(lambda e: e.activation(E1, D["GR"], ACT.Exp), tAT)
                tqg = V(lambda e: e.tensor_tensor(D["qT"], D["qT"], E1, ALU.mult), a, tqT)
                l0 = lev[:, 0, :].unsqueeze(1).to_broadcast([128, 4, 128])
                idb = ident.unsqueeze(1).to_broadcast([128, 4, 128])
                t = V(lambda e: e.tensor_tensor(h4(D["X"]), h4(D["Lm"]), l0, ALU.mult), tqg, tL)
                tT = V(lambda e: e.tensor_tensor(h4(D["T"]), idb, h4(D["X"]), ALU.subtract), t, tqT)
                B, b1, w0 = bank()
                tk = transposes([B[:, 128 * h:128 * h + 128] for h in range(4)],
                                [D["T"][:, 128 * h:128 * h + 128] for h in range(4)], [w0, tT])
                yield
                tTT = A(lambda e: e.activation(D["TT"], B, ACT.Copy), tk)
                free_bank(b1, tTT)
                for s in range(1, 7):
                    ls = lev[:, s, :].unsqueeze(1).to_broadcast([128, 4, 128])
                    B, b1, w0 = bank()
                    P.wait(w0, tLT, tT)
                    tk = mm4(B, D["LT"], D["T"])
                    yield
                    tX = V(lambda e: e.tensor_tensor(h4(D["X"]), h4(B), ls, ALU.mult), tk, P.last())
                    free_bank(b1, tX)
                    B, b1, w0 = bank()
                    P.wait(w0, tX, tTT)
                    tk = mm4(B, D["X"], D["TT"])
                    yield
                    if s < 6:
                        B2, b2, w0 = bank()
                        P.wait(w0)
                        tk2 = mm4(B2, D["TT"], D["X"])
                    else:
                        tk2 = tk
                    tTT = V(lambda e: e.tensor_tensor(D["TT"], D["TT"], B, ALU.subtract), tk, tk2)
                    free_bank(b1, tTT)
                    if s < 6:
                        tT = V(lambda e: e.tensor_tensor(D["T"], D["T"], B2, ALU.subtract), tk2)
                        free_bank(b2, tT)
                B, b1, w0 = bank()
                tk = transposes([B[:, 128 * h:128 * h + 128] for h in range(4)],
                                [Ft[2][:, h, cs] for h in range(4)], [w0])
                yield
                tvb = V(lambda e: e.tensor_tensor(h4(D["GR"]), h4(B), bc(be[:, n, :]), ALU.mult), tk, tbe, tqg)
                free_bank(b1, tvb)
                tke = V(lambda e: e.tensor_tensor(h4(D["Lm"]), h4(D["kn"]), bc(s_[:, 16:20]), ALU.mult), tbg, tkn, tTT)
                tkd = V(lambda e: e.tensor_tensor(h4(D["LT"]), h4(D["kn"]), bc(s_[:, 20:24]), ALU.mult), tdg, tkn, tTT)
                B, b1, w0 = bank()
                P.wait(w0, tTT, tvb, tke)
                tk = mm4(B, D["TT"], D["GR"])
                yield
                tu = A(lambda e: e.activation(D["T"], B, ACT.Copy), tk)
                free_bank(b1, tu)
                B, b1, w0 = bank()
                P.wait(w0)
                tk = mm4(B, D["Lm"], D["TT"])
                yield
                tw = A(lambda e: e.activation(D["X"], B, ACT.Copy), tk)
                free_bank(b1, tw)
                B, b1, w0 = bank()
                P.wait(w0, tw, V.last())
                tk = mm4(B, D["X"], St[:, :])
                yield
                tv = V(lambda e: e.tensor_tensor(D["T"], D["T"], B, ALU.subtract), tk, tu)
                free_bank(b1, tv)
                B, b1, w0 = bank()
                P.wait(w0, tqg, tv, tAT)
                for h in range(4):
                    hs_ = slice(128 * h, 128 * h + 128)
                    P(lambda e: e.matmul(B[:, hs_], D["qT"][:, hs_], St[:, hs_], start=True, stop=False))
                    to = P(lambda e: e.matmul(B[:, hs_], D["AT"][:, hs_], D["T"][:, hs_], start=False, stop=True))
                B2, b2, w0 = bank()
                P.wait(w0, tkd)
                tk = mm4(B2, D["LT"], D["T"])
                yield
                a = V(lambda e: e.tensor_tensor(h4(St[:, :]), h4(St[:, :]), bc(s_[:, 24:28]), ALU.mult), to, tgl)
                tS = V(lambda e: e.tensor_tensor(St[:, :], St[:, :], B2, ALU.add), a, tk)
                free_bank(b2, tS)
                a = A(lambda e: e.activation(D["X"], B, ACT.Square), to)
                a = V(lambda e: e.tensor_reduce(s_[:, 28:32], h4(D["X"]), AX.X, ALU.add), a)
                r = rstd(s_[:, 32:36], s_[:, 28:32], 4, 1.0 / 128, 1e-6, a)
                a = V(lambda e: e.tensor_tensor(h4(D["X"]), h4(B), bc(s_[:, 32:36]), ALU.mult), r)
                free_bank(b1, a)
                B, b1, w0 = bank()
                tk = transposes([B[:, 128 * h:128 * h + 128] for h in range(4)],
                                [D["X"][:, 128 * h:128 * h + 128] for h in range(4)], [w0, a])
                yield
                assert len(za) == 4
                a = V(lambda e: e.scalar_tensor_tensor(YT[:, :, cs], h4(B), c2("dn_onorm_2", i)[:, 0:1],
                                                       SZ[:, :, cs], ALU.mult, ALU.mult), tk, za)
                free_bank(b1, a)
            za.append(a)
            stk.close()

        def to_branch(YT, yt, stk_y):
            YH, YL = sb([128, 4, 512], f32r, stk_y), sb([128, 4, 512], f32r, stk_y)
            yr = {}
            for c in range(4):
                yr[c] = store_split(YT[:, c, :], c, (YH[:, c, :], YL[:, c, :]), None, yt)
            return YH, YL, yr

        def pooling(i, SZ, ready):
            stk = scope()
            U2 = [sb([128, 528], stack=stk) for _ in range(2)]
            YT = sb([128, 4, 512], stack=stk)
            W1, W2 = sb([128, 528], stack=stk), sb([128, 528], stack=stk)
            for u_ in U2:
                tz = G(lambda e: e.memset(u_[:, 0:16], 0.0))
            pooled = {}
            pcs = con("pc").rearrange("p (g n) -> p g n", g=4)

            def ev(b, B, tok):
                U = U2[b % 2]
                a = A(lambda e: e.activation(U[:, 16:528], B[:, :], ACT.Copy), tok, pooled.get(b - 2))
                src, w, t = U[:, :], 1, [a, tz]
                bufs = [W1, W2]
                for m in range(b + 1):
                    dst = bufs[m % 2]
                    t = V(lambda e, dst=dst, src=src, w=w: e.tensor_tensor(dst[:, 2 * w - 1:528], src[:, 2 * w - 1:528],
                                                                           src[:, w - 1:528 - w], ALU.add), t)
                    src, w = dst[:, :], 2 * w
                o = YT[:, b, :]
                t = V(lambda e, src=src, w=w: e.scalar_tensor_tensor(o[:, 16:512], src[:, 32:528], 1.0 / w,
                                                                     U[:, 32:528], ALU.mult, ALU.subtract), t)
                t1 = V(lambda e, src=src: e.tensor_tensor(o[:, 0:16], src[:, 16:32], pcs[:, b, :], ALU.mult), t)
                pooled[b] = V(lambda e: e.tensor_tensor(o[:, 0:16], o[:, 0:16], U[:, 16:32], ALU.subtract), t1)
                return [a]

            yield from gemm("ub", "FM", (AH, AL), 512, 8, 512, ev, ready)
            zt = {}

            def ev_z(b, B, tok):
                zt[b] = silu_psum(SZ[:, b, :], B[:, :], tok)
                return [zt[b]]

            yield from gemm("zb", "FM", (AH, AL), 512, 8, 512, ev_z, ready)
            u = use("pw")
            W = RAW[u % NR][:, 0:512].rearrange("p (g n) -> p g n", g=4)
            ps = c2("pool_scale_2", i)
            for b in range(4):
                B, bn, w0 = bank()
                tok = P(lambda e: e.matmul(B, W[:, b, :], YT[:, b, :], start=True, stop=True), parts[u], w0, pooled[b])
                t = V(lambda e: e.scalar_tensor_tensor(SZ[:, b, :], B, ps[:, b:b + 1], SZ[:, b, :],
                                                       ALU.mult, ALU.mult), tok, zt[b])
                free_bank(bn, t)
                zt[b] = t
            release_raw(u, tok)
            stk.close()
            return zt

        def sparse_in(i, SM, SZ, KT, QT, VV, IQ, IK, wi, ready, ya):
            sub = scope()
            TMs = [sb([128, 4, 512], stack=sub) for _ in range(2)]
            rt = [sb([128, 5, 64], stack=sub) for _ in range(4)]
            sq = sb([128, 512], stack=sub)
            sm = task[0].st
            rac, ras = (con(n_).rearrange("p (t n) -> p t n", t=4) for n_ in ("rac", "ras"))
            rots = {}

            def heads(key, TM, gname):
                g = r2(gname, i).unsqueeze(1).to_broadcast([128, 4, 128])
                rot = rots[key] = {}

                def ev(b, B, tok):
                    a = A(lambda e: e.activation(sq[:, :], B, ACT.Square), tok, V.last())
                    a = V(lambda e: e.tensor_reduce(sm[:, 0:4], sq[:, :].rearrange("p (h n) -> p h n", h=4), AX.X,
                                                    ALU.add), a)
                    r = rstd(sm[:, 8:12], sm[:, 0:4], 4, 1.0 / 128, 1e-6, a)
                    tm = TM[:, b, :].rearrange("p (h n) -> p h n", h=4)
                    f = V(lambda e: e.tensor_tensor(tm, B.rearrange("p (h n) -> p h n", h=4),
                                                    sm[:, 8:12].unsqueeze(2).to_broadcast([128, 4, 128]), ALU.mult), r)
                    a = V(lambda e: e.tensor_tensor(tm, tm, g, ALU.mult), f)
                    co = rac[:, b, :].unsqueeze(1).to_broadcast([128, 4, 64])
                    si = ras[:, b, :].unsqueeze(1).to_broadcast([128, 4, 64])
                    rot[b] = rotate((tm[:, :, 0:64], tm[:, :, 64:128]), tm[:, :, 0:64], tm[:, :, 64:128], co, si,
                                    [x_[:, 0:4, :] for x_ in rt], [a, V.last(), G.last()])
                    return [f]

                yield from gemm(key, "TM", (AH, AL), 512, 8, 512, ev, ready)

            def turn_heads(key, TM, dst):
                for h in range(4):
                    B, bn, w0 = bank()
                    tk = transposes([B[:, 128 * t:128 * t + 128] for t in range(4)],
                                    [TM[:, t, 128 * h:128 * h + 128] for t in range(4)],
                                    [w0, [rots[key][b] for b in range(4)]])
                    a = A(lambda e: e.activation(dst[:, h, :], B, ACT.Copy), tk)
                    free_bank(bn, a)

            yield from heads("kc", TMs[0], "k_norm_2")
            yield from heads("qc", TMs[1], "q_norm_2")
            turn_heads("kc", TMs[0], KT)

            def ev_v(b, B, tok):
                return [A(lambda e: e.activation(VV[:, b, :], B, ACT.Copy), tok)]

            yield from gemm("vc", "TM", (AH, AL), 512, 8, 512, ev_v, ready)
            turn_heads("qc", TMs[1], QT)
            ric, ris = (con(n_).rearrange("p (t n) -> p t n", t=4) for n_ in ("ric", "ris"))
            for t in range(4):
                v = SM[:, t, 8:328].rearrange("p (h n) -> p h n", h=5)
                tmp = [x_[:, :, 0:32] for x_ in rt]
                ir = rotate((v[:, :, 0:32], v[:, :, 32:64]), v[:, :, 0:32], v[:, :, 32:64],
                            ric[:, t, :].unsqueeze(1).to_broadcast([128, 5, 32]),
                            ris[:, t, :].unsqueeze(1).to_broadcast([128, 5, 32]), tmp, [V.last(), G.last()])
            V(lambda e: e.tensor_scalar(wi, SM[:, :, 328:332], 1.0 / 16, None, ALU.mult))

            def ev_z(b, B, tok):
                return [silu_psum(SZ[:, b, :], B, tok, ya)]

            yield from gemm("zc", "FM", (AH, AL), 512, 8, 512, ev_z, ready)
            for h in range(5):
                B, bn, w0 = bank()
                tk = transposes([B[0:64, 128 * t:128 * t + 128] for t in range(4)],
                                [SM[:, t, 8 + 64 * h:72 + 64 * h] for t in range(4)], [w0, ir])
                dst = IQ[:, h, :] if h < 4 else IK[:, :]
                a = A(lambda e: e.activation(dst, B[0:64, :], ACT.Copy), tk)
                free_bank(bn, a)
            sub.close()

        def sparse(i, SZ, KT, QT, VV, IQ, IK, wi, out):
            stk = scope()
            fence()
            sm = task[0].st
            scs = [sb([128, 512], stack=stk) for _ in range(1)]
            rl = [sb([128, 512], stack=stk) for _ in range(2)]
            biases = [sb([128, 512], stack=stk) for _ in range(2)]
            PP, PT = sb([128, 2, 512], stack=stk), sb([128, 2, 512], stack=stk)
            O = sb([128, 512], stack=stk)
            m8 = sm[:, 40:48]
            rlf, tbs = [None, None], {}

            def select(t):
                nk, sc, bias = 128 * (t + 1), scs[0], biases[t % 2]
                cs = slice(128 * t, 128 * t + 128)
                if t == 0:
                    tbs[t] = V(lambda e: e.tensor_copy(bias[:, 0:128], con("cb")))
                    return
                for h in range(4):
                    B, bn, w0 = bank()
                    tk = P(lambda e: e.matmul(B[:, 0:nk], IQ[:, h, cs], IK[:, 0:nk], start=True, stop=True), w0)
                    q = rl[h % 2]
                    a = A(lambda e: e.activation(q[:, 0:nk], B[:, 0:nk], ACT.Relu), tk, rlf[h % 2])
                    free_bank(bn, a)
                    w_ = wi[:, t, h:h + 1]
                    if h == 0:
                        acc = V(lambda e: e.tensor_scalar(sc[:, 0:nk], q[:, 0:nk], w_, None, ALU.mult), a)
                    else:
                        acc = V(lambda e: e.scalar_tensor_tensor(sc[:, 0:nk], q[:, 0:nk], w_, sc[:, 0:nk],
                                                                 ALU.mult, ALU.add), a, acc)
                    rlf[h % 2] = acc
                    yield
                a = V(lambda e: e.tensor_tensor(sc[:, cs], sc[:, cs], con("tri"), ALU.min), acc)
                for _ in range(16):
                    a = V(lambda e: e.max(out=m8, in_=sc[:, 0:nk]), a)
                    a = V(lambda e: e.match_replace(out=sc[:, 0:nk], in_to_replace=m8, in_values=sc[:, 0:nk],
                                                    imm_value=MARK), a)
                    yield
                tbs[t] = V(lambda e: e.tensor_scalar(bias[:, 0:nk], sc[:, 0:nk], -3.2e38, -BIG, ALU.is_gt, ALU.mult),
                           a)

            free = {"p": None, "t": None, "o": None}

            def attend(t):
                nk, bias = 128 * (t + 1), biases[t % 2]
                cs = slice(128 * t, 128 * t + 128)
                for hp in range(2):
                    bs = []
                    for j in range(2):
                        B, bn, w0 = bank()
                        h = 2 * hp + j
                        bs.append((B, bn, P(lambda e: e.matmul(B[:, 0:nk], QT[:, h, cs], KT[:, h, 0:nk],
                                                               start=True, stop=True), w0)))
                    mx, nm, rs, ri = (sm[:, 16 + 2 * j:18 + 2 * j] for j in range(4))
                    for j, (B, bn, tk) in enumerate(bs):
                        a = V(lambda e: e.tensor_tensor(PP[:, j, 0:nk], B[:, 0:nk], bias[:, 0:nk], ALU.add), tk, tbs[t],
                              free["p"])
                        free_bank(bn, a)
                    a = V(lambda e: e.tensor_reduce(mx, PP[:, :, 0:nk], AX.X, ALU.max), a)
                    a = G(lambda e: e.tensor_scalar(nm, mx, -SM2, None, ALU.mult), a)
                    for j in range(2):
                        te = A(lambda e: e.activation(PP[:, j, 0:nk], PP[:, j, 0:nk], ACT.Exp, bias=nm[:, j:j + 1],
                                                      scale=SM2, accum_out=rs[:, j:j + 1]), a)
                    yield
                    tr = V(lambda e: e.reciprocal(ri, rs), te)
                    for j in range(2):
                        B, bn, w0 = bank()
                        tk = transposes([B[:, 128 * k:128 * k + 128] for k in range(t + 1)],
                                        [PP[:, j, 128 * k:128 * k + 128] for k in range(t + 1)], [w0, te])
                        e_ = A(lambda e: e.activation(PT[:, j, 0:nk], B[:, 0:nk], ACT.Copy), tk, free["t"])
                        free_bank(bn, e_)
                    free["p"] = tk
                    yield
                    B, bn, w0 = bank()
                    P.wait(w0, e_)
                    for j in range(2):
                        h = 2 * hp + j
                        for k in range(t + 1):
                            tk = P(lambda e: e.matmul(B[:, 128 * j:128 * j + 128], PT[:, j, 128 * k:128 * k + 128],
                                                      VV[:, k, 128 * h:128 * h + 128], start=(k == 0), stop=(k == t)))
                    free["t"] = tk
                    a = V(lambda e: e.tensor_tensor(O[:, 256 * hp:256 * hp + 256].rearrange("p (h n) -> p h n", h=2),
                                                    B[:, 0:256].rearrange("p (h n) -> p h n", h=2),
                                                    ri.unsqueeze(2).to_broadcast([128, 2, 128]), ALU.mult),
                          tk, tr, free["o"])
                    free_bank(bn, a)
                    yield
                B, bn, w0 = bank()
                free["o"] = transposes([B[:, 128 * h:128 * h + 128] for h in range(4)],
                                       [O[:, 128 * h:128 * h + 128] for h in range(4)], [w0, a])
                ty = V(lambda e: e.tensor_tensor(SZ[:, :, cs], B.rearrange("p (h n) -> p h n", h=4), SZ[:, :, cs],
                                                 ALU.mult), free["o"])
                free_bank(bn, ty)
                out.append(ty)
                yield

            yield from select(0)
            for t in range(4):
                nxt = select(t + 1) if t < 3 else iter(())
                for _ in attend(t):
                    for _ in range(3):
                        next(nxt, None)
                    yield
                for _ in nxt:
                    yield
            stk.close()

        def to_branch(SZ, Y, waits):
            return {c: store_split(SZ[:, c, :], c, (Y[0][:, c, :], Y[1][:, c, :]), None, waits) for c in range(4)}

        def block2():
            first.close()
            for i in range(L):
                base = scope()
                M = sb([128, 8, 512], stack=base)
                smc = scope()
                SM = sb([128, 4, 332], stack=smc)
                SZ = sb([128, 4, 512], stack=base)
                wi = sb([128, 4, 4], stack=base)
                sub = scope()
                ready = prep(X, 4, lambda k: c2("norm_g_2", i)[:, k:k + 1], None, sub, [])

                def ev_s(b, B, tok):
                    return [A(lambda e: e.activation(SM[:, b, :], B[:, 0:332], ACT.Copy), tok)]

                yield from gemm("sm", "TM", (AH, AL), 512, 8, 332, ev_s, ready)
                sub.close()
                fsc = scope()
                F = [sb([128, 4, 512], stack=fsc) for _ in range(3)]
                yield from delta_in(i, F, ready)
                za, mt = [], {}

                def pool_part():
                    def ev_za(b, B, tok):
                        za.append(silu_psum(SZ[:, b, :], B, tok))
                        return [za[-1]]

                    yield from gemm("za", "FM", (AH, AL), 512, 8, 512, ev_za, ready)
                    sub, zsc = scope(), scope()
                    SZ1 = sb([128, 4, 512], stack=zsc)
                    pt = yield from pooling(i, SZ1, ready)
                    Y = [sb([128, 4, 512], f32r, sub) for _ in range(2)]
                    yr = to_branch(SZ1, Y, list(pt.values()))
                    zsc.close()
                    GT = sb([128, 4, 512], stack=sub)
                    gf = {}
                    for hf in range(2):
                        gt = {}
                        yield from gates(i, 1, hf, GT, gt, ready, gf)
                        gf = yield from branch(True, hf, GT, gt, M, Y, yr, mt)
                    sub.close()

                both(pool_part(), delta(i, F, SM, SZ, za), R1)
                fsc.close()
                ysc = scope()
                YA = [sb([128, 4, 512], f32r, ysc) for _ in range(2)]
                yra = to_branch(SZ, YA, za[-1:])
                asc = scope()
                KT, QT, VV = (sb([128, 4, 512], stack=asc) for _ in range(3))
                IQ, IK = sb([64, 4, 512], stack=asc), sb([64, 512], stack=asc)
                yield from sparse_in(i, SM, SZ, KT, QT, VV, IQ, IK, wi[:, :, :], ready, list(yra.values()))
                smc.close()
                yc = []
                g2 = {}
                gsc = scope()

                def gate_part():
                    sub = scope()
                    GT = sb([128, 4, 512], stack=sub)
                    gf = {}
                    for hf in range(2):
                        gt = {}
                        yield from gates(i, 0, hf, GT, gt, ready, gf)
                        gf = yield from branch(False, hf, GT, gt, M, YA, yra, mt)
                    sub.close()
                    ysc.close()
                    for hf in range(2):
                        g2[hf] = (sb([128, 4, 512], stack=gsc), {})
                        yield from gates(i, 2, hf, g2[hf][0], g2[hf][1], ready, {})

                both(gate_part(), sparse(i, SZ, KT, QT, VV, IQ, IK, wi[:, :, :], yc), R2_)
                asc.close()
                Y = [sb([128, 4, 512], f32r, gsc) for _ in range(2)]
                yr = to_branch(SZ, Y, yc)
                for hf in range(2):
                    yield from branch(False, hf, g2[hf][0], g2[hf][1], M, Y, yr, mt)
                mr = {k: store_split(M[:, k, :], k, (AH[:, k, :], AL[:, k, :]), None, mt[k], P.last())
                      for k in range(8)}
                gsc.close()
                for hf in range(2):
                    def ev(b, B, tok):
                        xs = X[:, b, 512 * hf:512 * hf + 512]
                        return [V(lambda e: e.tensor_tensor(xs, xs, B, ALU.add), tok)]
                    yield from gemm("wout", "TM", (AH, AL), 512, 8, 512, ev, mr)
                base.close()
                if stop == f"l{i}":
                    return

        R1, R2_ = 1.0, 1.0
        if stop != "b2only":
            run(block1())
        else:
            while state["used"] < next(j for j, u in enumerate(units) if u[0] == "sm"):
                u = state["used"]
                state["used"] += 1
                release_raw(u, parts[u])
        if stop is None or stop[0] in "bl":
            run(block2())
        fence()
        s_out = sem("s_out")
        S.wait(V.last(), A.last(), G.last(), P.last())
        t = S.dma(lambda e: e.dma_start(a_out.rearrange("b (t p) d -> p (b t) d", p=128), X[:, :, :]), s_out)
        S.wait(t)
        for p in s_raw:
            if p.n:
                S.wait((p, p.n))


def pack(inputs):
    a = {k: np.asarray(v) for k, v in inputs.items()}

    def unit(u):
        _, name, index, row, tiles, cols = u
        m = a[name][index]
        if name == "pool_w_2":
            return m.transpose(1, 0, 2).reshape(-1)
        m = np.concatenate([m[row:row + 128 * tiles, c0:c1] for c0, c1 in cols], axis=1)
        return m.reshape(tiles, 128, -1).transpose(1, 0, 2).reshape(-1)

    def col(v):
        return v.reshape(-1, 128).T

    def taps(w):
        return w.reshape(w.shape[0], -1, 128).transpose(2, 1, 0).reshape(128, -1)

    def cols(parts, i):
        return np.concatenate([taps(a[n][i]) if n in ("conf_dw_w", "sc_dw_w", "conv_w_2") else col(a[n][i])
                               for n, _ in parts], axis=1)

    def tiled(v, nt):
        return v.reshape(nt, 128, -1).transpose(1, 0, 2)

    out = {
        "wbig": np.concatenate([unit(u) for u in plan()]),
        "wmod": np.concatenate([unit(u) for i in range(L) for u in mod_plan(i)]),
        "x": tiled(a["x"], 4),
        "ctx": tiled(a["ctx"], 2),
        "cv": np.stack([col(a["c"]), col(a["c_ctx"])], axis=2),
        "cols1": np.stack([cols(COLS1, i) for i in range(L)], axis=1),
        "cols2": np.stack([cols(COLS2, i) for i in range(L)], axis=1),
        "rows2": np.stack([np.concatenate([np.broadcast_to(a[n][i][None, :], (128, w)) for n, w in ROWS2], axis=1)
                           for i in range(L)], axis=1),
        "const": constants(),
    }
    return {"in_" + k: np.ascontiguousarray(v) for k, v in out.items()}


def kernel(**inputs):
    import concourse.bacc as _bacc
    from concourse.bass_utils import run_bass_kernel_spmd as _run

    arrays = pack(inputs)
    nc = _bacc.Bacc("TRN2", target_bir_lowering=False, num_devices=1)
    args = [nc.dram_tensor(k, v.shape, mybir.dt.from_np(v.dtype), kind="ExternalInput").ap()
            for k, v in arrays.items()]
    args.append(nc.dram_tensor("out_0", (1, 512, 1024), mybir.dt.float32, kind="ExternalOutput").ap())
    program(nc, *args)
    r = _run(nc, [arrays], core_ids=[0])
    return r.results[0]["out_0"]
```

```python
import math
from contextlib import ExitStack

import numpy as np
import concourse.bass as bass
from concourse import mybir

L = 2
NH, QD = 8, 96
BIG = 1.0e30
SMALL = -3.0e38
MARK = -3.3e38
SM1 = 1.0 / math.sqrt(96.0)
SM2 = 128.0 ** -0.5

IN1 = [("cf", [(416, 928)]), ("zt", [(0, 416)]), ("sc", [(1184, 1696)]), ("sb", [(928, 1184)])]
IN2 = {"sm": [(2048, 2056), (5128, 5452)], "qa": [(0, 512)], "ka": [(512, 1024)], "va": [(1024, 1536)],
       "za": [(1536, 2048)], "ub": [(2056, 2568)], "zb": [(2568, 3080)], "qc": [(3080, 3592)],
       "kc": [(3592, 4104)], "vc": [(4104, 4616)], "zc": [(4616, 5128)]}


def gate_cols(n, half):
    at = 5452 + 1024 * n + 512 * half
    return [(at, at + 512)]


def width(cols):
    return sum(b - a for a, b in cols)


def plan():
    out = []

    def block(key, name, index, row, tiles, cols):
        for r in range(0, tiles, 2):
            out.append((key, name, index, row + 128 * r, 2, cols))

    def mix1(i, last_ctx=False):
        for key, cols in IN1[1:2] if last_ctx else IN1:
            block(key, "w_in", (i,), 0, 8, cols)
        if not last_ctx:
            for h in range(2):
                out.append(("wq", "w_q_b", (i,), 0, 2, [(384 * h, 384 * h + 384)]))
        out.append(("wkv", "w_kv_b", (i,), 0, 1, [(0, 1024)]))
        if not last_ctx:
            for h in range(2):
                block("wo", "w_o", (i,), 0, 8, [(512 * h, 512 * h + 512)])

    def mlp(i):
        for g in range(4):
            for h in range(2):
                block("w1", "w_mlp_in", (i,), 0, 8, [(1024 * g + 512 * h, 1024 * g + 512 * h + 512)])
            for h in range(2):
                block("w2", "w_mlp_out", (i,), 1024 * g, 8, [(512 * h, 512 * h + 512)])

    mix1(0)
    mix1(0)
    mlp(0)
    mix1(1, last_ctx=True)
    mlp(0)
    mix1(1)
    mlp(1)

    def gate(i, n, h):
        block("gate", "w_in_2", (i,), 0, 8, gate_cols(n, h))

    def br(i, n, h):
        block("br", "w_branch_2", (i, n), 0, 4, [(512 * h, 512 * h + 512)])

    for i in range(L):
        for key in ("sm", "qa", "ka", "va", "za", "ub", "zb"):
            block(key, "w_in_2", (i,), 0, 8, IN2[key])
        out.append(("pw", "pool_w_2", (i,), 0, 4, [(0, 128)]))
        for h in range(2):
            gate(i, 1, h)
            br(i, 1, h)
        for key in ("kc", "qc", "vc", "zc"):
            block(key, "w_in_2", (i,), 0, 8, IN2[key])
        for h in range(2):
            gate(i, 0, h)
            br(i, 0, h)
        for h in range(2):
            gate(i, 2, h)
        for h in range(2):
            br(i, 2, h)
        for h in range(2):
            block("wout", "w_out_2", (i,), 0, 8, [(512 * h, 512 * h + 512)])
    return out


def mod_plan(i):
    return [("mod", "w_mod", (i,), 0, 8, [(128 * j, 128 * j + 128)]) for j in range(48)]


COLS1 = [("b_mod", 48), ("g_pre_mix", 8), ("g_post_mix", 8), ("g_pre_mlp", 8), ("g_post_mlp", 8),
         ("g_q", 2), ("g_kv", 1), ("conf_dw_w", 62), ("conf_dw_b", 2), ("conf_ln_g", 2), ("conf_ln_b", 2),
         ("sc_dw_w", 6), ("g_branch", 8)]
COLS2 = [("norm_g_2", 8), ("gate_b_2", 24), ("conv_w_2", 48), ("dn_onorm_2", 1), ("pool_scale_2", 4)]
ROWS2 = [("a_log_2", 4), ("dt_bias_2", 4), ("q_norm_2", 128), ("k_norm_2", 128)]


def places(parts):
    at, out = 0, {}
    for name, n in parts:
        out[name] = (at, at + n)
        at += n
    return out, at


CONSTS = [("ident", 128), ("ut", 128), ("ml", 128), ("mu", 128), ("lev", 7 * 128), ("tri", 128), ("cb", 128),
          ("pc", 64), ("r1c", 4 * 16), ("r1s", 4 * 16), ("rac", 4 * 64), ("ras", 4 * 64),
          ("ric", 4 * 32), ("ris", 4 * 32)]


def constants():
    at, n = places(CONSTS)
    c = np.zeros((128, n), np.float32)

    def put(name, a):
        c[:, at[name][0]:at[name][1]] = np.asarray(a, np.float32).reshape(128, -1)

    i, j = np.arange(128)[:, None], np.arange(128)[None, :]
    put("ident", i == j)
    put("ut", i <= j)
    put("ml", np.where(j < i, 0.0, -BIG))
    put("mu", np.where(i <= j, 0.0, -BIG))
    put("lev", np.stack([(i // (2 << s) == j // (2 << s)) & ((i >> s) % 2 == 1) & ((j >> s) % 2 == 0)
                         for s in range(7)], 1))
    put("tri", np.where(j <= i, 3.3e38, SMALL))
    put("cb", np.where(j <= i, 0.0, -BIG))
    pc = np.zeros((4, 16), np.float32)
    for g, w in enumerate((2, 4, 8, 16)):
        pc[g] = np.float32(1.0) / np.minimum(np.arange(1, 17), w).astype(np.float32)
    put("pc", np.broadcast_to(pc.reshape(1, 64), (128, 64)))

    def tables(pos, dim):
        inv = (10000.0 ** (-np.arange(0, dim, 2, dtype=np.float64) / dim)).astype(np.float32)
        ang = (pos.astype(np.float32)[:, None] * inv[None, :]).astype(np.float64)
        return np.cos(ang).astype(np.float32), np.sin(ang).astype(np.float32)

    def tiled(a):
        return a.reshape(4, 128, -1).transpose(1, 0, 2)

    t = np.arange(512)
    inv = (1.0 / (10000.0 ** (np.arange(0, 16, 2, dtype=np.float64) / 16)).astype(np.float32)).astype(np.float32)
    ar = ((t // 64).astype(np.float32)[:, None] * inv).astype(np.float64)
    ac = ((t % 64).astype(np.float32)[:, None] * inv).astype(np.float64)
    both = np.concatenate([ar, ac], 1)
    put("r1c", tiled(np.cos(both)))
    put("r1s", tiled(np.sin(both)))
    for name, dim in (("ra", 128), ("ri", 64)):
        co, si = tables(t, dim)
        put(name + "c", tiled(co))
        put(name + "s", tiled(si))
    return c






class Sem:
    def __init__(self, handle, name):
        self.h, self.name, self.n = handle, name, 0


class Engine:

    def __init__(self, eng, sem, chain, task):
        self.eng, self.sem, self.chain, self.seen, self.task = eng, sem, chain, {}, task

    def wait(self, *toks):
        for t in toks:
            if t is None:
                continue
            if isinstance(t, list):
                self.wait(*t)
                continue
            sem, value = t
            if self.seen.get(sem.name, 0) < value:
                self.seen[sem.name] = value
                self.eng.wait_ge(sem.h, value)

    def __call__(self, make, *waits):
        self.wait(*waits)
        if self.chain:
            self.wait(self.last())
        self.sem.n += 1
        make(self.eng).then_inc(self.sem.h, 1)
        self.task[0].lasts[self.sem.name] = (self.sem, self.sem.n)
        return (self.sem, self.sem.n)

    def quiet(self, make, *waits):
        self.wait(*waits)
        make(self.eng)

    def dma(self, make, sem, *waits):
        self.wait(*waits)
        sem.n += 16
        make(self.eng).then_inc(sem.h, 16)
        return (sem, sem.n)

    def last(self):
        return (self.sem, self.sem.n) if self.sem.n else None


class Task:

    def __init__(self, banks, small, st):
        self.gb, self.small, self.st, self.lasts = banks, small, st, {}


class Scope:

    def __init__(self, arena, task):
        self.arena, self.task, self.held = arena, task, []

    def close(self):
        for a, b in self.held:
            self.arena.free(a, b, list(self.task[0].lasts.values()))
        self.held = []


class Arena:

    def __init__(self, lo, hi):
        self.holes = [(lo, hi, [])]

    def take(self, n):
        n = (n + 31) // 32 * 32
        total, start, toks = 0, None, []
        for a, b, t in self.holes:
            if start is None or a != start + total:
                start, total, toks = a, 0, []
            total, toks = total + b - a, toks + t
            if total >= n:
                break
        assert start is not None and total >= n, (n, [(a, b) for a, b, _ in self.holes])
        out = []
        for a, b, t in self.holes:
            if b <= start or a >= start + n:
                out.append((a, b, t))
            elif b > start + n:
                out.append((start + n, b, t))
        self.holes = out
        return start, start + n, toks

    def free(self, a, b, toks):
        self.holes = sorted(self.holes + [(a, b, toks)], key=lambda h: h[0])


def program(nc, a_wbig, a_wmod, a_x, a_ctx, a_cv, a_cols1, a_cols2, a_rows2, a_const, a_out, stop=None):
    f32, f32r = mybir.dt.float32, mybir.dt.float32r
    ALU, ACT, AX = mybir.AluOpType, mybir.ActivationFunctionType, mybir.AxisListType
    C1, NC1 = places(COLS1)
    C2, NC2 = places(COLS2)
    R2, NR2 = places(ROWS2)
    CC, NCC = places(CONSTS)
    units = plan()
    ctx = ExitStack()
    with ctx:
        names = [0]
        arena = Arena((nc.sbuf_base + 31) // 32 * 32, nc.sbuf_top // 32 * 32)
        task = [None]

        def scope():
            return Scope(arena, task)

        whole = scope()

        def sb(shape, dt=f32, stack=None):
            names[0] += 1
            a, b, toks = arena.take(4 * int(np.prod(shape[1:])))
            (stack or whole).held.append((a, b))
            for e_ in (V, A, G, S):
                e_.wait(*toks)
            return nc.alloc_sbuf_tensor_at(f"t{names[0]}", shape, dt, offset=a)

        def sem(name):
            return Sem(ctx.enter_context(nc.semaphore(name)), name)

        V, A, G, P, S = (Engine(e, sem(n), n in ("s_v", "s_a", "s_g"), task) for e, n in ((nc.vector, "s_v"), (nc.scalar, "s_a"), (nc.gpsimd, "s_g"),
                                                        (nc.tensor, "s_p"), (nc.sync, "s_s")))

        X = sb([128, 4, 1024])
        first = scope()
        XC = sb([128, 2, 1024], stack=first)
        AH, AL = sb([128, 8, 512], f32r), sb([128, 8, 512], f32r)
        NR, NS = 3, 3
        RAW = [sb([128, 1024]) for _ in range(NR)]
        WH = [sb([128, 1024], f32r) for _ in range(NS)]
        WL = [sb([128, 1024], f32r) for _ in range(NS)]
        K = sb([128, NCC])
        cols2 = sb([128, L, NC2])
        rows2 = sb([128, L, NR2])
        cols1 = sb([128, L, NC1], stack=first)
        SCV = sb([128, 8, 2], stack=first)
        MODS = [sb([128, 48, 2], stack=first) for _ in range(L)]
        SA1S = [sb([128, 2, 8, 2], stack=first) for _ in range(L)]
        GPS = [sb([128, 2, 8, 2], stack=first) for _ in range(L)]
        half = sb([128, 16])

        def con(name):
            return K[:, CC[name][0]:CC[name][1]]

        def c1(name, i):
            return cols1[:, i, C1[name][0]:C1[name][1]]

        def c2(name, i):
            return cols2[:, i, C2[name][0]:C2[name][1]]

        def r2(name, i):
            return rows2[:, i, R2[name][0]:R2[name][1]]

        ident = con("ident")

        PS = ctx.enter_context(nc.psum_tensor("ps", [128, 4096], f32))
        BK = [PS[:, 512 * n:512 * n + 512] for n in range(8)]
        bfree = [[] for _ in range(8)]
        busy = [False] * 8
        main, side = (Task(list(b_), list(c_), sb([128, 64])) for b_, c_ in
                      (((0, 1, 2, 3), (4, 5, 6, 7)), ((4, 5, 6, 7), (4, 5, 6, 7))))
        task[0] = main

        def pair():
            sm = task[0].small
            n = next(n for n in sm if n % 2 == 0 and n + 1 in sm and not busy[n] and not busy[n + 1])
            sm.remove(n)
            sm.remove(n + 1)
            sm += [n, n + 1]
            busy[n] = busy[n + 1] = True
            return PS[:, 512 * n:512 * n + 1024], n, bfree[n] + bfree[n + 1]

        def free_pair(n, toks):
            for m in (n, n + 1):
                busy[m] = False
                bfree[m] = list(toks)

        def bank():
            sm = task[0].small
            n = next(n for n in sm if not busy[n])
            sm.remove(n)
            sm.append(n)
            busy[n] = True
            return BK[n], n, list(bfree[n])

        def free_bank(n, *toks):
            busy[n] = False
            bfree[n] = list(toks)

        def run(gen):
            for _ in gen:
                pass

        def both(gen, other, ratio=1.0, late=0):
            due, left = -ratio * late, True
            main.small = list(main.gb)
            side.lasts = dict(main.lasts)
            for _ in gen:
                due += ratio
                while left and due >= 1.0:
                    due -= 1.0
                    task[0] = side
                    left = next(other, "end") != "end"
                task[0] = main
            task[0] = side
            side.small, side.spare = list(range(4, 8)), None
            if left:
                run(other)
            task[0] = main
            main.small = [4, 5, 6, 7]
            for k_, v_ in side.lasts.items():
                main.lasts[k_] = max(main.lasts.get(k_, v_), v_, key=lambda t: t[1])

        s_in = sem("s_in")
        s_raw = [sem(f"s_raw{n}") for n in range(NR)]
        s_in1 = sem("s_in1")
        for dst, src in ((SCV[:, :, :], a_cv), (cols1[:, :, :], a_cols1), (K[:, :], a_const)):
            S.dma(lambda e, dst=dst, src=src: e.dma_start(dst, src), s_in1)
        loaded = (s_in1, s_in1.n)

        def load_rest():
            for dst, src in ((XC[:, :, :], a_ctx), (cols2[:, :, :], a_cols2), (rows2[:, :, :], a_rows2),
                             (X[:, :, :], a_x)):
                S.dma(lambda e, dst=dst, src=src: e.dma_start(dst, src), s_in)
            for _ in range(NR):
                fetch()

        offs, at = [], 0
        for u in units:
            offs.append(at)
            at += 128 * u[4] * width(u[5])
        raw_free = [[] for _ in range(NR)]
        w_free = [[] for _ in range(NS)]
        state = {"fetched": 0, "split": 0, "used": 0, "nsplit": 0}
        parts = {}

        def fetch():
            u = state["fetched"]
            if u >= len(units):
                return
            n = units[u][4] * width(units[u][5])
            src = a_wbig[offs[u]:offs[u] + 128 * n].rearrange("(p n) -> p n", p=128)
            dst = RAW[u % NR][:, 0:n]
            parts[u] = S.dma(lambda e: e.dma_start(dst, src), s_raw[u % NR], raw_free[u % NR])
            state["fetched"] += 1

        released = set()

        def release_raw(u, *toks):
            raw_free[u % NR] = list(toks)
            released.add(u)
            while state["fetched"] < len(units) and state["fetched"] - NR in released:
                fetch()

        def direct(u):
            return units[u][0] in ("wq", "wkv", "pw")

        split_of = {}

        def split(u):
            if u >= len(units) or u in split_of or direct(u):
                return
            n = units[u][4] * width(units[u][5])
            s = state["nsplit"] % NS
            state["nsplit"] += 1
            raw, hi, lo = RAW[u % NR][:, 0:n], WH[s][:, 0:n], WL[s][:, 0:n]
            t1 = A(lambda e: e.activation(hi, raw, ACT.Copy), parts[u], w_free[s])
            t2 = G(lambda e: e.tensor_tensor(lo, raw, hi.bitcast(f32), ALU.subtract), parts[u], t1, w_free[s])
            split_of[u] = (s, hi, lo, t1, t2)
            release_raw(u, t1, t2)

        def use(key):
            u = state["used"]
            state["used"] += 1
            assert units[u][0] == key, (units[u][0], key)
            return u

        GAP = (8, 6, 4)
        fill = {"work": iter(()), "rate": 0.0, "due": 0.0}

        def tick():
            fill["due"] += fill["rate"]
            while fill["due"] >= 1.0:
                fill["due"] -= 1.0
                next(fill["work"], None)

        def start_fill(work, rate):
            fill.update(work=work, rate=rate, due=0.0)
            next(work)

        def gap(n):
            if task[0] is main:
                for _ in range(n):
                    next(fill["work"], None)

        def end_fill():
            run(fill["work"])
            fill["rate"] = 0.0

        later = []

        def defer(f):
            later.append(f)

        def flush():
            while later:
                later.pop(0)()

        def gemm(key, mode, act, T, tiles, w, evac, ready):
            aH, aL = act
            nb = T // 128 if mode == "TM" else w // 128
            GB, gfree = [BK[n] for n in task[0].gb], bfree
            for kh in range(tiles // 2):
                u = use(key)
                split(u)
                split(u + 1)
                if u + 2 < state["fetched"]:
                    split(u + 2)
                s, hi, lo, t1, t2 = split_of[u]
                hi3, lo3 = hi.rearrange("p (k n) -> p k n", k=2), lo.rearrange("p (k n) -> p k n", k=2)
                for k in range(2):
                    kk = 2 * kh + k
                    P.wait(t1, t2, ready[kk] if isinstance(ready, dict) else ready)
                    for b in range(nb):
                        if kk == 0:
                            P.wait(gfree[task[0].gb[b]])
                        for n, (wp, ap) in enumerate(((hi3, aH), (hi3, aL), (lo3, aH))):
                            if mode == "TM":
                                lhs, rhs = ap[:, kk, 128 * b:128 * b + 128], wp[:, k, :]
                                out = GB[b][:, 0:w]
                            else:
                                lhs, rhs = wp[:, k, 128 * b:128 * b + 128], ap[:, kk, 0:T]
                                out = GB[b][:, 0:T]
                            first, final = kk == 0 and n == 0, kk == tiles - 1 and n == 2

                            def mm(e, out=out, lhs=lhs, rhs=rhs, first=first, final=final):
                                return e.matmul(out, lhs, rhs, start=first, stop=final)

                            if n == 2 and (final or (k == 1 and b == nb - 1)):
                                tok = P(mm)
                            else:
                                P.quiet(mm)
                        if kk == tiles - 1:
                            gfree[task[0].gb[b]] = evac(b, GB[b], tok)
                        if b % 2:
                            tick()
                            if later and task[0] is main:
                                later.pop(0)()
                            yield
                w_free[s] = [tok]
            return tok

        def rstd(out, ss, n, inv, eps, *waits):
            t = V(lambda e: e.tensor_scalar(out, ss, inv, eps, ALU.mult, ALU.add), *waits)
            return G(lambda e: e.tensor_tensor(out, out, half[:, 0:n], ALU.pow), t)

        def sumsq(src, junk, out, *waits):
            return A(lambda e: e.activation(junk, src, ACT.Square, accum_out=out), *waits)

        t0 = G(lambda e: e.memset(half[:, :], -0.5))
        for e_ in (V, A, G, P):
            e_.wait(loaded)
        P.wait(t0)
        th = main.st[:, 0:16].rearrange("p (a b) -> p a b", a=8)
        t1 = A(lambda e: e.activation(th, SCV[:, :, :], ACT.Tanh, scale=0.5))
        t1 = V(lambda e: e.tensor_scalar(th, th, 0.5, 0.5, ALU.mult, ALU.add), t1)
        scv_ready = V(lambda e: e.tensor_tensor(SCV[:, :, :], SCV[:, :, :], th, ALU.mult), t1)

        def fence():
            toks = list(task[0].lasts.values())
            for e_ in (V, A, G, P):
                e_.wait(*toks)

        s_mod = [sem(f"s_mod{n}") for n in range(16)]
        modtok = {}

        def modulation(i, slots, lo, hi):
            sc = scope()
            ring = [sb([128, 8, 128], stack=sc) for _ in range(slots)]
            rows = [sb([2, 128], stack=sc) for _ in range(2)]
            free, used = [None] * slots, [None, None]
            got = {}
            bm = c1("b_mod", i)

            def load(j):
                if j < hi:
                    n = j % slots
                    src = a_wmod[(48 * i + j) * 131072:(48 * i + j + 1) * 131072].rearrange("(p n) -> p n", p=128)
                    dst = ring[n][:, :, :].rearrange("p k n -> p (k n)")
                    got[j] = S.dma(lambda e: e.dma_start(dst, src), s_mod[n], free[n])

            def turn(j, a):
                rw = rows[j % 2]
                B, bn, w0 = bank()
                P.wait(a, w0)
                used[j % 2] = P(lambda e: e.transpose(B[:, 0:2], rw[:, :], ident[0:2, 0:2]))
                t = A(lambda e: e.activation(MODS[i][:, j, :], B[:, 0:2], ACT.Identity, bias=bm[:, j:j + 1]),
                      used[j % 2])
                free_bank(bn, t)
                derived(i, j, t)

            for j in range(lo, lo + slots):
                load(j)
            yield
            for j in range(lo, hi):
                W, rw = ring[j % slots], rows[j % 2]
                B, bn, w0 = bank()
                P.wait(got[j], scv_ready, w0)
                for k in range(8):
                    def mm(e, k=k):
                        return e.matmul(B[0:2, 0:128], SCV[:, k, :], W[:, k, :], start=(k == 0), stop=(k == 7))
                    tok = P(mm) if k == 7 else P.quiet(mm)
                a = A(lambda e: e.activation(rw[:, :], B[0:2, 0:128], ACT.Copy), tok, used[j % 2])
                free_bank(bn, a)
                free[j % slots] = tok
                if j > lo:
                    turn(j - 1, last)
                    load(j - 1 + slots)
                last = a
                yield
            turn(hi - 1, last)
            sc.close()

        def derived(i, j, t):
            out, m = modtok.setdefault(i, []), j // 24
            if j % 24 == 15:
                gp, sc_ = c1(("g_pre_mix", "g_pre_mlp")[m], i), MODS[i][:, 24 * m + 8:24 * m + 16, :]
                t = G(lambda e: e.tensor_scalar(SA1S[i][:, m, :, :], sc_, 1.0, None, ALU.add), t)
                out.append(G(lambda e: e.tensor_tensor(SA1S[i][:, m, :, :], SA1S[i][:, m, :, :],
                                                       gp.unsqueeze(2).to_broadcast([128, 8, 2]), ALU.mult), t))
            if j % 24 == 23:
                gq, gt = c1(("g_post_mix", "g_post_mlp")[m], i), MODS[i][:, 24 * m + 16:24 * m + 24, :]
                out.append(G(lambda e: e.tensor_tensor(GPS[i][:, m, :, :], gt,
                                                       gq.unsqueeze(2).to_broadcast([128, 8, 2]), ALU.mult), t))

        def first_modulation():
            sc = scope()
            W = [sb([128, 8, 128], stack=sc) for _ in range(16)]
            row = [sb([2, 512], stack=sc) for _ in range(2)]
            bm = c1("b_mod", 0)
            got = {}

            def load(j):
                src = a_wmod[j * 131072:(j + 1) * 131072].rearrange("(p n) -> p n", p=128)
                dst = W[j % 16][:, :, :].rearrange("p k n -> p (k n)")
                got[j] = S.dma(lambda e: e.dma_start(dst, src), s_mod[j % 16])

            for j in range(16):
                load(j)
            yield
            used = [None, None]
            for g in range(4):
                B, bn, w0 = bank()
                P.wait(scv_ready, w0)
                for j in range(4 * g, 4 * g + 4):
                    P.wait(got[j])
                    for k in range(8):
                        tok = P(lambda e: e.matmul(B[0:2, 128 * (j - 4 * g):128 * (j - 4 * g) + 128], SCV[:, k, :],
                                                   W[j % 16][:, k, :], start=(k == 0), stop=(k == 7)))
                rw = row[g % 2]
                a = A(lambda e: e.activation(rw[:, :], B[0:2, :], ACT.Copy), tok, used[g % 2])
                free_bank(bn, a)
                B, bn, w0 = bank()
                P.wait(a, w0)
                for q in range(4):
                    used[g % 2] = P(lambda e: e.transpose(B[:, 2 * q:2 * q + 2], rw[:, 128 * q:128 * q + 128],
                                                          ident[0:2, 0:2]))
                t = V(lambda e: e.tensor_tensor(MODS[0][:, 4 * g:4 * g + 4, :],
                                                B[:, 0:8].rearrange("p (a b) -> p a b", b=2),
                                                bm[:, 4 * g:4 * g + 4].unsqueeze(2).to_broadcast([128, 4, 2]),
                                                ALU.add), used[g % 2])
                free_bank(bn, t)
                derived(0, 4 * g + 3, t)
            sc.close()

        def store_split(src, k, dst, tmp_free, *waits):
            h, l = dst
            t1 = V(lambda e: e.tensor_copy(h, src), *waits)
            t2 = G(lambda e: e.tensor_tensor(l, src, h.bitcast(f32), ALU.subtract), t1, *waits)
            return [t1, t2]

        rs = sb([128, 16], stack=first)
        written = {}

        def prep(x, nt, scale, shift, stk, afree):
            T = 128 * nt
            A.wait(afree)
            J, jn, w0 = pair()
            tk = None
            for t in range(nt):
                tk = sumsq(x[:, t, :], J[:, :], task[0].st[:, t:t + 1], w0 if t == 0 else None,
                           written.get((id(x), t)))
            free_pair(jn, [tk])
            r = task[0].st[:, 8:8 + nt]
            tr = rstd(r, task[0].st[:, 0:nt], nt, 1.0 / 1024, 1e-6, tk)
            gap(GAP[2])
            xn = [sb([128, nt, 128], stack=stk) for _ in range(2)]
            tm = [sb([128, T], stack=stk) for _ in range(2)]
            xfree, tfree = [None, None], [[], []]
            ready = {}
            xt = {}

            def scaled(k):
                y = xn[k % 2]
                xt[k] = V(lambda e: e.tensor_tensor(y[:, :, :], x[:, :, 128 * k:128 * k + 128],
                                                    r.unsqueeze(2).to_broadcast([128, nt, 128]), ALU.mult),
                          tr, xfree[k % 2])

            scaled(0)
            for k in range(8):
                y, f = xn[k % 2], tm[k % 2]
                B, bn, w0 = bank()
                tok = xfree[k % 2] = transposes([B[:, 128 * t:128 * t + 128] for t in range(nt)],
                                                [y[:, t, :] for t in range(nt)], [xt[k], w0])
                if k < 7:
                    scaled(k + 1)
                if shift is None:
                    e1 = A(lambda e: e.activation(f[:, :], B[:, 0:T], ACT.Copy, scale=scale(k)), tok, tfree[k % 2])
                else:
                    e1 = A(lambda e: e.activation(f[:, :], B[:, 0:T], ACT.Identity, bias=shift(k),
                                                  scale=scale(k)), tok, tfree[k % 2])
                free_bank(bn, e1)
                ready[k] = store_split(f[:, :], k, (AH[:, k, 0:T], AL[:, k, 0:T]), None, e1, afree)
                gap(k < GAP[0])
                tfree[k % 2] = ready[k]
            return ready

        def row_of(col, stk, *waits):
            row = sb([128, 1024], stack=stk)
            Q, qn, w0 = pair()
            P.wait(w0, *waits)
            P.wait(modtok[0], modtok.get(1))
            for j in range(8):
                tok = P(lambda e: e.matmul(Q[:, 128 * j:128 * j + 128],
                                           col[:, j:j + 1].to_broadcast([128, 128]), ident, start=True, stop=True))
            t = A(lambda e: e.activation(row[:, :], Q[:, :], ACT.Copy), tok)
            free_pair(qn, [t])
            return row, t


        def residual(x, y, nt, row, trow, halves):
            gap(GAP[1])
            ss = rs[:, 0:2 * nt].rearrange("p (t h) -> p t h", h=2)
            r = rs[:, 8:8 + nt]
            a = V(lambda e: e.tensor_tensor(r, ss[:, :, 0], ss[:, :, 1], ALU.add), halves)
            tr = rstd(r, r, nt, 1.0 / 1024, 1e-6, a)
            for t in range(nt):
                if row is None:
                    a = V(lambda e: e.scalar_tensor_tensor(x[:, t, :], y[:, t, :], r[:, t:t + 1], x[:, t, :],
                                                           ALU.mult, ALU.add), tr)
                else:
                    a = V(lambda e: e.scalar_tensor_tensor(y[:, t, :], y[:, t, :], r[:, t:t + 1], row[:, :],
                                                           ALU.mult, ALU.mult), tr, trow)
                    a = V(lambda e: e.tensor_tensor(x[:, t, :], x[:, t, :], y[:, t, :], ALU.add), a)
                written[(id(x), t)] = a

        def rotate(dst, p1, p2, co, si, tmp, waits):
            d1, d2 = dst
            ta, tb, tc, td = tmp
            a = V(lambda e: e.tensor_tensor(ta, p1, co, ALU.mult), *waits)
            b = V(lambda e: e.tensor_tensor(tb, p2, si, ALU.mult))
            c = G(lambda e: e.tensor_tensor(tc, p2, co, ALU.mult), *waits)
            d = G(lambda e: e.tensor_tensor(td, p1, si, ALU.mult))
            u = V(lambda e: e.tensor_tensor(d1, ta, tb, ALU.subtract), a, b, c, d)
            return [u, V(lambda e: e.tensor_tensor(d2, tc, td, ALU.add), c, d)]

        def transposes(out, srcs, waits):
            P.wait(*waits)
            for j, (o, s_) in enumerate(zip(out, srcs)):
                f = (lambda e, o=o, s_=s_: e.transpose(o, s_, ident))
                if j < len(srcs) - 1:
                    P.quiet(f)
                else:
                    return P(f)

        def attention1(qtm, ktm, Vb, nk, nt, Z8, stk, finish, aside):
            KT = [sb([96, nk * 128], stack=stk) for _ in range(2)]
            QT = [sb([96, nt * 128], stack=stk) for _ in range(2)]
            PP = [sb([128, nk * 128], stack=stk) for _ in range(2)]
            PT = [sb([128, nk * 128], stack=stk) for _ in range(2)]
            sm = task[0].st
            free_h, free_p, free_t, free_s = [[], []], [None] * 3, [None] * 2, [None] * 3
            nh = (nk + 1) // 2 * 128
            was = task[0].small
            task[0].small = list(range(8))
            kq = {}

            def load_head(h, last):
                b = h % 2
                Q, qn, w0 = pair()
                tok = transposes([Q[0:96, 128 * t:128 * t + 128] for t in range(nt)],
                                 [qtm[:, t, 96 * h:96 * h + 96] for t in range(nt)], [w0])
                eq = A(lambda e: e.activation(QT[b][:, :], Q[0:96, 0:128 * nt], ACT.Copy), tok, free_h[b])
                got, at = [eq], eq
                for k0 in range(0, nk, 4):
                    kn = min(4, nk - k0)
                    base = 512 if k0 == 0 else 0
                    tok = transposes([Q[0:64, base + 128 * j:base + 128 * j + 128] for j in range(kn)],
                                     [ktm[:, k0 + j, 64 * h:64 * h + 64] for j in range(kn)],
                                     [at if k0 else None])
                    at = V(lambda e: e.tensor_copy(KT[b][0:64, 128 * k0:128 * (k0 + kn)],
                                                   Q[0:64, base:base + 128 * kn]), tok, free_h[b], eq)
                    got.append(at)
                if h < 2:
                    for k0 in range(0, nk, 4):
                        kn = min(4, nk - k0)
                        tok = transposes([Q[0:96, 128 * j:128 * j + 128] for j in range(kn)],
                                         [ktm[:, k0 + j, 448:544] for j in range(kn)], [at, eq])
                        at = V(lambda e: e.tensor_copy(KT[b][64:96, 128 * k0:128 * (k0 + kn)],
                                                       Q[64:96, 0:128 * kn]), tok)
                        got.append(at)
                free_pair(qn, [at, eq])
                kq[h] = got

            def logits(u):
                h, t = divmod(u, nt)
                b, n, m = h % 2, u % 3, u % 2
                Q, qn, w0 = pair()
                P.wait(w0, kq[h])
                for j in range(2):
                    c0, cn = j * nh, min(nh, nk * 128 - j * nh)
                    tok = P(lambda e: e.matmul(Q[:, 512 * j:512 * j + cn], QT[b][:, 128 * t:128 * t + 128],
                                               KT[b][:, c0:c0 + cn], start=True, stop=True))
                free_h[b] = [tok]
                lg = Q.rearrange("p (a n) -> p a n", a=2)[:, :, 0:nh]
                mx, nm, rs, ri = (sm[:, 32 + 4 * n + j:33 + 4 * n + j] for j in range(4))
                a = V(lambda e: e.tensor_reduce(mx, lg, AX.XY, ALU.max), tok, free_s[n])
                a = V(lambda e: e.tensor_scalar(nm, mx, -SM1, None, ALU.mult), a)
                te = A(lambda e: e.activation(PP[m][:, :].rearrange("p (a n) -> p a n", a=2), lg, ACT.Exp,
                                              bias=nm, scale=SM1, accum_out=rs), a, free_p[m])
                return Q, qn, te, rs, ri

            def turned(u, job):
                Q, qn, te, rs, ri = job
                n, m = u % 3, u % 2
                tn = V(lambda e: e.reciprocal(ri, rs), te)
                tok = transposes([Q[:, 128 * j:128 * j + 128] for j in range(nk)],
                                 [PP[m][:, 128 * j:128 * j + 128] for j in range(nk)], [te])
                free_p[m] = tok
                c = min(512, 128 * nk)
                ev = [A(lambda e: e.activation(PT[m][:, 0:c], Q[:, 0:c], ACT.Copy), tok, free_t[m])]
                if nk > 4:
                    ev.append(V(lambda e: e.tensor_copy(PT[m][:, 512:128 * nk], Q[:, 512:128 * nk]), tok, free_t[m]))
                return Q, qn, ev, ri, tn

            def valued(u, job):
                Q, qn, ev, ri, tn = job
                h, t = divmod(u, nt)
                m = u % 2
                P.wait(ev)
                for j in range(nk):
                    tok = P(lambda e: e.matmul(Q[:, 896:960], PT[m][:, 128 * j:128 * j + 128],
                                               Vb[:, j, 64 * h:64 * h + 64], start=(j == 0), stop=(j == nk - 1)))
                free_t[m] = tok
                o = V(lambda e: e.tensor_scalar(Z8[:, t, 64 * h:64 * h + 64], Q[:, 896:960], ri, None, ALU.mult),
                      tok, tn)
                free_s[u % 3] = o
                free_pair(qn, [o] + ev)
                return o

            P.wait(A.last(), V.last(), G.last())
            load_head(0, None)
            jobs, turn_ = {}, {}
            n_u = NH * nt
            for u in range(n_u + 2):
                if u < n_u:
                    jobs[u] = logits(u)
                if u >= 2:
                    o = valued(u - 2, turn_.pop(u - 2))
                    if u - 2 >= n_u - nt:
                        finish(u - 2 - n_u + nt, o)
                if 1 <= u <= n_u:
                    turn_[u - 1] = turned(u - 1, jobs.pop(u - 1))
                if u % nt == (1 if nt > 1 else 0) and u // nt + 1 < NH:
                    load_head(u // nt + 1, None)
                next(aside, None)
                yield
            task[0].small = was

        def mix1(i, s, x, nt, Z8, qtm, ktm, Vb, zT, zsc, last_ctx):
            T = 128 * nt
            t_off = 0 if s else 2
            rope = not s
            psc, sub = scope(), scope()
            ready = prep(x, nt, lambda k: SA1S[i][:, 0, k, s:s + 1], lambda k: MODS[i][:, k, s:s + 1], psc, modtok[i])
            psc.close()
            z = Z8[:, 0:416 * nt].rearrange("p (t n) -> p t n", t=nt)
            kr = z[:, 0:nt, 384:416]
            sub2 = scope()
            J = sb([128, 256], stack=sub2)
            tmp = [sb([128, nt, 2, 8], stack=sub2) for _ in range(4)]
            zt, zr, got = [], [], {}

            def latents():
                def ev_z(b, B, tok):
                    t = A(lambda e: e.activation(z[:, b, 0:416], B[:, 0:416], ACT.Copy), tok)
                    zt.append(t)
                    return [t]

                yield from gemm("zt", "TM", (AH, AL), T, 8, 416, ev_z, ready)
                st = task[0].st
                for t in range(nt):
                    sumsq(z[:, t, 0:256], J[:, :], st[:, t:t + 1], A.last())
                    tk = sumsq(z[:, t, 256:384], J[:, 0:128], st[:, 4 + t:5 + t], A.last())
                for c, n_ in ((0, 256), (4, 128)):
                    rr = st[:, 8 + c:8 + c + nt]
                    a = G(lambda e: e.tensor_scalar(rr, st[:, c:c + nt], 1.0 / n_, 1e-6, ALU.mult, ALU.add), tk)
                    a = G(lambda e: e.tensor_tensor(rr, rr, half[:, 0:nt], ALU.pow), a)
                for t in range(nt):
                    G(lambda e: e.tensor_scalar(z[:, t, 0:256], z[:, t, 0:256], st[:, 8 + t:9 + t], None, ALU.mult), a)
                    got["z"] = G(lambda e: e.tensor_scalar(z[:, t, 256:384], z[:, t, 256:384],
                                                           st[:, 12 + t:13 + t], None, ALU.mult), a)

            def turned_latents():
                gq, gkv = c1("g_q", i), c1("g_kv", i)
                for j in range(2 if last_ctx else 0, 3):
                    B, bn, w0 = bank()
                    tok = transposes([B[:, 128 * t:128 * t + 128] for t in range(nt)],
                                     [z[:, t, 128 * j:128 * j + 128] for t in range(nt)], [got["z"], w0])
                    sc = gq[:, j:j + 1] if j < 2 else gkv[:, 0:1]
                    zr.append(A(lambda e: e.activation(zT[:, j, 0:T], B[:, 0:T], ACT.Copy, scale=sc), tok))
                    free_bank(bn, zr[-1])
                if not rope:
                    return zt
                kv = kr.rearrange("p t (h a c) -> p t h a c", h=2, a=2)
                co = con("r1c").rearrange("p (t h c) -> p t h c", t=4, h=2)
                si = con("r1s").rearrange("p (t h c) -> p t h c", t=4, h=2)
                return rotate((kv[:, :, :, 0, :], kv[:, :, :, 1, :]), kv[:, :, :, 0, :], kv[:, :, :, 1, :], co, si,
                              [x_[:, :, :, :] for x_ in tmp], [zt])

            if last_ctx:
                yield from latents()
                krt = turned_latents()
            if not last_ctx:
                Cv = sb([128, 2, T], stack=sub)
                S2 = sb([128, 2, T], stack=sub)
                gg = S2
                m1 = sb([128, 512], stack=sub)
                m2 = sb([128, 256], stack=sub)
                cst = sb([128, nt, 16], stack=sub)
                rt = [sb([128, 8, 2, 8], stack=sub2) for _ in range(4)]
                U = sb([128, 2, T + 30], stack=sub2)
                H2 = sb([128, 2, T + 2], stack=sub2)
                for c in range(2):
                    G(lambda e: e.memset(U[:, c, 0:15], 0.0))
                    tz = G(lambda e: e.memset(U[:, c, T + 15:T + 30], 0.0))
                hold = {}

                def ev_cf(b, B, tok):
                    if b < 2:
                        hold[b] = A(lambda e: e.activation(U[:, b, 15:15 + T], B[:, 0:T], ACT.Copy), tok)
                        return [hold[b]]
                    c = b - 2
                    t = A(lambda e: e.activation(gg[:, c, :], B[:, 0:T], ACT.Tanh, scale=0.5), tok)
                    t1 = V(lambda e: e.tensor_scalar(gg[:, c, :], gg[:, c, :], 0.5, 0.5, ALU.mult, ALU.add), t)
                    hold[b] = V(lambda e: e.tensor_tensor(U[:, c, 15:15 + T], U[:, c, 15:15 + T], gg[:, c, :],
                                                          ALU.mult), t1, hold[c])
                    return [t]

                yield from gemm("cf", "FM", (AH, AL), T, 8, 512, ev_cf, ready)
                W = c1("conf_dw_w", i).rearrange("p (c k) -> p c k", c=2)
                db = c1("conf_dw_b", i)
                for c in range(2):
                    t = V(lambda e: e.tensor_scalar(Cv[:, c, :], U[:, c, 0:T], W[:, c, 0:1], db[:, c:c + 1],
                                                    ALU.mult, ALU.add), hold[2 + c], tz)
                    for k in range(1, 31):
                        t = V(lambda e, k=k: e.scalar_tensor_tensor(Cv[:, c, :], U[:, c, k:k + T], W[:, c, k:k + 1],
                                                                    Cv[:, c, :], ALU.mult, ALU.add), t)
                yield from latents()
                for c in range(2):
                    G(lambda e: e.memset(H2[:, c, 0:1], 0.0))
                    tz = G(lambda e: e.memset(H2[:, c, T + 1:T + 2], 0.0))
                hs = {}

                def ev_sc(b, B, tok):
                    if b < 2:
                        hs[b] = A(lambda e: e.activation(H2[:, b, 1:1 + T], B[:, 0:T], ACT.Copy), tok)
                        return [hs[b]]
                    hs[b] = V(lambda e: e.tensor_tensor(H2[:, b - 2, 1:1 + T], B[:, 0:T], H2[:, b - 2, 1:1 + T],
                                                        ALU.mult), tok, hs[b - 2])
                    W3 = c1("sc_dw_w", i).rearrange("p (c k) -> p c k", c=2)
                    c = b - 2
                    t = V(lambda e: e.tensor_scalar(S2[:, c, :], H2[:, c, 0:T], W3[:, c, 0:1], None, ALU.mult),
                          hs[b], tz)
                    for k in range(1, 3):
                        t = V(lambda e, k=k: e.scalar_tensor_tensor(S2[:, c, :], H2[:, c, k:k + T], W3[:, c, k:k + 1],
                                                                    S2[:, c, :], ALU.mult, ALU.add), t)
                    hs[b] = t
                    return [hs[b]]

                yield from gemm("sc", "FM", (AH, AL), T, 8, 512, ev_sc, ready)
                krt = turned_latents()

                def ev_sb(b, B, tok):
                    hs[b] = V(lambda e: e.tensor_tensor(S2[:, b, :], B[:, 0:T], S2[:, b, :], ALU.mult), tok, hs[b + 2])
                    return [hs[b]]

                adone = yield from gemm("sb", "FM", (AH, AL), T, 8, 256, ev_sb, ready)
            co = con("r1c").rearrange("p (t h c) -> p t h c", t=4, h=2)
            si = con("r1s").rearrange("p (t h c) -> p t h c", t=4, h=2)
            if not last_ctx:
                us = [use("wq"), use("wq")]
                Wq = [RAW[u % NR][:, 0:768].rearrange("p (k n) -> p k n", k=2) for u in us]
                for t in range(nt):
                    Q, qn, w0 = pair()
                    P.wait(parts[us[0]], parts[us[1]], w0, zr)
                    for hf in range(2):
                        for k in range(2):
                            tok = P(lambda e: e.matmul(Q[:, 512 * hf:512 * hf + 384], zT[:, k, 128 * t:128 * t + 128],
                                                       Wq[hf][:, k, :], start=(k == 0), stop=(k == 1)))
                    ev = A(lambda e: e.activation(qtm[:, t, :].rearrange("p (a n) -> p a n", a=2),
                                                  Q[:, :].rearrange("p (a n) -> p a n", a=2)[:, :, 0:384], ACT.Copy), tok)
                    free_pair(qn, [ev])
                    if rope:
                        v = qtm[:, t, :].rearrange("p (h n) -> p h n", h=8)[:, :, 64:96]
                        v = v.rearrange("p h (b a c) -> p h b a c", b=2, a=2)
                        rotate((v[:, :, :, 0, :], v[:, :, :, 1, :]), v[:, :, :, 0, :], v[:, :, :, 1, :],
                               co[:, t, :, :].unsqueeze(1).to_broadcast([128, 8, 2, 8]),
                               si[:, t, :, :].unsqueeze(1).to_broadcast([128, 8, 2, 8]),
                               [x_[:, :, :, :] for x_ in rt], [ev, V.last(), G.last()])
                for u in us:
                    release_raw(u, tok)
            V(lambda e: e.tensor_copy(ktm[:, t_off:t_off + nt, 512:544], kr), krt)
            u = use("wkv")
            for t in range(nt):
                Q, qn, w0 = pair()
                P.wait(parts[u], w0, zr)
                for hf in range(2):
                    tok = P(lambda e: e.matmul(Q[:, 512 * hf:512 * hf + 512], zT[:, 2, 128 * t:128 * t + 128],
                                               RAW[u % NR][:, 512 * hf:512 * hf + 512], start=True, stop=True))
                q3 = Q[:, :].rearrange("p (h n) -> p h n", h=8)
                k3 = ktm[:, t_off + t, 0:512].rearrange("p (h n) -> p h n", h=8)
                e1 = A(lambda e: e.activation(k3, q3[:, :, 0:64], ACT.Copy), tok)
                e2 = V(lambda e: e.tensor_copy(Vb[:, t_off + t, :].rearrange("p (h n) -> p h n", h=8),
                                               q3[:, :, 64:128]), tok, e1)
                free_pair(qn, [e1, e2])
            release_raw(u, tok)
            if last_ctx:
                sub2.close()
                sub.close()
                return
            g_br, G_ln = c1("g_branch", i), LN[i]
            sub2.close()
            zsc.close()
            tcv = [V.last(), adone]
            done = {0: [], 4: []}

            def put(src, c0, t, *waits):
                B, bn, w0 = bank()
                tok = transposes([B[:, 128 * c:128 * c + 128] for c in range(4)],
                                 [src[:, 128 * c:128 * c + 128] for c in range(4)], [w0, *waits])
                v = src.rearrange("p (c n) -> p c n", c=4)
                h, l = (x_[:, c0:c0 + 4, 128 * t:128 * t + 128] for x_ in (AH, AL))
                a = V(lambda e: e.tensor_tensor(v, B.rearrange("p (c n) -> p c n", c=4),
                                                g_br[:, c0:c0 + 4].unsqueeze(2).to_broadcast([128, 4, 128]),
                                                ALU.mult), tok)
                free_bank(bn, a)
                a = V(lambda e: e.tensor_copy(h, v), a, adone)
                b = G(lambda e: e.tensor_tensor(l, v, h.bitcast(f32), ALU.subtract), a, adone)
                done[c0] += [a, b]
                return [a, b]

            def conv_tail():
                free = []
                for t in range(nt):
                    ts, s_ = slice(128 * t, 128 * t + 128), cst[:, t, :]
                    B, bn, w0 = bank()
                    tok = transposes([B[:, 128 * c:128 * c + 128] for c in range(4)],
                                     [Cv[:, 0, ts], Cv[:, 1, ts], S2[:, 0, ts], S2[:, 1, ts]], [w0, tcv])
                    a = A(lambda e: e.activation(m1[:, :], B, ACT.Copy), tok, free)
                    free_bank(bn, a)
                    yield
                    u, v = m1[:, 0:256], m1[:, 256:512]
                    a = V(lambda e: e.bn_stats(s_[:, 0:6], u), a)
                    a = V(lambda e: e.bn_aggr(s_[:, 6:8], s_[:, 0:6]), a)
                    a = G(lambda e: e.tensor_scalar(s_[:, 8:9], s_[:, 7:8], 1e-6, None, ALU.add), a)
                    b = G(lambda e: e.tensor_tensor(s_[:, 8:9], s_[:, 8:9], half[:, 0:1], ALU.pow), a)
                    yield
                    a = G(lambda e: e.tensor_scalar(u, u, s_[:, 6:7], s_[:, 8:9], ALU.subtract, ALU.mult), b)
                    a = G(lambda e: e.tensor_tensor(u, u, G_ln[:, 0, :], ALU.mult), a)
                    a = G(lambda e: e.tensor_tensor(u, u, G_ln[:, 1, :], ALU.add), a)
                    yield
                    c = A(lambda e: e.activation(m2[:, :], u, ACT.Tanh, scale=0.5), a)
                    a = G(lambda e: e.tensor_scalar(m2[:, :], m2[:, :], 0.5, 0.5, ALU.mult, ALU.add), c)
                    a = G(lambda e: e.tensor_tensor(u, u, m2[:, :], ALU.mult), a)
                    yield
                    c = sumsq(u, m2[:, :], s_[:, 9:10], a)
                    c = sumsq(v, m2[:, :], s_[:, 10:11], c)
                    a = G(lambda e: e.tensor_scalar(s_[:, 11:13], s_[:, 9:11], 1.0 / 256, 1e-6, ALU.mult, ALU.add), c)
                    d = G(lambda e: e.tensor_tensor(s_[:, 11:13], s_[:, 11:13], half[:, 0:2], ALU.pow), a)
                    a = G(lambda e: e.tensor_scalar(u, u, s_[:, 11:12], None, ALU.mult), d)
                    a = G(lambda e: e.tensor_scalar(v, v, s_[:, 12:13], None, ALU.mult), d)
                    yield
                    free = put(m1[:, :], 4, t, a)
                    yield

            def finish(t, o):
                src = at[:, t, :]
                B, bn, w0 = bank()
                ss, rr_ = cst[:, t, 13:14], cst[:, t, 14:15]
                a = sumsq(src, B, ss, o, w0)
                free_bank(bn, a)
                a = G(lambda e: e.tensor_scalar(rr_, ss, 1.0 / 512, 1e-6, ALU.mult, ALU.add), a)
                a = G(lambda e: e.tensor_tensor(rr_, rr_, half[:, 0:1], ALU.pow), a)
                a = V(lambda e: e.tensor_scalar(src, src, rr_, None, ALU.mult), a)
                put(src, 0, t, a)

            end_fill()
            asub = scope()
            at = Z8[:, 0:512 * nt].rearrange("p (t n) -> p t n", t=nt)
            tail = conv_tail()
            yield from attention1(qtm, ktm, Vb, 2 if s else 6, nt, at, asub, finish, tail)
            run(tail)
            asub.close()
            sub.close()
            return {k: done[k // 4 * 4] for k in range(8)}

        def project(key, nt, y, ready, row, trow):
            yt = []
            for hf in range(2):
                def ev(b, B, tok):
                    cs = slice(512 * hf, 512 * hf + 512)
                    t = V(lambda e: e.tensor_tensor(y[:, b, cs], B[:, :], row[:, cs], ALU.mult), tok, trow)
                    a = A(lambda e: e.activation(B[:, :], B[:, :], ACT.Square,
                                                 accum_out=rs[:, 2 * b + hf:2 * b + hf + 1]), t)
                    yt.extend([t, a])
                    return [t, a]
                yield from gemm(key, "TM", (AH, AL), 128 * nt, 8, 512, ev, ready)
            return yt

        def mlp(i, s, x, nt):
            T = 128 * nt
            stk = scope()
            ready = prep(x, nt, lambda k: SA1S[i][:, 1, k, s:s + 1], lambda k: MODS[i][:, 24 + k, s:s + 1], stk, modtok[i])
            BH, BL = sb([128, 8, T], f32r, stk), sb([128, 8, T], f32r, stk)
            Y = sb([128, nt, 1024], stack=stk)
            r = [sb([128, T], stack=stk) for _ in range(3)]
            rfree = [None] * 3
            bfree, cnt = None, 0
            for g in range(4):
                done = {}
                for hf in range(2):
                    def ev(b, B, tok, hf=hf):
                        kk = 4 * hf + b
                        q = r[kk % 3]
                        a = A(lambda e: e.activation(q[:, :], B[:, 0:T], ACT.Relu), tok, rfree[kk % 3])
                        c = V(lambda e: e.tensor_tensor(q[:, :], q[:, :], q[:, :], ALU.mult), a)
                        done[kk] = store_split(q[:, :], kk, (BH[:, kk, :], BL[:, kk, :]), None, c, bfree)
                        rfree[kk % 3] = done[kk]
                        return [a]
                    yield from gemm("w1", "FM", (AH, AL), T, 8, 512, ev, ready)
                for hf in range(2):
                    def ev(b, B, tok, hf=hf, g=g):
                        y = Y[:, b, 512 * hf:512 * hf + 512]
                        if g == 0:
                            ytok[(b, hf)] = V(lambda e: e.tensor_copy(y, B[:, :]), tok)
                        else:
                            ytok[(b, hf)] = V(lambda e: e.tensor_tensor(y, B[:, :], y, ALU.add), tok, ytok[(b, hf)])
                        t = ytok[(b, hf)]
                        if g == 3:
                            ytok[(b, hf)] = A(lambda e: e.activation(B[:, :], y, ACT.Square,
                                                                     accum_out=rs[:, 2 * b + hf:2 * b + hf + 1]), t)
                        return [t, ytok[(b, hf)]]
                    if g == 0 and hf == 0:
                        ytok = {}
                    bfree = yield from gemm("w2", "TM", (BH, BL), T, 8, 512, ev, done)
                if g == 0:
                    row, trow = row_of(GPS[i][:, 1, :, s], stk)
            residual(x, Y, nt, row, trow, list(ytok.values()))
            stk.close()

        LN = [sb([128, 2, 256], stack=first) for _ in range(L)]

        def ln_rows():
            for i in range(L):
                B, bn, w0 = bank()
                P.wait(w0)
                for j, name in enumerate(("conf_ln_g", "conf_ln_b")):
                    for c in range(2):
                        col = c1(name, i)[:, c:c + 1].to_broadcast([128, 128])
                        tok = P(lambda e: e.matmul(B[:, 256 * j + 128 * c:256 * j + 128 * c + 128], col, ident,
                                                   start=True, stop=True))
                t = A(lambda e: e.activation(LN[i][:, :, :].rearrange("p a b -> p (a b)"), B[:, :], ACT.Copy), tok)
                free_bank(bn, t)

        def block1():
            first_mod = first_modulation()
            next(first_mod)
            load_rest()
            run(first_mod)
            for e_ in (V, A, G):
                e_.wait((s_in, s_in.n))
            ln_rows()
            start_fill(modulation(0, 4, 16, 24), 0.25)
            def context(i):
                own, zsc = scope(), scope()
                kvs = scope()
                ktm, Vb = sb([128, 6, 544], stack=kvs), sb([128, 6, 512], stack=kvs)
                Z8 = sb([128, 1024], stack=own)
                qtm = sb([128, 2, 768], stack=own) if i == 0 else None
                zT = sb([128, 3, 256], stack=zsc)
                ready = yield from mix1(i, 1, XC, 2, Z8, qtm, ktm, Vb, zT, zsc, i > 0)
                if i == 0:
                    sub = scope()
                    y = sb([128, 2, 1024], stack=sub)
                    row, trow = row_of(GPS[i][:, 0, :, 1], sub)
                    start_fill(modulation(0, 4, 24, 48), 0.2)
                    yt = yield from project("wo", 2, y, ready, row, trow)
                    residual(XC, y, 2, None, None, yt)
                    sub.close()
                zsc.close()
                own.close()
                return ktm, Vb, kvs

            def latent(i, ktm, Vb, kvs):
                own, zsc = scope(), scope()
                Z8 = sb([128, 2048], stack=own)
                qtm = sb([128, 4, 768], stack=own)
                zT = sb([128, 3, 512], stack=zsc)
                ready = yield from mix1(i, 0, X, 4, Z8, qtm, ktm, Vb, zT, zsc, False)
                own.close()
                kvs.close()
                stk = scope()
                y = sb([128, 4, 1024], stack=stk)
                row, trow = row_of(GPS[i][:, 0, :, 0], stk)
                if i == 0:
                    start_fill(modulation(1, 6, 0, 48), 0.0)
                yt = yield from project("wo", 4, y, ready, row, trow)
                residual(X, y, 4, None, None, yt)
                stk.close()

            kv = yield from context(0)
            yield from latent(0, *kv)
            if stop == "mix0":
                return
            fill["rate"] = MR
            yield from mlp(0, 1, XC, 2)
            kv = yield from context(1)
            end_fill()
            yield from mlp(0, 0, X, 4)
            if stop == "mlp0":
                return
            yield from latent(1, *kv)
            if stop == "mix1":
                return
            yield from mlp(1, 0, X, 4)

        def silu_psum(dst, B, tok, *waits):
            a = A(lambda e: e.activation(dst, B, ACT.Tanh, scale=0.5), tok, *waits)
            b = G(lambda e: e.tensor_scalar(dst, dst, 0.5, 0.5, ALU.mult, ALU.add), a)
            return V(lambda e: e.tensor_tensor(dst, B, dst, ALU.mult), b)

        hgb = []

        def gates(i, n, hf, GT, gt, ready, gfree_):
            bt = hgb[i][:, :]

            def ev_g(b, B, tok):
                c = A(lambda e: e.activation(GT[:, b, :], B, ACT.Tanh, scale=0.5,
                                             bias=bt[:, 8 * n + 4 * hf + b:8 * n + 4 * hf + b + 1]), tok,
                      gfree_.get(b))
                gt[b] = G(lambda e: e.tensor_scalar(GT[:, b, :], GT[:, b, :], 0.5, 0.5, ALU.mult, ALU.add), c)
                return [c]

            yield from gemm("gate", "FM", (AH, AL), 512, 8, 512, ev_g, ready)

        def branch(first, hf, GT, gt, M, Y, yready, mt):
            gf = {}

            def ev_b(b, B, tok):
                m = M[:, 4 * hf + b, :]
                if first:
                    gf[b] = mt[4 * hf + b] = V(lambda e: e.tensor_tensor(m, B, GT[:, b, :], ALU.mult), tok, gt[b])
                    return [gf[b]]
                a = V(lambda e: e.tensor_tensor(GT[:, b, :], B, GT[:, b, :], ALU.mult), tok, gt[b])
                gf[b] = mt[4 * hf + b] = V(lambda e: e.tensor_tensor(m, m, GT[:, b, :], ALU.add), a, mt[4 * hf + b])
                return [a]

            yield from gemm("br", "FM", Y, 512, 4, 512, ev_b, yready)
            return gf

        def delta_in(i, F, ready):
            sub = scope()
            U = sb([128, 4, 515], stack=sub)
            tz = None
            for c in range(4):
                tz = G(lambda e: e.memset(U[:, c, 0:3], 0.0))
            cw = c2("conv_w_2", i).rearrange("p (c k) -> p c k", c=12)
            ufree = [None] * 4
            tmp, tfree = [sb([128, 512], stack=sub) for _ in range(2)], [None, None]
            for n, key in enumerate(("qa", "ka", "va")):
                def ev(b, B, tok, n=n):
                    a = A(lambda e: e.activation(U[:, b, 3:515], B[:, :], ACT.Copy), tok, ufree[b])
                    defer(lambda: conv(n, b, a))
                    if b:
                        defer(lambda: silu(n, b - 1))
                    if b == 3:
                        defer(lambda: silu(n, b))
                    return [a]

                def conv(n, b, a):
                    f, w = F[n][:, b, :], cw[:, 4 * n + b, :]
                    t = V(lambda e: e.tensor_scalar(f, U[:, b, 0:512], w[:, 0:1], None, ALU.mult), a, tz)
                    for k in range(1, 4):
                        t = V(lambda e, k=k: e.scalar_tensor_tensor(f, U[:, b, k:k + 512], w[:, k:k + 1], f,
                                                                    ALU.mult, ALU.add), t)
                    ufree[b] = t

                def silu(n, b):
                    f, q = F[n][:, b, :], tmp[b % 2][:, :]
                    c = A(lambda e: e.activation(q, f, ACT.Tanh, scale=0.5), ufree[b], tfree[b % 2])
                    t = G(lambda e: e.tensor_scalar(q, q, 0.5, 0.5, ALU.mult, ALU.add), c)
                    tfree[b % 2] = V(lambda e: e.tensor_tensor(f, f, q, ALU.mult), t)

                yield from gemm(key, "FM", (AH, AL), 512, 8, 512, ev, ready)

            flush()
            sub.close()

        def delta(i, F, SM, SZ, za):
            stk = scope()
            be = sb([128, 4, 4], stack=stk)
            gg = sb([128, 4, 4], stack=stk)
            gt = sb([128, 4, 4], stack=stk)
            gc = sb([128, 4, 4], stack=stk)
            ea = sb([128, 4], stack=stk)
            a = A(lambda e: e.activation(be[:, :, :], SM[:, :, 0:4], ACT.Tanh, scale=0.5))
            tbe = V(lambda e: e.tensor_scalar(be[:, :, :], be[:, :, :], 0.5, 0.5, ALU.mult, ALU.add), a)
            t = V(lambda e: e.tensor_tensor(gg[:, :, :], SM[:, :, 4:8],
                                            r2("dt_bias_2", i).unsqueeze(1).to_broadcast([128, 4, 4]), ALU.add))
            t = V(lambda e: e.tensor_scalar(gt[:, :, :], gg[:, :, :], -1.0, None, ALU.mult), t)
            t = V(lambda e: e.tensor_tensor(gt[:, :, :], gt[:, :, :], gg[:, :, :], ALU.min), t)
            c = A(lambda e: e.activation(ea[:, :], r2("a_log_2", i), ACT.Exp))
            c = A(lambda e: e.activation(gt[:, :, :], gt[:, :, :], ACT.Exp), t)
            c = A(lambda e: e.activation(gt[:, :, :], gt[:, :, :], ACT.Ln, bias=1.0), c)
            t = V(lambda e: e.scalar_tensor_tensor(gg[:, :, :], gg[:, :, :], 0.0, gt[:, :, :], ALU.max, ALU.add), c)
            t = V(lambda e: e.tensor_tensor(gg[:, :, :], gg[:, :, :],
                                            ea[:, :].unsqueeze(1).to_broadcast([128, 4, 4]), ALU.mult), t)
            tg = V(lambda e: e.tensor_scalar(gg[:, :, :], gg[:, :, :], -1.0, None, ALU.mult), t)
            B, bn, w0 = bank()
            tok = P(lambda e: e.matmul(B[:, 0:16], con("ut"), gg[:, :, :].rearrange("p a b -> p (a b)"),
                                       start=True, stop=True), tg, w0)
            tgc = V(lambda e: e.tensor_copy(gc[:, :, :].rearrange("p a b -> p (a b)"), B[:, 0:16]), tok)
            free_bank(bn, tgc)

            def h4(ap):
                return ap.rearrange("p (h n) -> p h n", h=4)

            def bc(col):
                return col.unsqueeze(2).to_broadcast([128, 4, 128])

            def mask(ap):
                return ap.unsqueeze(1).to_broadcast([128, 4, 128])

            def mm4(o, lhs, rhs, *waits):
                P.wait(*waits)
                for h in range(4):
                    def mm(e, h=h):
                        return e.matmul(o[:, 128 * h:128 * h + 128], lhs[:, h, :], rhs[:, h, :], start=True, stop=True)
                    tok = P(mm) if h == 3 else P.quiet(mm)
                return tok

            def turn4(o, src, *waits):
                return transposes([o[:, 128 * h:128 * h + 128] for h in range(4)], [src[:, h, :] for h in range(4)],
                                  list(waits))

            def rstd_g(out, ss, inv, *waits):
                t = G(lambda e: e.tensor_scalar(out, ss, inv, 1e-6, ALU.mult, ALU.add), *waits)
                return G(lambda e: e.tensor_tensor(out, out, half[:, 0:4], ALU.pow), t)

            St = h4(sb([128, 512], stack=stk)[:, :])
            state = [V(lambda e: e.memset(St, 0.0))]
            lev = con("lev").rearrange("p (s n) -> p s n", s=7)
            turn_of = [0]

            def chunk(n, D, s_):
                cs = slice(128 * n, 128 * n + 128)
                qT, kT, vb = (F[j][:, :, cs] for j in range(3))
                kn, T, Lm, LT, AT, TT, X = (D[j] for j in range(7))
                GR = T
                prev = list(task[0].lasts.values())
                B, b1, w0 = bank()
                tk = turn4(B, kT, w0, prev)
                C, b2, w0 = bank()
                tq = turn4(C, qT, w0)
                yield
                a = A(lambda e: e.activation(X, h4(B), ACT.Square), tk, prev)
                a = V(lambda e: e.tensor_reduce(s_[:, 0:4], X, AX.X, ALU.add), a)
                r = rstd_g(s_[:, 4:8], s_[:, 0:4], 1.0, a)
                c = A(lambda e: e.activation(AT, h4(C), ACT.Square), tq)
                c = V(lambda e: e.tensor_reduce(s_[:, 8:12], AT, AX.X, ALU.add), c)
                r2_ = rstd_g(s_[:, 12:16], s_[:, 8:12], 1.0, c)
                r2_ = G(lambda e: e.tensor_scalar(s_[:, 12:16], s_[:, 12:16], SM2, None, ALU.mult), r2_)
                tkn = V(lambda e: e.tensor_tensor(kn, h4(B), bc(s_[:, 4:8]), ALU.mult), r)
                free_bank(b1, tkn)
                tqn = V(lambda e: e.tensor_tensor(AT, h4(C), bc(s_[:, 12:16]), ALU.mult), r2_)
                free_bank(b2, tqn)
                B, b1, w0 = bank()
                P.wait(w0)
                for h in range(4):
                    tk = P(lambda e, h=h: e.matmul(B[:, 128 * h:128 * h + 128],
                                                   gg[:, n, h:h + 1].to_broadcast([128, 128]), con("ut"),
                                                   start=True, stop=True))
                C, b2, w0 = bank()
                tv = turn4(C, vb, w0)
                yield
                tgr = A(lambda e: e.activation(GR, h4(B), ACT.Copy), tk)
                free_bank(b1, tgr)
                tvb = V(lambda e: e.tensor_tensor(vb, h4(C), bc(be[:, n, :]), ALU.mult), tv, tbe)
                free_bank(b2, tvb)
                gl = GR[:, :, 127]
                a = A(lambda e: e.activation(s_[:, 16:20], gc[:, n, :], ACT.Exp), tgc)
                tbg = G(lambda e: e.tensor_tensor(s_[:, 16:20], s_[:, 16:20], be[:, n, :], ALU.mult), a, tbe)
                a = G(lambda e: e.tensor_tensor(s_[:, 20:24], gl, gc[:, n, :], ALU.subtract), tgr, tgc)
                tdg = A(lambda e: e.activation(s_[:, 20:24], s_[:, 20:24], ACT.Exp), a)
                tgl = A(lambda e: e.activation(s_[:, 24:28], gl, ACT.Exp), tgr)
                B, b1, w0 = bank()
                tk = turn4(B, kn, w0, tkn)
                C, b2, w0 = bank()
                tq = turn4(C, AT, w0, tqn)
                yield
                tkT = A(lambda e: e.activation(kT, h4(B), ACT.Copy), tk)
                free_bank(b1, tkT)
                tqT = A(lambda e: e.activation(qT, h4(C), ACT.Copy), tq)
                free_bank(b2, tqT)
                a = V(lambda e: e.tensor_tensor(X, mask(con("ml")), GR, ALU.subtract), tgr, tkn)
                a = V(lambda e: e.tensor_tensor(X, X, bc(gc[:, n, :]), ALU.add), a)
                a = A(lambda e: e.activation(X, X, ACT.Exp), a)
                a = V(lambda e: e.tensor_tensor(X, X, bc(be[:, n, :]), ALU.mult), a)
                B, b1, w0 = bank()
                tk = mm4(B, kT, kT, w0, tkT)
                C, b2, w0 = bank()
                tq = mm4(C, kT, qT, w0, tqT)
                yield
                tL = V(lambda e: e.tensor_tensor(Lm, h4(B), X, ALU.mult), tk, a)
                free_bank(b1, tL)
                a = V(lambda e: e.tensor_tensor(X, mask(con("mu")), GR, ALU.add), tL)
                a = V(lambda e: e.tensor_tensor(X, X, bc(gc[:, n, :]), ALU.subtract), a)
                a = A(lambda e: e.activation(X, X, ACT.Exp), a)
                B, b1, w0 = bank()
                tk = turn4(B, Lm, w0, tL)
                yield
                tAT = V(lambda e: e.tensor_tensor(AT, h4(C), X, ALU.mult), tq, a)
                free_bank(b2, tAT)
                tLT = A(lambda e: e.activation(LT, h4(B), ACT.Copy), tk)
                free_bank(b1, tLT)
                a = A(lambda e: e.activation(X, GR, ACT.Exp), tAT)
                tqg = V(lambda e: e.tensor_tensor(qT, qT, X, ALU.mult), a, tqT)
                t = V(lambda e: e.tensor_tensor(X, Lm, mask(lev[:, 0, :]), ALU.mult), tqg)
                tT = V(lambda e: e.tensor_tensor(T, mask(ident), X, ALU.subtract), t)
                tke = G(lambda e: e.tensor_tensor(Lm, kn, bc(s_[:, 16:20]), ALU.mult), tbg, tkn, tLT, t)
                B, b1, w0 = bank()
                tk = turn4(B, T, w0, tT)
                yield
                tTT = A(lambda e: e.activation(TT, h4(B), ACT.Copy), tk)
                free_bank(b1, tTT)
                tx = None
                for s in range(1, 7):
                    w = 1 << s

                    def part(ap, h, odd):
                        return ap[:, h, :].rearrange("p (g t b) -> p g t b", t=2, b=w)[:, :, odd, :]

                    def parts4(ap, odd):
                        return ap.rearrange("p h (g t b) -> p h g t b", t=2, b=w)[:, :, :, odd, :]

                    def dense(o, h=None):
                        if h is None:
                            return o[:, 0:256].rearrange("p (h g b) -> p h g b", h=4, b=w)
                        return o[:, 64 * h:64 * h + 64].rearrange("p (g b) -> p g b", b=w)

                    def mmh(o, lhs, rhs, odd, *waits):
                        P.wait(*waits)
                        for h in range(4):
                            def mm(e, h=h):
                                return e.matmul(dense(o, h), lhs[:, h, :], part(rhs, h, odd), start=True, stop=True)
                            tok = P(mm) if h == 3 else P.quiet(mm)
                        return tok

                    tz = G(lambda e: e.memset(parts4(X, 1), 0.0), tx, tT)
                    B, b1, w0 = bank()
                    tk = mmh(B, LT, T, 0, w0, tLT, tT)
                    yield
                    msk = lev[:, s, :].rearrange("p (g t b) -> p g t b", t=2, b=w)[:, :, 0, :]
                    tX = V(lambda e: e.tensor_tensor(parts4(X, 0), dense(B),
                                                     msk.unsqueeze(1).to_broadcast([128, 4, 64 // w, w]), ALU.mult),
                           tk, tx, tz)
                    free_bank(b1, tX)
                    if s == 6:
                        tkd = G(lambda e: e.tensor_tensor(LT, kn, bc(s_[:, 20:24]), ALU.mult), tdg, tkn, tk)
                    B, b1, w0 = bank()
                    tx = tk = mmh(B, X, TT, 1, w0, tX, tTT)
                    if s < 6:
                        C, b2, w0 = bank()
                        tx = mmh(C, TT, X, 0, w0)
                    yield
                    tTT = V(lambda e: e.tensor_tensor(parts4(TT, 1), parts4(TT, 1), dense(B), ALU.subtract), tk, tx)
                    free_bank(b1, tTT)
                    if s < 6:
                        tT = V(lambda e: e.tensor_tensor(parts4(T, 0), parts4(T, 0), dense(C), ALU.subtract), tx)
                        free_bank(b2, tT)
                B, b1, w0 = bank()
                tk = mm4(B, TT, vb, w0, tTT, tvb)
                C, b2, w0 = bank()
                tq = mm4(C, Lm, TT, w0, tke)
                yield
                tu = A(lambda e: e.activation(T, h4(B), ACT.Copy), tk)
                free_bank(b1, tu)
                tw = A(lambda e: e.activation(X, h4(C), ACT.Copy), tq)
                free_bank(b2, tw)
                while turn_of[0] < n:
                    yield
                B, b1, w0 = bank()
                tk = mm4(B, X, St, w0, tw, state[0])
                yield
                tv = V(lambda e: e.tensor_tensor(T, T, h4(B), ALU.subtract), tk, tu)
                free_bank(b1, tv)
                B, b1, w0 = bank()
                P.wait(w0, tqg, tv, tAT)
                for h in range(4):
                    hs_ = slice(128 * h, 128 * h + 128)
                    P(lambda e: e.matmul(B[:, hs_], qT[:, h, :], St[:, h, :], start=True, stop=False))
                    to = P(lambda e: e.matmul(B[:, hs_], AT[:, h, :], T[:, h, :], start=False, stop=True))
                C, b2, w0 = bank()
                tk = mm4(C, LT, T, w0, tkd)
                yield
                a = V(lambda e: e.tensor_tensor(St, St, bc(s_[:, 24:28]), ALU.mult), to, tgl)
                state[0] = V(lambda e: e.tensor_tensor(St, St, h4(C), ALU.add), a, tk)
                free_bank(b2, state[0])
                turn_of[0] = n + 1
                a = A(lambda e: e.activation(X, h4(B), ACT.Square), to)
                a = V(lambda e: e.tensor_reduce(s_[:, 28:32], X, AX.X, ALU.add), a)
                r = rstd_g(s_[:, 32:36], s_[:, 28:32], 1.0 / 128, a)
                a = V(lambda e: e.tensor_tensor(X, h4(B), bc(s_[:, 32:36]), ALU.mult), r)
                free_bank(b1, a)
                B, b1, w0 = bank()
                tk = turn4(B, X, w0, a)
                yield
                assert len(za) >= 4
                a = V(lambda e: e.scalar_tensor_tensor(SZ[:, :, cs], h4(B), c2("dn_onorm_2", i)[:, 0:1],
                                                       SZ[:, :, cs], ALU.mult, ALU.mult), tk, za[0:4])
                free_bank(b1, a)
                za.append(a)

            def lane(ns):
                D = [h4(sb([128, 512], stack=stk)[:, :]) for _ in range(7)]
                s_ = sb([128, 36], stack=stk)
                for n in ns:
                    yield from chunk(n, D, s_)

            lanes = [lane((0, 2)), lane((1, 3))]
            while lanes:
                lanes = [l_ for l_ in lanes if next(l_, "end") != "end"]
                yield
            stk.close()

        def pooling(i, SZ, ready):
            stk = scope()
            U2 = [sb([128, 528], stack=stk)]
            YT = sb([128, 4, 512], stack=stk)
            W1, W2 = sb([128, 528], stack=stk), sb([128, 528], stack=stk)
            for u_ in U2:
                tz = G(lambda e: e.memset(u_[:, 0:16], 0.0))
            pooled = {}
            pcs = con("pc").rearrange("p (g n) -> p g n", g=4)

            def ev(b, B, tok):
                U = U2[0]
                a = A(lambda e: e.activation(U[:, 16:528], B[:, :], ACT.Copy), tok, pooled.get(b - 1))
                src, w, t = U[:, :], 1, [a, tz]
                bufs = [W1, W2]
                for m in range(b + 1):
                    dst = bufs[m % 2]
                    t = V(lambda e, dst=dst, src=src, w=w: e.tensor_tensor(dst[:, 2 * w - 1:528], src[:, 2 * w - 1:528],
                                                                           src[:, w - 1:528 - w], ALU.add), t)
                    src, w = dst[:, :], 2 * w
                o = YT[:, b, :]
                t = V(lambda e, src=src, w=w: e.scalar_tensor_tensor(o[:, 16:512], src[:, 32:528], 1.0 / w,
                                                                     U[:, 32:528], ALU.mult, ALU.subtract), t)
                t1 = V(lambda e, src=src: e.tensor_tensor(o[:, 0:16], src[:, 16:32], pcs[:, b, :], ALU.mult), t)
                pooled[b] = V(lambda e: e.tensor_tensor(o[:, 0:16], o[:, 0:16], U[:, 16:32], ALU.subtract), t1)
                return [a]

            yield from gemm("ub", "FM", (AH, AL), 512, 8, 512, ev, ready)
            zt = {}

            def ev_z(b, B, tok):
                zt[b] = silu_psum(SZ[:, b, :], B[:, :], tok)
                return [zt[b]]

            yield from gemm("zb", "FM", (AH, AL), 512, 8, 512, ev_z, ready)
            u = use("pw")
            W = RAW[u % NR][:, 0:512].rearrange("p (g n) -> p g n", g=4)
            ps = c2("pool_scale_2", i)
            for b in range(4):
                B, bn, w0 = bank()
                tok = P(lambda e: e.matmul(B, W[:, b, :], YT[:, b, :], start=True, stop=True), parts[u], w0, pooled[b])
                t = V(lambda e: e.scalar_tensor_tensor(SZ[:, b, :], B, ps[:, b:b + 1], SZ[:, b, :],
                                                       ALU.mult, ALU.mult), tok, zt[b])
                free_bank(bn, t)
                zt[b] = t
            release_raw(u, tok)
            stk.close()
            return zt

        def sparse_in(i, SM, SZ, KT, QT, VV, IQ, IK, wi, ready, ya):
            sub = scope()
            TMs = [sb([128, 4, 512], stack=sub) for _ in range(2)]
            rt = [sb([128, 5, 64], stack=sub) for _ in range(4)]
            sq = sb([128, 512], stack=sub)
            sm = task[0].st
            rac, ras = (con(n_).rearrange("p (t n) -> p t n", t=4) for n_ in ("rac", "ras"))
            rots, sqf, rtf = {}, [None] * 5, [None]

            def heads(key, TM, gname):
                g = r2(gname, i).unsqueeze(1).to_broadcast([128, 4, 128])
                rot = rots[key] = {}

                got = {}

                def ev(b, B, tok):
                    a = A(lambda e: e.activation(TM[:, b, :], B, ACT.Copy), tok)
                    defer(lambda: squares(b, a))
                    if b:
                        defer(lambda: scaled(b - 1))
                        defer(lambda: rotated(b - 1))
                    if b == 3:
                        defer(lambda: scaled(b))
                        defer(lambda: rotated(b))
                    return [a]

                def squares(b, a):
                    ss, rr_ = sm[:, 4 * b:4 * b + 4], sm[:, 16 + 4 * b:20 + 4 * b]
                    a = A(lambda e: e.activation(sq[:, :], TM[:, b, :], ACT.Square), a, sqf[0])
                    a = V(lambda e: e.tensor_reduce(ss, sq[:, :].rearrange("p (h n) -> p h n", h=4), AX.X, ALU.add),
                          a)
                    sqf[0] = a
                    got[b] = rstd(rr_, ss, 4, 1.0 / 128, 1e-6, a, sqf[1 + b])

                def scaled(b):
                    tm = TM[:, b, :].rearrange("p (h n) -> p h n", h=4)
                    rr_ = sm[:, 16 + 4 * b:20 + 4 * b]
                    a = V(lambda e: e.tensor_tensor(tm, tm, rr_.unsqueeze(2).to_broadcast([128, 4, 128]), ALU.mult),
                          got[b])
                    sqf[1 + b] = a
                    got[b] = V(lambda e: e.tensor_tensor(tm, tm, g, ALU.mult), a)

                def rotated(b):
                    tm = TM[:, b, :].rearrange("p (h n) -> p h n", h=4)
                    co = rac[:, b, :].unsqueeze(1).to_broadcast([128, 4, 64])
                    si = ras[:, b, :].unsqueeze(1).to_broadcast([128, 4, 64])
                    rot[b] = rotate((tm[:, :, 0:64], tm[:, :, 64:128]), tm[:, :, 0:64], tm[:, :, 64:128], co, si,
                                    [x_[:, 0:4, :] for x_ in rt], [got[b], rtf[0]])
                    rtf[0] = rot[b]

                yield from gemm(key, "TM", (AH, AL), 512, 8, 512, ev, ready)

            def turn_heads(key, TM, dst):
                for h in range(4):
                    B, bn, w0 = bank()
                    tk = transposes([B[:, 128 * t:128 * t + 128] for t in range(4)],
                                    [TM[:, t, 128 * h:128 * h + 128] for t in range(4)],
                                    [w0, [rots[key][b] for b in range(4)]])
                    a = A(lambda e: e.activation(dst[:, h, :], B, ACT.Copy), tk)
                    free_bank(bn, a)

            yield from heads("kc", TMs[0], "k_norm_2")
            yield from heads("qc", TMs[1], "q_norm_2")
            turn_heads("kc", TMs[0], KT)

            def ev_v(b, B, tok):
                return [A(lambda e: e.activation(VV[:, b, :], B, ACT.Copy), tok)]

            yield from gemm("vc", "TM", (AH, AL), 512, 8, 512, ev_v, ready)
            flush()
            turn_heads("qc", TMs[1], QT)
            ric, ris = (con(n_).rearrange("p (t n) -> p t n", t=4) for n_ in ("ric", "ris"))
            for t in range(4):
                v = SM[:, t, 8:328].rearrange("p (h n) -> p h n", h=5)
                tmp = [x_[:, :, 0:32] for x_ in rt]
                ir = rotate((v[:, :, 0:32], v[:, :, 32:64]), v[:, :, 0:32], v[:, :, 32:64],
                            ric[:, t, :].unsqueeze(1).to_broadcast([128, 5, 32]),
                            ris[:, t, :].unsqueeze(1).to_broadcast([128, 5, 32]), tmp, [V.last(), G.last()])
            V(lambda e: e.tensor_scalar(wi, SM[:, :, 328:332], 1.0 / 16, None, ALU.mult))

            def ev_z(b, B, tok):
                return [silu_psum(SZ[:, b, :], B, tok, ya)]

            yield from gemm("zc", "FM", (AH, AL), 512, 8, 512, ev_z, ready)
            for h in range(5):
                B, bn, w0 = bank()
                tk = transposes([B[0:64, 128 * t:128 * t + 128] for t in range(4)],
                                [SM[:, t, 8 + 64 * h:72 + 64 * h] for t in range(4)], [w0, ir])
                dst = IQ[:, h, :] if h < 4 else IK[:, :]
                a = A(lambda e: e.activation(dst, B[0:64, :], ACT.Copy), tk)
                free_bank(bn, a)
            sub.close()

        def sparse(i, SZ, KT, QT, VV, IQ, IK, wi, out):
            stk = scope()
            fence()
            sm = task[0].st
            scs = [sb([128, 512], stack=stk) for _ in range(1)]
            rl = [sb([128, 512], stack=stk) for _ in range(2)]
            biases = [sb([128, 512], stack=stk) for _ in range(2)]
            PP, PT = sb([128, 2, 512], stack=stk), sb([128, 2, 512], stack=stk)
            O = sb([128, 512], stack=stk)
            m8 = sm[:, 40:48]
            rlf, tbs = [None, None], {}

            def select(t):
                nk, sc, bias = 128 * (t + 1), scs[0], biases[t % 2]
                cs = slice(128 * t, 128 * t + 128)
                if t == 0:
                    tbs[t] = V(lambda e: e.tensor_copy(bias[:, 0:128], con("cb")))
                    return
                for h in range(4):
                    B, bn, w0 = bank()
                    tk = P(lambda e: e.matmul(B[:, 0:nk], IQ[:, h, cs], IK[:, 0:nk], start=True, stop=True), w0)
                    q = rl[h % 2]
                    a = A(lambda e: e.activation(q[:, 0:nk], B[:, 0:nk], ACT.Relu), tk, rlf[h % 2])
                    free_bank(bn, a)
                    w_ = wi[:, t, h:h + 1]
                    if h == 0:
                        acc = V(lambda e: e.tensor_scalar(sc[:, 0:nk], q[:, 0:nk], w_, None, ALU.mult), a)
                    else:
                        acc = V(lambda e: e.scalar_tensor_tensor(sc[:, 0:nk], q[:, 0:nk], w_, sc[:, 0:nk],
                                                                 ALU.mult, ALU.add), a, acc)
                    rlf[h % 2] = acc
                    yield
                a = V(lambda e: e.tensor_tensor(sc[:, cs], sc[:, cs], con("tri"), ALU.min), acc)
                for _ in range(16):
                    a = V(lambda e: e.max(out=m8, in_=sc[:, 0:nk]), a)
                    a = V(lambda e: e.match_replace(out=sc[:, 0:nk], in_to_replace=m8, in_values=sc[:, 0:nk],
                                                    imm_value=MARK), a)
                    yield
                tbs[t] = V(lambda e: e.tensor_scalar(bias[:, 0:nk], sc[:, 0:nk], -3.2e38, -BIG, ALU.is_gt, ALU.mult),
                           a)

            free = {"p": None, "t": None, "o": None}

            def attend(t):
                nk, bias = 128 * (t + 1), biases[t % 2]
                cs = slice(128 * t, 128 * t + 128)
                for hp in range(2):
                    bs = []
                    for j in range(2):
                        B, bn, w0 = bank()
                        h = 2 * hp + j
                        bs.append((B, bn, P(lambda e: e.matmul(B[:, 0:nk], QT[:, h, cs], KT[:, h, 0:nk],
                                                               start=True, stop=True), w0)))
                    mx, nm, rs, ri = (sm[:, 16 + 2 * j:18 + 2 * j] for j in range(4))
                    for j, (B, bn, tk) in enumerate(bs):
                        a = V(lambda e: e.tensor_tensor(PP[:, j, 0:nk], B[:, 0:nk], bias[:, 0:nk], ALU.add), tk, tbs[t],
                              free["p"])
                        free_bank(bn, a)
                    a = V(lambda e: e.tensor_reduce(mx, PP[:, :, 0:nk], AX.X, ALU.max), a)
                    a = G(lambda e: e.tensor_scalar(nm, mx, -SM2, None, ALU.mult), a)
                    for j in range(2):
                        te = A(lambda e: e.activation(PP[:, j, 0:nk], PP[:, j, 0:nk], ACT.Exp, bias=nm[:, j:j + 1],
                                                      scale=SM2, accum_out=rs[:, j:j + 1]), a)
                    yield
                    tr = V(lambda e: e.reciprocal(ri, rs), te)
                    for j in range(2):
                        B, bn, w0 = bank()
                        tk = transposes([B[:, 128 * k:128 * k + 128] for k in range(t + 1)],
                                        [PP[:, j, 128 * k:128 * k + 128] for k in range(t + 1)], [w0, te])
                        e_ = A(lambda e: e.activation(PT[:, j, 0:nk], B[:, 0:nk], ACT.Copy), tk, free["t"])
                        free_bank(bn, e_)
                    free["p"] = tk
                    yield
                    B, bn, w0 = bank()
                    P.wait(w0, e_)
                    for j in range(2):
                        h = 2 * hp + j
                        for k in range(t + 1):
                            tk = P(lambda e: e.matmul(B[:, 128 * j:128 * j + 128], PT[:, j, 128 * k:128 * k + 128],
                                                      VV[:, k, 128 * h:128 * h + 128], start=(k == 0), stop=(k == t)))
                    free["t"] = tk
                    a = V(lambda e: e.tensor_tensor(O[:, 256 * hp:256 * hp + 256].rearrange("p (h n) -> p h n", h=2),
                                                    B[:, 0:256].rearrange("p (h n) -> p h n", h=2),
                                                    ri.unsqueeze(2).to_broadcast([128, 2, 128]), ALU.mult),
                          tk, tr, free["o"])
                    free_bank(bn, a)
                    yield
                B, bn, w0 = bank()
                free["o"] = transposes([B[:, 128 * h:128 * h + 128] for h in range(4)],
                                       [O[:, 128 * h:128 * h + 128] for h in range(4)], [w0, a])
                ty = V(lambda e: e.tensor_tensor(SZ[:, :, cs], B.rearrange("p (h n) -> p h n", h=4), SZ[:, :, cs],
                                                 ALU.mult), free["o"])
                free_bank(bn, ty)
                out.append(ty)
                yield

            yield from select(0)
            for t in range(4):
                nxt = select(t + 1) if t < 3 else iter(())
                for _ in attend(t):
                    for _ in range(3):
                        next(nxt, None)
                    yield
                for _ in nxt:
                    yield
            stk.close()

        def to_branch(SZ, Y, waits):
            return {c: store_split(SZ[:, c, :], c, (Y[0][:, c, :], Y[1][:, c, :]), None, waits) for c in range(4)}

        def block2():
            first.close()
            for i in range(L):
                hgb.append(sb([128, 24]))
                t = V(lambda e: e.tensor_scalar(hgb[i][:, :], c2("gate_b_2", i), 0.5, None, ALU.mult))
                A.wait(t)
            for i in range(L):
                base = scope()
                M = sb([128, 8, 512], stack=base)
                smc = scope()
                SM = sb([128, 4, 332], stack=smc)
                SZ = sb([128, 4, 512], stack=base)
                wi = sb([128, 4, 4], stack=base)
                sub = scope()
                ready = prep(X, 4, lambda k: c2("norm_g_2", i)[:, k:k + 1], None, sub, [])

                def ev_s(b, B, tok):
                    return [A(lambda e: e.activation(SM[:, b, :], B[:, 0:332], ACT.Copy), tok)]

                yield from gemm("sm", "TM", (AH, AL), 512, 8, 332, ev_s, ready)
                sub.close()
                fsc = scope()
                F = [sb([128, 4, 512], stack=fsc) for _ in range(3)]
                yield from delta_in(i, F, ready)
                za, mt = [], {}

                def pool_part():
                    def ev_za(b, B, tok):
                        za.append(silu_psum(SZ[:, b, :], B, tok))
                        return [za[-1]]

                    yield from gemm("za", "FM", (AH, AL), 512, 8, 512, ev_za, ready)
                    sub, zsc = scope(), scope()
                    SZ1 = sb([128, 4, 512], stack=zsc)
                    pt = yield from pooling(i, SZ1, ready)
                    Y = [sb([128, 4, 512], f32r, sub) for _ in range(2)]
                    yr = to_branch(SZ1, Y, list(pt.values()))
                    zsc.close()
                    GT = sb([128, 4, 512], stack=sub)
                    gf = {}
                    for hf in range(2):
                        gt = {}
                        yield from gates(i, 1, hf, GT, gt, ready, gf)
                        gf = yield from branch(True, hf, GT, gt, M, Y, yr, mt)
                    sub.close()

                both(pool_part(), delta(i, F, SM, SZ, za), R1, LATE)
                fsc.close()
                ysc = scope()
                YA = [sb([128, 4, 512], f32r, ysc) for _ in range(2)]
                yra = to_branch(SZ, YA, za[-1:])
                asc = scope()
                KT, QT, VV = (sb([128, 4, 512], stack=asc) for _ in range(3))
                IQ, IK = sb([64, 4, 512], stack=asc), sb([64, 512], stack=asc)
                yield from sparse_in(i, SM, SZ, KT, QT, VV, IQ, IK, wi[:, :, :], ready, list(yra.values()))
                smc.close()
                yc = []
                g2 = {}
                gsc = scope()

                def gate_part():
                    sub = scope()
                    GT = sb([128, 4, 512], stack=sub)
                    gf = {}
                    for hf in range(2):
                        gt = {}
                        yield from gates(i, 0, hf, GT, gt, ready, gf)
                        gf = yield from branch(False, hf, GT, gt, M, YA, yra, mt)
                    sub.close()
                    ysc.close()
                    for hf in range(2):
                        g2[hf] = (sb([128, 4, 512], stack=gsc), {})
                        yield from gates(i, 2, hf, g2[hf][0], g2[hf][1], ready, {})

                both(gate_part(), sparse(i, SZ, KT, QT, VV, IQ, IK, wi[:, :, :], yc), R2_)
                asc.close()
                Y = [sb([128, 4, 512], f32r, gsc) for _ in range(2)]
                yr = to_branch(SZ, Y, yc)
                for hf in range(2):
                    yield from branch(False, hf, g2[hf][0], g2[hf][1], M, Y, yr, mt)
                mr = {k: store_split(M[:, k, :], k, (AH[:, k, :], AL[:, k, :]), None, mt[k], P.last())
                      for k in range(8)}
                gsc.close()
                for hf in range(2):
                    def ev(b, B, tok):
                        xs = X[:, b, 512 * hf:512 * hf + 512]
                        written[(id(X), b)] = t = V(lambda e: e.tensor_tensor(xs, xs, B, ALU.add), tok)
                        return [t]
                    yield from gemm("wout", "TM", (AH, AL), 512, 8, 512, ev, mr)
                base.close()
                if stop == f"l{i}":
                    return

        R1, R2_, MR, LATE = 0.6, 0.33, 0.05, 0
        if stop != "b2only":
            run(block1())
        else:
            load_rest()
            for e_ in (V, A, G):
                e_.wait((s_in, s_in.n))
            while state["used"] < next(j for j, u in enumerate(units) if u[0] == "sm"):
                u = state["used"]
                state["used"] += 1
                release_raw(u, parts[u])
        if stop is None or stop[0] in "bl":
            run(block2())
        fence()
        s_out = sem("s_out")
        S.wait(V.last(), A.last(), G.last(), P.last())
        t = S.dma(lambda e: e.dma_start(a_out.rearrange("b (t p) d -> p (b t) d", p=128), X[:, :, :]), s_out)
        S.wait(t)
        for p in s_raw:
            if p.n:
                S.wait((p, p.n))


def pack(inputs):
    a = {k: np.asarray(v) for k, v in inputs.items()}

    def unit(u):
        _, name, index, row, tiles, cols = u
        m = a[name][index]
        if name == "pool_w_2":
            return m.transpose(1, 0, 2).reshape(-1)
        m = np.concatenate([m[row:row + 128 * tiles, c0:c1] for c0, c1 in cols], axis=1)
        return m.reshape(tiles, 128, -1).transpose(1, 0, 2).reshape(-1)

    def col(v):
        return v.reshape(-1, 128).T

    def taps(w):
        return w.reshape(w.shape[0], -1, 128).transpose(2, 1, 0).reshape(128, -1)

    def cols(parts, i):
        return np.concatenate([taps(a[n][i]) if n in ("conf_dw_w", "sc_dw_w", "conv_w_2") else col(a[n][i])
                               for n, _ in parts], axis=1)

    def tiled(v, nt):
        return v.reshape(nt, 128, -1).transpose(1, 0, 2)

    out = {
        "wbig": np.concatenate([unit(u) for u in plan()]),
        "wmod": np.concatenate([unit(u) for i in range(L) for u in mod_plan(i)]),
        "x": tiled(a["x"], 4),
        "ctx": tiled(a["ctx"], 2),
        "cv": np.stack([col(a["c"]), col(a["c_ctx"])], axis=2),
        "cols1": np.stack([cols(COLS1, i) for i in range(L)], axis=1),
        "cols2": np.stack([cols(COLS2, i) for i in range(L)], axis=1),
        "rows2": np.stack([np.concatenate([np.broadcast_to(a[n][i][None, :], (128, w)) for n, w in ROWS2], axis=1)
                           for i in range(L)], axis=1),
        "const": constants(),
    }
    return {"in_" + k: np.ascontiguousarray(v) for k, v in out.items()}


def kernel(**inputs):
    import concourse.bacc as _bacc
    from concourse.bass_utils import run_bass_kernel_spmd as _run

    arrays = pack(inputs)
    nc = _bacc.Bacc("TRN2", target_bir_lowering=False, num_devices=1)
    args = [nc.dram_tensor(k, v.shape, mybir.dt.from_np(v.dtype), kind="ExternalInput").ap()
            for k, v in arrays.items()]
    args.append(nc.dram_tensor("out_0", (1, 512, 1024), mybir.dt.float32, kind="ExternalOutput").ap())
    program(nc, *args)
    r = _run(nc, [arrays], core_ids=[0])
    return r.results[0]["out_0"]
```
